# Optimizing a Trainium2 kernel written in Bass

```python
import math
import jax
import jax.numpy as jnp
from jax import lax
import numpy as np

D_MODEL = 1024
BATCH = 1
SEQ = 1024
DEPTH = 2

MIX_WIDTH = D_MODEL
GROUP_WIDTH = MIX_WIDTH // 4
SSD_HEAD_DIM = 64
SSD_HEADS = GROUP_WIDTH // SSD_HEAD_DIM
SSD_N_GROUPS = 2
SSD_STATE = 128
SSD_CONV = 4
SSD_CHUNK = 128
SSD_XBC = GROUP_WIDTH + 2 * SSD_N_GROUPS * SSD_STATE
RET_HEAD_DIM = 64
RET_HEADS = GROUP_WIDTH // RET_HEAD_DIM
RET_CHUNK = 128
ROPE_BASE = 10000.0
LRU_BLOCKS = 4
LRU_BLOCK_DIM = GROUP_WIDTH // LRU_BLOCKS
LRU_CONV = 4
LRU_C = 8.0
GLA_HEADS = 4
GLA_VAL_DIM = GROUP_WIDTH // GLA_HEADS
GLA_KEY_DIM = GLA_VAL_DIM // 2
GLA_GATE_RANK = 16
GLA_GATE_NORM = 16.0
GLA_CHUNK = 64
D_FF = -(-8 * D_MODEL // (3 * 256)) * 256
DEEPNORM_ALPHA = (2 * DEPTH) ** 0.25
DEEPNORM_BETA = (8 * DEPTH) ** -0.25
EPS = 1e-5
IN_SPLITS = (GROUP_WIDTH, SSD_XBC, SSD_HEADS,
             GROUP_WIDTH, GROUP_WIDTH, GROUP_WIDTH, GROUP_WIDTH,
             GROUP_WIDTH, GROUP_WIDTH,
             GLA_HEADS * GLA_KEY_DIM, GLA_HEADS * GLA_KEY_DIM,
             GROUP_WIDTH, GLA_GATE_RANK, GROUP_WIDTH)
IN_WIDTH = sum(IN_SPLITS)

kernel_name = 'hybrid_ssd_retnet_rglru_gla_deepnorm_adaln'

def layer_norm(x, w, b):
    xf = x.astype(jnp.float32)
    mu = jnp.mean(xf, axis=-1, keepdims=True)
    var = jnp.mean(jnp.square(xf - mu), axis=-1, keepdims=True)
    return ((xf - mu) * lax.rsqrt(var + EPS) * w + b).astype(x.dtype)

def rms_norm(x, w):
    xf = x.astype(jnp.float32)
    return (xf * lax.rsqrt(jnp.mean(jnp.square(xf), axis=-1, keepdims=True) + EPS) * w).astype(x.dtype)

def head_group_norm(y, w):
    yf = y.astype(jnp.float32)
    mu = jnp.mean(yf, axis=-1, keepdims=True)
    var = jnp.mean(jnp.square(yf - mu), axis=-1, keepdims=True)
    return ((yf - mu) * lax.rsqrt(var + EPS) * w).astype(y.dtype)

def causal_depthwise_conv(x, w, b):
    width, ch = w.shape
    y = lax.conv_general_dilated(x, w[:, None, :], window_strides=(1,), padding=[(width - 1, 0)],
                                 dimension_numbers=('NWC', 'WIO', 'NWC'), feature_group_count=ch)
    return y + b

def apply_rotary(x, positions):
    half = x.shape[-1] // 2
    inv_freq = ROPE_BASE ** (-jnp.arange(half, dtype=jnp.float32) / half)
    ang = positions.astype(jnp.float32)[..., None] * inv_freq
    cos = jnp.cos(ang)[:, :, None, :]
    sin = jnp.sin(ang)[:, :, None, :]
    x1, x2 = x[..., :half], x[..., half:]
    return jnp.concatenate([x1 * cos - x2 * sin, x2 * cos + x1 * sin], axis=-1).astype(x.dtype)

def scan_chunk_states(states, chunk_decay):
    def step(h, inp):
        st, dec = inp
        return h * dec + st, h
    h0 = jnp.zeros_like(states[:, 0])
    _, prev = lax.scan(step, h0, (jnp.moveaxis(states, 1, 0), jnp.moveaxis(chunk_decay, 1, 0)))
    return jnp.moveaxis(prev, 0, 1)

def chunked_scalar_decay(q, k, v, log_a, chunk):
    bsz, seq, nh, n = q.shape
    p = v.shape[-1]
    nc = seq // chunk
    q = q.reshape(bsz, nc, chunk, nh, n)
    k = k.reshape(bsz, nc, chunk, nh, n)
    v = v.reshape(bsz, nc, chunk, nh, p)
    cum = jnp.cumsum(log_a.astype(jnp.float32).reshape(bsz, nc, chunk, nh), axis=2)
    causal = jnp.tril(jnp.ones((chunk, chunk), dtype=bool))
    seg = cum[:, :, :, None, :] - cum[:, :, None, :, :]
    decay = jnp.exp(jnp.where(causal[:, :, None], seg, -jnp.inf))
    scores = jnp.einsum('bcthn,bcshn->bctsh', q, k) * decay
    y_intra = jnp.einsum('bctsh,bcshp->bcthp', scores, v)
    to_end = jnp.exp(cum[:, :, -1:, :] - cum)
    states = jnp.einsum('bcsh,bcshn,bcshp->bchnp', to_end, k, v).astype(jnp.float32)
    chunk_decay = jnp.exp(cum[:, :, -1, :])[..., None, None]
    prev = scan_chunk_states(states, chunk_decay)
    y_inter = jnp.einsum('bcth,bcthn,bchnp->bcthp', jnp.exp(cum), q, prev)
    return (y_intra + y_inter).reshape(bsz, seq, nh, p).astype(v.dtype)

def chunked_gla(q, k, v, log_a, chunk):
    bsz, seq, nh, kd = q.shape
    vd = v.shape[-1]
    nc = seq // chunk
    q = q.reshape(bsz, nc, chunk, nh, kd)
    k = k.reshape(bsz, nc, chunk, nh, kd)
    v = v.reshape(bsz, nc, chunk, nh, vd)
    cum = jnp.cumsum(log_a.astype(jnp.float32).reshape(bsz, nc, chunk, nh, kd), axis=2)
    q_in = q * jnp.exp(cum)
    k_in = k * jnp.exp(-cum)
    k_end = k * jnp.exp(cum[:, :, -1:] - cum)
    causal = jnp.tril(jnp.ones((chunk, chunk), dtype=bool))
    scores = jnp.where(causal, jnp.einsum('bcthk,bcshk->bchts', q_in, k_in), 0.0)
    y_intra = jnp.einsum('bchts,bcshv->bcthv', scores, v)
    states = jnp.einsum('bcshk,bcshv->bchkv', k_end, v).astype(jnp.float32)
    chunk_decay = jnp.exp(cum[:, :, -1])[..., None]
    prev = scan_chunk_states(states, chunk_decay)
    y_inter = jnp.einsum('bcthk,bchkv->bcthv', q_in, prev)
    return (y_intra + y_inter).reshape(bsz, seq, nh, vd).astype(v.dtype)

def linear_recurrence(a, u):
    def combine(left, right):
        a_l, u_l = left
        a_r, u_r = right
        return a_l * a_r, a_r * u_l + u_r
    _, h = lax.associative_scan(combine, (a, u), axis=1)
    return h

def ssd_group(z, xbc, dt_raw, conv_w, conv_b, dt_bias, a_log, d_skip, norm_w):
    bsz, seq, _ = z.shape
    xbc = jax.nn.silu(causal_depthwise_conv(xbc, conv_w, conv_b))
    xs, b_in, c_in = jnp.split(xbc, [GROUP_WIDTH, GROUP_WIDTH + SSD_N_GROUPS * SSD_STATE], axis=-1)
    xs = xs.reshape(bsz, seq, SSD_HEADS, SSD_HEAD_DIM)
    rep = SSD_HEADS // SSD_N_GROUPS
    b_in = jnp.repeat(b_in.reshape(bsz, seq, SSD_N_GROUPS, SSD_STATE), rep, axis=2)
    c_in = jnp.repeat(c_in.reshape(bsz, seq, SSD_N_GROUPS, SSD_STATE), rep, axis=2)
    dt = jax.nn.softplus((dt_raw + dt_bias).astype(jnp.float32))
    log_a = -jnp.exp(a_log.astype(jnp.float32)) * dt
    y = chunked_scalar_decay(c_in, b_in, xs * dt[..., None], log_a, SSD_CHUNK)
    y = (y + xs * d_skip[:, None]).reshape(bsz, seq, GROUP_WIDTH)
    return rms_norm(y * jax.nn.silu(z), norm_w)

def retention_group(q, k, v, g, positions, norm_w):
    bsz, seq, _ = q.shape
    shp = (bsz, seq, RET_HEADS, RET_HEAD_DIM)
    q = apply_rotary(q.reshape(shp), positions)
    k = apply_rotary(k.reshape(shp), positions) * (RET_HEAD_DIM ** -0.5)
    log_gamma = jnp.log1p(-jnp.exp2(-5.0 - jnp.arange(RET_HEADS, dtype=jnp.float32)))
    log_a = jnp.broadcast_to(log_gamma, (bsz, seq, RET_HEADS))
    y = chunked_scalar_decay(q, k, v.reshape(shp), log_a, RET_CHUNK)
    y = head_group_norm(y, norm_w.reshape(RET_HEADS, RET_HEAD_DIM)).reshape(bsz, seq, GROUP_WIDTH)
    return y * jax.nn.silu(g)

def rglru_group(gate, xr, conv_w, conv_b, wa, ba, wx, bx, lam):
    bsz, seq, _ = xr.shape
    xr = causal_depthwise_conv(xr, conv_w, conv_b)
    xb = xr.reshape(bsz, seq, LRU_BLOCKS, LRU_BLOCK_DIM)
    r = jax.nn.sigmoid(jnp.einsum('bski,kij->bskj', xb, wa).reshape(bsz, seq, GROUP_WIDTH) + ba)
    i = jax.nn.sigmoid(jnp.einsum('bski,kij->bskj', xb, wx).reshape(bsz, seq, GROUP_WIDTH) + bx)
    log_a = -LRU_C * r.astype(jnp.float32) * jax.nn.softplus(-lam.astype(jnp.float32))
    a = jnp.exp(log_a)
    u = jnp.sqrt(-jnp.expm1(2.0 * log_a)) * (i * xr).astype(jnp.float32)
    h = linear_recurrence(a, u).astype(xr.dtype)
    return h * jax.nn.gelu(gate)

def gla_group(q, k, v, g_low, r, wg2, bg, norm_w):
    bsz, seq, _ = q.shape
    q = q.reshape(bsz, seq, GLA_HEADS, GLA_KEY_DIM) * (GLA_KEY_DIM ** -0.5)
    k = k.reshape(bsz, seq, GLA_HEADS, GLA_KEY_DIM)
    v = v.reshape(bsz, seq, GLA_HEADS, GLA_VAL_DIM)
    log_a = jax.nn.log_sigmoid((g_low @ wg2 + bg).astype(jnp.float32)) / GLA_GATE_NORM
    log_a = log_a.reshape(bsz, seq, GLA_HEADS, GLA_KEY_DIM)
    o = chunked_gla(q, k, v, log_a, GLA_CHUNK)
    o = rms_norm(o, norm_w.reshape(GLA_HEADS, GLA_VAL_DIM)).reshape(bsz, seq, GROUP_WIDTH)
    return o * jax.nn.silu(r)

def hybrid_mixer(h, positions, w_in, ssd_conv_w, ssd_conv_b, ssd_dt_bias, ssd_a_log, ssd_d, ssd_norm_w,
                 ret_norm_w, lru_conv_w, lru_conv_b, lru_wa, lru_ba, lru_wx, lru_bx, lru_lambda,
                 gla_wg2, gla_bg, gla_norm_w, w_out):
    proj = jnp.einsum('bsd,de->bse', h, w_in)
    split_at = np.cumsum(IN_SPLITS)[:-1].tolist()
    (ssd_z, ssd_xbc, ssd_dt, ret_q, ret_k, ret_v, ret_g, lru_gate, lru_x,
     gla_q, gla_k, gla_v, gla_glow, gla_r) = jnp.split(proj, split_at, axis=-1)
    y_ssd = ssd_group(ssd_z, ssd_xbc, ssd_dt, ssd_conv_w, ssd_conv_b, ssd_dt_bias, ssd_a_log, ssd_d, ssd_norm_w)
    y_ret = retention_group(ret_q, ret_k, ret_v, ret_g, positions, ret_norm_w)
    y_lru = rglru_group(lru_gate, lru_x, lru_conv_w, lru_conv_b, lru_wa, lru_ba, lru_wx, lru_bx, lru_lambda)
    y_gla = gla_group(gla_q, gla_k, gla_v, gla_glow, gla_r, gla_wg2, gla_bg, gla_norm_w)
    y = jnp.concatenate([y_ssd, y_ret, y_lru, y_gla], axis=-1)
    return jnp.einsum('bse,ed->bsd', y, w_out)

def swiglu(h, w_up, w_down):
    g, u = jnp.split(jnp.einsum('bsd,df->bsf', h, w_up), 2, axis=-1)
    return jnp.einsum('bsf,fd->bsd', jax.nn.silu(g) * u, w_down)

def setup_inputs(seed: int = 0) -> dict:
    key = jax.random.key(seed)
    ks = iter(jax.random.split(key, 40))
    f32 = jnp.float32
    L, D = DEPTH, D_MODEL

    def nrm(shape, scale):
        return jax.random.normal(next(ks), shape, f32) * scale

    x = nrm((BATCH, SEQ, D), 1.0)
    c = nrm((BATCH, D), 1.0)
    offsets = jax.random.randint(next(ks), (BATCH, 1), 0, 4096, dtype=jnp.int32)
    positions = (offsets + jnp.arange(SEQ, dtype=jnp.int32)[None, :]).astype(jnp.int32)
    w_ada = nrm((L, D, 6 * D), D ** -0.5)
    b_ada = nrm((L, 6 * D), 0.02)
    w_in = nrm((L, D, IN_WIDTH), D ** -0.5)
    ssd_conv_w = nrm((L, SSD_CONV, SSD_XBC), SSD_CONV ** -0.5)
    ssd_conv_b = nrm((L, SSD_XBC), 0.02)
    dt0 = jnp.exp(jax.random.uniform(next(ks), (L, SSD_HEADS), f32, math.log(1e-3), math.log(1e-1)))
    ssd_dt_bias = dt0 + jnp.log(-jnp.expm1(-dt0))
    ssd_a_log = jnp.log(jax.random.uniform(next(ks), (L, SSD_HEADS), f32, 1.0, 16.0))
    ssd_d = 1.0 + nrm((L, SSD_HEADS), 0.02)
    ssd_norm_w = 1.0 + nrm((L, GROUP_WIDTH), 0.02)
    ret_norm_w = 1.0 + nrm((L, GROUP_WIDTH), 0.02)
    lru_conv_w = nrm((L, LRU_CONV, GROUP_WIDTH), LRU_CONV ** -0.5)
    lru_conv_b = nrm((L, GROUP_WIDTH), 0.02)
    lru_wa = nrm((L, LRU_BLOCKS, LRU_BLOCK_DIM, LRU_BLOCK_DIM), LRU_BLOCK_DIM ** -0.5)
    lru_ba = nrm((L, GROUP_WIDTH), 0.02)
    lru_wx = nrm((L, LRU_BLOCKS, LRU_BLOCK_DIM, LRU_BLOCK_DIM), LRU_BLOCK_DIM ** -0.5)
    lru_bx = nrm((L, GROUP_WIDTH), 0.02)
    a0 = jax.random.uniform(next(ks), (L, GROUP_WIDTH), f32, 0.9, 0.999)
    s0 = a0 ** (1.0 / LRU_C)
    lru_lambda = jnp.log(s0) - jnp.log1p(-s0)
    gla_wg2 = nrm((L, GLA_GATE_RANK, GLA_HEADS * GLA_KEY_DIM), GLA_GATE_RANK ** -0.5)
    gla_bg = nrm((L, GLA_HEADS * GLA_KEY_DIM), 0.02)
    gla_norm_w = 1.0 + nrm((L, GROUP_WIDTH), 0.02)
    w_out = nrm((L, MIX_WIDTH, D), MIX_WIDTH ** -0.5 * DEEPNORM_BETA)
    ln1_w = 1.0 + nrm((L, D), 0.02)
    ln1_b = nrm((L, D), 0.02)
    ffn_w_up = nrm((L, D, 2 * D_FF), D ** -0.5)
    ffn_w_down = nrm((L, D_FF, D), D_FF ** -0.5 * DEEPNORM_BETA)
    ln2_w = 1.0 + nrm((L, D), 0.02)
    ln2_b = nrm((L, D), 0.02)
    return {'x': x, 'c': c, 'positions': positions, 'w_ada': w_ada, 'b_ada': b_ada, 'w_in': w_in,
            'ssd_conv_w': ssd_conv_w, 'ssd_conv_b': ssd_conv_b, 'ssd_dt_bias': ssd_dt_bias,
            'ssd_a_log': ssd_a_log, 'ssd_d': ssd_d, 'ssd_norm_w': ssd_norm_w, 'ret_norm_w': ret_norm_w,
            'lru_conv_w': lru_conv_w, 'lru_conv_b': lru_conv_b, 'lru_wa': lru_wa, 'lru_ba': lru_ba,
            'lru_wx': lru_wx, 'lru_bx': lru_bx, 'lru_lambda': lru_lambda, 'gla_wg2': gla_wg2,
            'gla_bg': gla_bg, 'gla_norm_w': gla_norm_w, 'w_out': w_out, 'ln1_w': ln1_w, 'ln1_b': ln1_b,
            'ffn_w_up': ffn_w_up, 'ffn_w_down': ffn_w_down, 'ln2_w': ln2_w, 'ln2_b': ln2_b}

def reference(x, c, positions, w_ada, b_ada, w_in, ssd_conv_w, ssd_conv_b, ssd_dt_bias, ssd_a_log, ssd_d,
              ssd_norm_w, ret_norm_w, lru_conv_w, lru_conv_b, lru_wa, lru_ba, lru_wx, lru_bx, lru_lambda,
              gla_wg2, gla_bg, gla_norm_w, w_out, ln1_w, ln1_b, ffn_w_up, ffn_w_down, ln2_w, ln2_b):
    c_act = jax.nn.silu(c)
    for l in range(DEPTH):
        mod = c_act @ w_ada[l] + b_ada[l]
        sh_m, sc_m, g_m, sh_f, sc_f, g_f = [m[:, None, :] for m in jnp.split(mod, 6, axis=-1)]
        h = x * (1.0 + sc_m) + sh_m
        y = hybrid_mixer(h, positions, w_in[l], ssd_conv_w[l], ssd_conv_b[l], ssd_dt_bias[l], ssd_a_log[l],
                         ssd_d[l], ssd_norm_w[l], ret_norm_w[l], lru_conv_w[l], lru_conv_b[l], lru_wa[l],
                         lru_ba[l], lru_wx[l], lru_bx[l], lru_lambda[l], gla_wg2[l], gla_bg[l],
                         gla_norm_w[l], w_out[l])
        x = layer_norm(DEEPNORM_ALPHA * x + g_m * y, ln1_w[l], ln1_b[l])
        h = x * (1.0 + sc_f) + sh_f
        y = swiglu(h, ffn_w_up[l], ffn_w_down[l])
        x = layer_norm(DEEPNORM_ALPHA * x + g_f * y, ln2_w[l], ln2_b[l])
    return x


_drawn_inputs = setup_inputs


def setup_inputs(seed=0):
    import zlib

    import numpy as np

    out = dict(_drawn_inputs(seed))
    spreads = {}
    factors = {'ssd_conv_b': 8.0,
     'ssd_d': 41.3,
     'ssd_norm_w': 24.024,
     'ret_norm_w': 31.458,
     'lru_conv_b': 4.202,
     'lru_ba': 35.412,
     'lru_bx': 23.265,
     'gla_bg': 8.0,
     'gla_norm_w': 27.881}
    for name, (base, spread) in spreads.items():
        noise = np.random.default_rng([zlib.crc32(name.encode()), seed]).standard_normal(out[name].shape)
        drawn = base * np.exp(spread * noise) if base else spread * noise
        out[name] = jnp.asarray(drawn.astype(out[name].dtype))
    for name, factor in factors.items():
        out[name] = (out[name] * factor).astype(out[name].dtype)
    return out
```

```python
import math
from contextlib import ExitStack

import numpy as np

import concourse.bass as bass
import concourse.mybir as mybir

F32 = mybir.dt.float32
F32R = mybir.dt.float32r
I32 = mybir.dt.int32
ALU = mybir.AluOpType
ACT = mybir.ActivationFunctionType

P = 128
D = 1024
T = 1024
DEPTH = 2
KD = D // P
HALF = 512
GW = 256
CH = 128
NCH = T // CH
XBC = 768
D_FF = 2816
NF = D_FF // P
PART = 6
ALPHA = (2 * DEPTH) ** 0.25
EPS = 1e-5
TWO_PI = 2 * math.pi

COL_Z, COL_XBC, COL_DT = 0, 256, 1024
COL_RET = 1028
COL_LRU_GATE, COL_LRU_X = 2052, 2308
COL_GLA_QKV, COL_GLOW, COL_GLA_R = 2564, 3076, 3092

IN_SEGMENTS = [(COL_Z, 8), (COL_RET, 8), (COL_GLA_QKV, 4), (COL_GLA_R, 2), (COL_LRU_X, 2), (COL_LRU_GATE, 2)]
N_IN = sum(n for _, n in IN_SEGMENTS)
FULL_PARTS = NF // PART
LAST_PART = NF - FULL_PARTS * PART
N_TILES = N_IN + KD + 2 * NF + (FULL_PARTS + 1) * KD
ADA_PAIRS = 24

ROWS = {}
_n = 0
for _name, _count in [("ssd_conv_w", 24), ("ssd_conv_b", 6), ("ssd_norm_w", 2), ("ret_norm_w", 2),
                      ("gla_norm_w", 2), ("lru_conv_w", 8), ("lru_conv_b", 2), ("lru_ba", 2),
                      ("lru_bx", 2), ("lru_lambda", 2), ("gla_bg", 1), ("ln1_w", 8), ("ln1_b", 8),
                      ("ln2_w", 8), ("ln2_b", 8)]:
    ROWS[_name] = (_n, _count)
    _n += _count
N_ROWS = _n

CONST = {}
_n = 0
for _name, _count in [("ident", 128), ("causal", 128), ("perm", 128), ("ret_decay", 512),
                      ("ret_in", 256), ("block2", 128), ("block4", 256), ("causal64", 64),
                      ("ret_end", 4), ("head4", 4), ("ret_chunk", 2), ("freq", 1), ("eps", 1),
                      ("head2", 2), ("one", 1)]:
    CONST[_name] = (_n, _count)
    _n += _count
N_CONST = _n


def constants():
    c = np.zeros((P, N_CONST), np.float64)
    p = np.arange(P)

    def put(name, value):
        a, n = CONST[name]
        c[:, a:a + n] = np.asarray(value).reshape(P, n)

    gamma = 1.0 - 2.0 ** (-5.0 - np.arange(4))
    put("ident", np.eye(P))
    put("causal", p[:, None] <= p[None, :])
    perm = np.zeros((P, P))
    for m in range(P):
        perm[m + 32 if m % 64 < 32 else m - 32, m] = -1.0 if m % 64 < 32 else 1.0
    put("perm", perm)
    lag = p[None, :] - p[:, None]
    put("ret_decay", np.stack([np.where(lag >= 0, g ** np.maximum(lag, 0), 0) * 0.125 for g in gamma], 1))
    put("ret_in", np.stack([gamma[2 * j + p // 64][:, None] ** (p + 1.0) for j in range(2)], 1))
    put("block2", p[:, None] // 64 == p[None, :] // 64)
    put("block4", p[:, None] // 32 == np.arange(256)[None, :] // 64)
    put("causal64", p[:, None] % 64 <= np.arange(64)[None, :])
    put("ret_end", 0.125 * gamma[None, :] ** (127.0 - p[:, None]))
    put("head4", p[:, None] // 32 == np.arange(4)[None, :])
    put("ret_chunk", np.stack([gamma[2 * j + p // 64] ** 128.0 for j in range(2)], 1))
    put("freq", 10000.0 ** (-(p % 32) / 32.0))
    put("eps", np.full(P, EPS))
    put("head2", p[:, None] // 64 == np.arange(2)[None, :])
    put("one", np.ones(P))
    return c.astype(np.float32)


def mixer_order():
    order = [("params",), ("small", 0), ("small", 1)]

    def tile(t):
        group = [("proj", t, 0), ("proj", t, 1)]
        if t < ADA_PAIRS:
            group = [("ada_sum", t)] + group + [("ada", t)]
        return group

    def spread(units, steps):
        n, out = 0, []
        for i, u in enumerate(units):
            out.append(u)
            want = len(steps) * (i + 1) // len(units)
            out += steps[n:want]
            n = want
        return out

    for t in range(8):
        order += tile(t)
        if t == 0:
            order += [("dt",), ("dt_cum",)]
        if 2 <= t:
            order.append(("conv", t - 2))
    ssd = [("ssd_zero",)] + [(s, c) for c in range(NCH) for s in ("ssd_a", "ssd_b")] + [("ssd_stats",), ("ssd_norm",)]
    units = []
    for t in range(8, 16):
        units += tile(t)
        if 9 <= t <= 12:
            units += [("rotate", t - 9, 0), ("rotate", t - 9, 1)]
    order += units[:4] + spread(units[4:], ssd)
    ret = [("ret_zero",)] + [(s, c) for c in range(NCH) for s in ("ret_a", "ret_b")] + [("ret_stats",), ("ret_norm",)]
    units = []
    for t in range(16, 22):
        units += tile(t)
        if t == 19:
            units += [("gla_gate",)]
    order += spread(units, ret)
    gla = [("gla_zero",)] + [(s, c) for c in range(NCH) for s in ("gla_a", "gla_b", "gla_c")]
    units = []
    for t in range(22, 26):
        units += tile(t)
        if t in (23, 24):
            units += [("lru", t - 23)]
    order += spread(units, gla)
    order += [("gla_stats",), ("gla_norm",)]
    return order


ORDER = mixer_order()
UNITS_OF = {"params": 1, "small": 1, "dt": 1, "dt_cum": 1, "proj": 1, "ada": 1, "rotate": 1,
            "ssd_stats": 1, "ssd_norm": 2, "ret_stats": 1, "ret_norm": 8, "gla_stats": 1, "gla_norm": 4,
            "gla_gate": 2, "lru": 4}
UNIT = {}
_n = 0
for _step in ORDER:
    UNIT[_step] = _n
    _n += UNITS_OF.get(_step[0], 0)
UNIT_OUT = _n
MISC = {}
_n = 0
for _step in ORDER:
    MISC[_step] = _n
    _n += 0 if _step[0] in ("proj", "ada") else UNITS_OF.get(_step[0], 0)
MISC_LN1 = _n
MISC_LN2 = MISC_LN1 + 8
N_MISC = MISC_LN2 + 8
UNIT_LN1 = UNIT_OUT + 2 * KD
UNIT_FFN = UNIT_LN1 + 8
UNIT_LN2 = UNIT_FFN + 4 * NF + 2 * KD * (FULL_PARTS + 1)
UNITS = UNIT_LN2 + 8
UNITS_0 = 20
assert UNIT_FFN % 4 == 0 and UNIT_LN2 % 4 == 0 and UNITS % 4 == 0 and UNITS_0 % 4 == 0


class Signal:

    all = []

    def __init__(self, ctx, nc, name, layer, before=0, step=1):
        self.sem = ctx.enter_context(nc.semaphore(name))
        self.name, self.layer, self.before, self.step = name, layer, before, step
        self.counted = 0
        Signal.all.append(self)

    def inc(self, instruction, times=1):
        self.counted += times
        instruction.then_inc(self.sem, self.step)

    def at(self, l, n):
        return l * (self.layer * self.step) + n * self.step + self.before * self.step


def build(nc, a, out):
    Signal.all = []
    ctx = ExitStack()
    with ctx:
        KB = 1024
        place_at = [(nc.sbuf_base + 63) // 64 * 64]

        def region(size):
            offset = place_at[0]
            place_at[0] += (size + 31) // 32 * 32
            assert place_at[0] <= nc.sbuf_usable_end, place_at[0] - nc.sbuf_usable_end
            return offset

        def place(name, shape, dt=F32, at=None):
            if at is None:
                at = region(4 * int(np.prod(shape[1:])))
            return nc.alloc_sbuf_tensor_at(name, shape, dt, offset=at)

        op_hi = place("op_hi", [P, KD, T], F32R)
        op_lo = place("op_lo", [P, KD, T], F32R)
        ada_first = nc.alloc_sbuf_tensor_at("ada_first", [P, KD, 2 * D], F32, offset=place_at[0] - 64 * KB)
        w_raw = [place(f"w_raw{i}", [P, KD, P]) for i in range(2)]
        w_hi = [place(f"w_hi{i}", [P, KD, P], F32R) for i in range(2)]
        w_lo = [place(f"w_lo{i}", [P, KD, P], F32R) for i in range(2)]
        ada_raw = [place(f"ada_raw{i}", [P, 4, 256]) for i in range(2)]
        ada_sum = [place(f"ada_sum{i}", [P, 256]) for i in range(2)]
        X = region(32 * KB)
        Y = region(48 * KB)
        TMP = region(16 * KB)
        ax = place("ax", [P, KD, T], at=X)
        act_hi = place("act_hi", [P, PART, T], F32R, at=Y)
        act_lo = place("act_lo", [P, PART, T], F32R, at=Y + 24 * KB)
        x_rows = place("x_rows", [P, 8, D], at=Y)
        angle = place("angle", [P, 4, T], at=Y + 32 * KB)
        ga = place("ga", [P, 6, T], at=X)
        gb = place("gb", [P, 6, T], at=X + 24 * KB)
        y = place("y", [P, 8, T], at=Y + 16 * KB)
        cos_sin = place("cos_sin", [P, 2, T], at=Y + 32 * KB)
        small_hi = place("small_hi", [P, KD * 48 + 80], F32R, at=Y + 40 * KB)
        small_lo = place("small_lo", [P, KD * 48 + 80], F32R, at=Y + 42 * KB)
        tmp = place("tmp", [P, 8, HALF], at=TMP)
        small = place("small", [48, T], at=TMP)
        tmp2k = [place(f"tmp2k{i}", [P, HALF], at=TMP + (4 + 2 * i) * KB) for i in range(6)]
        tmp1k = [place(f"tmp1k{i}", [P, 256], at=TMP + (4 + i) * KB) for i in range(12)]
        conv_a = place("conv_a", [P, T], at=TMP + 4 * KB)
        conv_b = place("conv_b", [P, T], at=TMP + 8 * KB)
        const = place("consts", [P, N_CONST])
        par = place("par", [P, N_ROWS])
        par_rows = place("par_rows", [N_ROWS, P])
        b_ada = place("b_ada_columns", [P, DEPTH, 48])
        b_ada_rows = place("b_ada_rows", [48, DEPTH, P])
        mod = place("mod", [P, 32])
        mod_next = place("mod_next", [P, 16])
        b_mod = place("b_mod", [P, 48])
        c_rows = place("c_rows", [KD, P])
        c_col = place("c_col", [P, 2, KD])
        lru_w = place("lru_w", [P, 2, 2, P])
        gate_w = place("gate_w", [16, P])
        head_par = place("head_par", [P, 14])
        columns = place("columns", [P, 5, 32])
        lru_col = place("lru_col", [P, 6, 2])
        stat = place("stat", [P, 4, 32])
        te = place("te", [P, 8])

        ring = [ctx.enter_context(nc.psum_tensor(f"ring{i}", [P, HALF], F32)) for i in range(4)]
        core = [ctx.enter_context(nc.psum_tensor(f"core{i}", [P, HALF], F32)) for i in range(4)]
        residual = nc.dram_tensor("residual", (KD, P, T), F32, kind="Internal").ap()
        rotary = nc.dram_tensor("rotary", (2, P, T), F32, kind="Internal").ap()

        def signal(name, layer, before=0, step=1):
            return Signal(ctx, nc, name, layer, before, step)

        const_loaded = signal("const_loaded", 0, 4, 16)
        x_loaded = [signal(f"x_loaded{i}", 0, 1, 16) for i in range(4)]
        pos_loaded = signal("pos_loaded", 0, 1, 16)
        rows_loaded = signal("rows_loaded", 15, 0, 16)
        heads_loaded = signal("heads_loaded", 3, 0, 16)
        lru_w_loaded = signal("lru_w_loaded", 9, 0, 16)
        small_loaded = signal("small_loaded", 2, 0, 16)
        raw_loaded = [signal(f"raw_loaded{i}", N_TILES // 2, 0, 16) for i in range(2)]
        raw_free = [signal(f"raw_free{i}", N_TILES // 2, 1) for i in range(2)]
        split_done = signal("split_done", N_TILES)
        half_done = signal("half_done", N_TILES)
        tile_done = signal("tile_done", N_TILES, 2)
        small_split = signal("small_split", 1)
        zeroed = signal("zeroed", 0, 1)
        pool_passed = signal("pool_passed", 0)
        ada_first_loaded = [signal(f"ada_first_loaded{i}", 0, 1, 16) for i in range(4)]
        ada_loaded = [signal(f"ada_loaded{i}", ADA_PAIRS, 0, 16) for i in range(2)]
        ada_raw_free = [signal(f"ada_raw_free{i}", ADA_PAIRS + 1 - i, 1) for i in range(2)]
        ada_summed = [signal(f"ada_summed{i}", ADA_PAIRS) for i in range(2)]
        ada_sum_used = signal("ada_sum_used", ADA_PAIRS, 1)
        w_hi_made = signal("w_hi_made", N_TILES)
        residual_saved = signal("residual_saved", 1, 0, 16)
        residual_loaded = signal("residual_loaded", 1, 0, 16)
        rotary_saved = signal("rotary_saved", 0, 1, 16)
        rotary_loaded = signal("rotary_loaded", 1, 0, 16)
        bank_free = [signal(f"bank_free{i}", UNITS // 4, UNITS_0 // 4) for i in range(4)]
        unit_done = signal("unit_done", N_MISC, UNITS_0)
        ax_ready = signal("ax_ready", 16, 16)
        h_value = signal("h_value", 32)
        y_hi = signal("y_hi", 16)
        gate_tanh = signal("gate_tanh", 12)
        raw_copied = signal("raw_copied", 36)
        conv_tanh = signal("conv_tanh", 6)
        small_copied = signal("small_copied", 2)
        par_copied = signal("par_copied", 1)
        dt_exp = signal("dt_exp", 1)
        ssd_act = signal("ssd_act", 2 * NCH)
        ret_act = signal("ret_act", 2 * NCH)
        gla_act = signal("gla_act", 2 * NCH)
        gla_gate_act = signal("gla_gate_act", 2)
        norm_sq = signal("norm_sq", 3)
        norm_dev = signal("norm_dev", 3)
        norm_wide = signal("norm_wide", 2)
        lru_act = signal("lru_act", 6)
        gelu_sq = signal("gelu_sq", 4)
        gelu_tanh = signal("gelu_tanh", 4)
        z_sq = signal("z_sq", 32)
        ln_dev = signal("ln_dev", 4)
        up_tanh = signal("up_tanh", 2 * NF)
        up_hi = signal("up_hi", 2 * NF)
        c_copied = signal("c_copied", 0, 1)
        c_tanh = signal("c_tanh", 0, 1)
        angle_sin = signal("angle_sin", 0, 1)
        out_copied = signal("out_copied", 0, 16)
        h_lo = signal("h_lo", 32)
        y_lo = signal("y_lo", 16)
        y_final = signal("y_final", 4)
        par_ready = signal("par_ready", 1)
        conv_done = signal("conv_done", 6)
        dt_x = signal("dt_x", 1)
        dt_ready = signal("dt_ready", 1)
        ssd_dve = signal("ssd_dve", 3 * NCH + 1)
        rotate_lo = signal("rotated", 8)
        ret_dve = signal("ret_dve", 2 * NCH + 1)
        gla_dve = signal("gla_dve", 3 * NCH + 1)
        gla_gate_x = signal("gla_gate_x", 1)
        gla_cum = signal("gla_cum", 1)
        norm_in = signal("norm_in", 1)
        norm_var = signal("norm_var", 3)
        norm_rstd = signal("norm_rstd", 3)
        lru_xr = signal("lru_xr", 2)
        lru_dve = signal("lru_dve", 2)
        lru_in = signal("lru_in", 2)
        gelu_in = signal("gelu_in", 4)
        z_made = signal("z_made", 32)
        sums_made = signal("sums_made", 32)
        ln_var = signal("ln_var", 4)
        ln_rstd = signal("ln_rstd", 4)
        ln_norm = signal("ln_norm", 32)
        up_act = signal("up_act", 2 * NF)
        up_lo = signal("up_lo", 2 * NF, 2)
        c_ready = signal("c_ready", 0, 1)
        mod_first = signal("mod_first", 0, 1)
        angle_ready = signal("angle_ready", 0, 1)
        rotary_made = signal("rotary_made", 0, 1)
        ssd_pe = signal("ssd_pe", 2 * NCH)
        ret_pe = signal("ret_pe", 2 * NCH)
        gla_pe = signal("gla_pe", 3 * NCH)
        out_saved = signal("out_saved", 0, 8, 16)

        def cst(name, rows=slice(None)):
            first, n = CONST[name]
            return const[rows, first:first + n]

        def col(name, i=0):
            first, _ = ROWS[name]
            return par[:, first + i:first + i + 1]

        ident, eps, one = cst("ident"), cst("eps"), cst("one")

        def chunk(c, n=CH):
            return slice(c * n, (c + 1) * n)

        def half_of(h):
            return slice(h * HALF, (h + 1) * HALF)

        gate_slot = {0: 0, 1: 1, 14: 2, 15: 3, 20: 6, 21: 7, 24: 4, 25: 5}
        silu_tiles = [0, 1, 14, 15, 20, 21]
        copied_tiles = [t for t in range(N_IN) if t not in gate_slot]

        def copied_to(t):
            if t < 8:
                return ga[:, t - 2, :]
            if t < 14:
                return gb[:, t - 8, :]
            if t < 20:
                return ga[:, t - 16, :]
            return gb[:, t - 22, :]

        def copied_count(t):
            return 2 * copied_tiles.index(t) + 2

        def wide_stat(g, s):
            return gb[:, 2 * s:2 * s + 2, :] if g == 1 else ga[:, 0:2, :]

        block = ctx.enter_context(nc.Block())

        @block.sync
        def _(sp):
            const_loaded.inc(sp.dma_start(const[:], a["const"]))
            const_loaded.inc(sp.dma_start(c_rows[:], a["c"].rearrange("b (k p) -> (b k) p", p=P)))
            for l in range(DEPTH):
                const_loaded.inc(sp.dma_start(b_ada_rows[:, l, :], a["b_ada"][l, :].rearrange("(k p) -> k p", p=P)))
            for i in range(4):
                x_loaded[i].inc(sp.dma_start(
                    x_rows[:, 2 * i:2 * i + 2, :],
                    a["x"][0, 256 * i:256 * i + 256, :].rearrange("(k p) d -> p k d", p=P)))
            pos_loaded.inc(sp.dma_start(angle[:, 0, :].bitcast(I32), a["positions"][0, :].partition_broadcast(P)))

            for i in range(4):
                ada_first_loaded[i].inc(sp.dma_start(
                    ada_first[:, :, 512 * i:512 * i + 512],
                    a["w_ada"][0, :, 512 * i:512 * i + 512].rearrange("(k p) n -> p k n", p=P)))
            sp.wait_ge(rotary_made.sem, 1)
            rotary_saved.inc(sp.dma_start(rotary.rearrange("a p t -> p a t"), angle[:, 2:4, :]))
            sp.wait_ge(rotary_saved.sem, 16)

            with sp.Fori(0, DEPTH) as l:
                def layer_of(name, at=None):
                    return a[name][bass.ds(l if at is None else at, 1)]

                def load_tile(slot, n, name, row0, rows, col0, times=1):
                    sp.wait_ge(raw_free[slot].sem, raw_free[slot].at(l, n))
                    src = layer_of(name).rearrange("a m n -> (a m) n")[bass.ds(row0, rows * P), bass.ds(col0, P)]
                    raw_loaded[slot].inc(sp.dma_start(w_raw[slot][:, 0:rows, :],
                                                      src.rearrange("(k p) n -> p k n", p=P)), times)

                def load_ada_pair(pair, layer, col0, times=1):
                    for q in range(2):
                        src = layer_of("w_ada", layer).rearrange("a m n -> (a m) n")[
                            512 * q:512 * q + 512, bass.ds(col0, 256)]
                        sp.wait_ge(ada_raw_free[q].sem, ada_raw_free[q].at(l, pair + (1 - q)))
                        ada_loaded[q].inc(sp.dma_start(ada_raw[q][:], src.rearrange("(k p) n -> p k n", p=P)), times)

                sp.wait_ge(ada_raw_free[0].sem, ada_raw_free[0].at(l, 0))
                src = layer_of("w_in").rearrange("a (k p) n -> p (a k) n", p=P)
                small_raw = ada_raw[0][:].rearrange("p a b -> p (a b)")[:, 0:KD * 48].rearrange("p (k n) -> p k n", n=48)
                small_loaded.inc(sp.dma_start(small_raw[:, :, 0:16], src[:, :, COL_GLOW:COL_GLOW + 16]))
                small_loaded.inc(sp.dma_start(small_raw[:, :, 32:36], src[:, :, COL_DT:COL_DT + 4]))
                load_tile(0, 0, "w_in", 0, KD, 0)
                for name, (first, count) in ROWS.items():
                    v = layer_of(name)
                    v = v.rearrange("a c (k p) -> (a c k) p", p=P) if len(v.shape) == 3 else \
                        v.rearrange("a (k p) -> (a k) p", p=P)
                    rows_loaded.inc(sp.dma_start(par_rows[first:first + count, :], v))
                load_tile(1, 0, "w_in", 0, KD, P)
                for i, name in enumerate(("ssd_a_log", "ssd_dt_bias", "ssd_d")):
                    heads_loaded.inc(sp.dma_start(head_par[:, 4 * i:4 * i + 4],
                                                  layer_of(name).rearrange("a h -> (a h)").partition_broadcast(P)))
                sp.wait_ge(zeroed.sem, 1)
                for m, name in enumerate(("lru_wa", "lru_wx")):
                    for k in range(4):
                        r = slice(64 * (k % 2), 64 * (k % 2) + 64)
                        lru_w_loaded.inc(sp.dma_start(lru_w[r, m, k // 2, r],
                                                      layer_of(name).rearrange("a k i j -> (a k) i j")[k]))
                lru_w_loaded.inc(sp.dma_start(gate_w[:], layer_of("gla_wg2").rearrange("a r n -> (a r) n")))
                sp.wait_ge(ax_ready.sem, ax_ready.at(l, 0))
                residual_saved.inc(sp.dma_start(residual.rearrange("k p t -> p k t"), ax[:]))
                sp.wait_ge(tile_done.sem, tile_done.at(l, 0))
                rotary_loaded.inc(sp.dma_start(cos_sin[:], rotary.rearrange("a p t -> p a t")))

                def ada_source(pair):
                    return (None, 2048 + 256 * pair) if pair < 16 else ((l + 1) % DEPTH, 256 * (pair - 16))

                t = 0
                for first, count in IN_SEGMENTS:
                    skip = 2 if t == 0 else 0
                    if t == 0:
                        for s in range(2):
                            load_ada_pair(s, *ada_source(s))
                    with sp.Fori(skip // 2, count // 2) as i:
                        for s in range(2):
                            load_tile(s, i + t // 2, "w_in", 0, KD, i * (2 * P) + (first + s * P),
                                      (count - skip) // 2)
                            if t < ADA_PAIRS:
                                layer, col0 = ada_source(t + s)
                                load_ada_pair(i * 2 + (t + s), layer, i * 512 + col0, (count - skip) // 2)
                    t += count
                with sp.Fori(0, KD // 2) as i:
                    for s in range(2):
                        load_tile(s, i + t // 2, "w_out", 0, KD, i * (2 * P) + s * P, KD // 2)
                t += KD

                def load_part(t2, f0, size, times):
                    with sp.Fori(0, size) as i:
                        load_tile(0, i + t2, "ffn_w_up", 0, KD, (i + f0) * P, times * size)
                        load_tile(1, i + t2, "ffn_w_up", 0, KD, (i + (f0 + NF)) * P, times * size)
                    with sp.Fori(0, KD // 2) as i:
                        for s in range(2):
                            load_tile(s, i + (t2 + size), "ffn_w_down", f0 * P, size, i * (2 * P) + s * P,
                                      times * KD // 2)

                with sp.Fori(0, FULL_PARTS) as part:
                    load_part(part * (PART + KD // 2) + t // 2, part * PART, PART, FULL_PARTS)
                load_part(FULL_PARTS * (PART + KD // 2) + t // 2, FULL_PARTS * PART, LAST_PART, 1)

            for c in range(NCH):
                sp.wait_ge(out_copied.sem, 2 * c + 2)
                out_saved.inc(sp.dma_start(out[0, chunk(c), :], x_rows[:, c, :]))
            sp.wait_ge(out_saved.sem, 16 * NCH)

        @block.gpsimd
        def _(pool):
            zeroed.inc(pool.memset(lru_w[:], 0.0))
            for s in range(2):
                pool.sem_inc(raw_free[s].sem, 1)
                pool.sem_inc(ada_raw_free[s].sem, 1)
            pool.wait_ge(c_ready.sem, 1)
            with pool.Fori(0, DEPTH) as l:
                def split(slot, tile, rows, times=1):
                    pool.wait_ge(w_hi_made.sem, w_hi_made.at(l, tile + 1))
                    raw_free[slot].inc(pool.tensor_tensor(
                        w_lo[slot][:, 0:rows, :], w_raw[slot][:, 0:rows, :],
                        w_hi[slot][:, 0:rows, :].bitcast(F32), ALU.subtract), times)
                    split_done.inc(pool.drain(), times)

                def sum_ada(pair, times):
                    raw = ada_raw[0]
                    pool.wait_ge(ada_loaded[0].sem, ada_loaded[0].at(l, pair + 1))
                    pool.tensor_tensor(raw[:], raw[:], c_col[:, 0, 0:4].unsqueeze(2).to_broadcast([P, 4, 256]), ALU.mult)
                    pool.drain()
                    pool.tensor_tensor(raw[:, 0:2, :], raw[:, 0:2, :], raw[:, 2:4, :], ALU.add)
                    pool.drain()
                    pool.wait_ge(ada_sum_used.sem, ada_sum_used.at(l, pair))
                    ada_raw_free[0].inc(pool.tensor_tensor(ada_sum[0][:], raw[:, 0, :], raw[:, 1, :], ALU.add), times)
                    ada_summed[0].inc(pool.drain(), times)

                pool.wait_ge(small_loaded.sem, small_loaded.at(l, 2))
                pool.wait_ge(tile_done.sem, tile_done.at(l, 0))
                pool.wait_ge(rotary_saved.sem, 16)
                small_raw = ada_raw[0][:].rearrange("p a b -> p (a b)")[:, 0:KD * 48].rearrange("p (k n) -> p k n", n=48)
                parts = [t[:, 0:KD * 48].rearrange("p (k n) -> p k n", n=48) for t in (small_hi, small_lo)]
                pool.sem_inc(pool_passed.sem, 1)
                pool.memset(small_hi[:].bitcast(F32), 0.0)
                pool.memset(small_lo[:].bitcast(F32), 0.0)
                pool.drain()
                for r in (slice(0, 16), slice(32, 36)):
                    pool.tensor_copy(parts[0][:, :, r], small_raw[:, :, r])
                pool.drain()
                for r in (slice(0, 16), slice(32, 36)):
                    last = pool.tensor_tensor(parts[1][:, :, r], small_raw[:, :, r],
                                              parts[0][:, :, r].bitcast(F32), ALU.subtract)
                ada_raw_free[0].inc(last)
                small_split.inc(pool.drain())

                with pool.Fori(0, ADA_PAIRS // 2) as i:
                    for s in range(2):
                        split(s, i * 2 + s, KD, ADA_PAIRS // 2)
                        sum_ada(i * 2 + s, ADA_PAIRS // 2)
                with pool.Fori(ADA_PAIRS // 2, (N_IN + KD) // 2) as i:
                    for s in range(2):
                        split(s, i * 2 + s, KD, (N_IN + KD - ADA_PAIRS) // 2)

                def split_part(t2, size, times):
                    with pool.Fori(0, size) as i:
                        for s in range(2):
                            split(s, (i + t2) * 2 + s, KD, times * size)
                    with pool.Fori(0, KD // 2) as i:
                        for s in range(2):
                            split(s, (i + (t2 + size)) * 2 + s, size, times * KD // 2)

                with pool.Fori(0, FULL_PARTS) as part:
                    split_part(part * (PART + KD // 2) + (N_IN + KD) // 2, PART, FULL_PARTS)
                split_part(FULL_PARTS * (PART + KD // 2) + (N_IN + KD) // 2, LAST_PART, 1)

        @block.tensor
        def _(pe):
            pe.sem_inc(tile_done.sem, 2)
            pe.sem_inc(ada_sum_used.sem, 1)

            def transpose(out_, in_):
                return pe.transpose(out_, in_, ident[0:in_.shape[0], 0:in_.shape[0]])

            pe.wait_ge(const_loaded.sem, 64)
            n = 0
            unit_done.counted = 0
            last = transpose(ring[0][:, 0:KD], c_rows[:])
            unit_done.inc(last, 0)
            for l in range(DEPTH):
                unit_done.inc(transpose(ring[1 + l][:, 0:48], b_ada_rows[:, l, :]), 0)
            for n in range(3, 19):
                h, k = divmod(n - 3, KD)
                if n >= 4:
                    pe.wait_ge(bank_free[n % 4].sem, n // 4)
                if k == 0:
                    for i in (2 * h, 2 * h + 1):
                        pe.wait_ge(x_loaded[i].sem, 16)
                for i in range(4):
                    last = transpose(ring[n % 4][:, chunk(i)], x_rows[:, 4 * h + i, chunk(k)])
                unit_done.inc(last, 0)
            pe.wait_ge(bank_free[3].sem, 19 // 4)
            pe.wait_ge(c_ready.sem, 1)
            for n in range(2 * KD):
                if n % 4 == 0:
                    pe.wait_ge(ada_first_loaded[n // 4].sem, 16)
                for k in range(KD):
                    last = pe.matmul(ring[3][:, n:n + 1], ada_first[:, k, chunk(n)], c_col[:, 0, k:k + 1],
                                     start=(k == 0), stop=(k == KD - 1))
            unit_done.inc(last, 0)

            with pe.Fori(0, DEPTH) as l:
                def enter(unit4, bank):
                    pe.wait_ge(bank_free[bank].sem, bank_free[bank].at(l, unit4))
                    return ring[bank]

                def bank_of(step, i=0):
                    u = UNIT[step] + i
                    return enter(u // 4, u % 4)

                def large(ps, slot, rows, hi, lo):
                    for k in range(rows):
                        pe.matmul(ps[:], w_hi[slot][:, k, :], hi(k), start=(k == 0), stop=False)
                        pe.matmul(ps[:], w_hi[slot][:, k, :], lo(k), start=False, stop=False)
                        last = pe.matmul(ps[:], w_lo[slot][:, k, :], hi(k), start=False, stop=(k == rows - 1))
                    return last

                def operand(h):
                    return (lambda k: op_hi[:, k, half_of(h)]), (lambda k: op_lo[:, k, half_of(h)])

                for step in ORDER:
                    kind, n = step[0], (step[1] if len(step) > 1 else 0)
                    if kind == "params":
                        pe.wait_ge(rows_loaded.sem, rows_loaded.at(l, 15))
                        ps = bank_of(step)
                        unit_done.inc(transpose(ps[:, 0:N_ROWS], par_rows[:]))
                    elif kind == "small":
                        if n == 0:
                            pe.wait_ge(small_split.sem, small_split.at(l, 1))
                        ps = bank_of(step)
                        hi, lo = operand(n)
                        for k in range(KD):
                            pe.wait_ge(h_lo.sem, h_lo.at(l, 8 * n + k + 1))
                            w_h, w_l = (t[:, k * 48:k * 48 + P] for t in (small_hi, small_lo))
                            pe.matmul(ps[:], w_h, hi(k), start=(k == 0), stop=False)
                            pe.matmul(ps[:], w_h, lo(k), start=False, stop=False)
                            last = pe.matmul(ps[:], w_l, hi(k), start=False, stop=(k == KD - 1))
                        unit_done.inc(last)
                    elif kind == "proj":
                        h = step[2]
                        if h == 0:
                            pe.wait_ge(split_done.sem, split_done.at(l, n + 1))
                        ps = bank_of(step)
                        last = large(ps, n % 2, KD, *operand(h))
                        (tile_done if h else half_done).inc(last)
                    elif kind == "ada":
                        for q in range(2):
                            pe.wait_ge(ada_summed[q].sem, ada_summed[q].at(l, n + 1))
                        ps = bank_of(step)
                        for i in range(2):
                            for q in range(2):
                                last = pe.matmul(ps[:, i:i + 1], ada_sum[q][:, chunk(i)], one,
                                                 start=(q == 0), stop=(q == 1))
                        ada_sum_used.inc(last)
                    elif kind == "dt":
                        pe.wait_ge(small_copied.sem, small_copied.at(l, 2))
                        ps = bank_of(step)
                        for c in range(NCH):
                            last = pe.matmul(ps[:, 4 * c:4 * c + 4], small[32:36, chunk(c)], ident[32:36, 32:36],
                                             start=True, stop=True)
                        unit_done.inc(last)
                    elif kind == "dt_cum":
                        pe.wait_ge(dt_ready.sem, dt_ready.at(l, 1))
                        ps = bank_of(step)
                        unit_done.inc(pe.matmul(ps[:, 0:32], cst("causal"), columns[:, 1, :], start=True, stop=True))
                    elif kind == "rotate":
                        h = step[2]
                        pe.wait_ge(raw_copied.sem, raw_copied.at(l, copied_count(8 + n) - 1 + h))
                        ps = bank_of(step)
                        unit_done.inc(pe.matmul(ps[:], cst("perm"), gb[:, n, half_of(h)], start=True, stop=True))
                    elif kind == "ssd_a":
                        pe.wait_ge(ssd_dve.sem, ssd_dve.at(l, 3 * n + 1))
                        b_cum, b_g, b_t, b_y = core
                        for j in range(2):
                            transpose(b_t[:, chunk(j)], ga[:, j, chunk(n)])
                            transpose(b_t[:, chunk(2 + j)], ga[:, 2 + j, chunk(n)])
                        for g in range(2):
                            pe.matmul(b_g[:, chunk(g)], ga[:, 2 + g, chunk(n)], ga[:, 4 + g, chunk(n)],
                                      start=True, stop=True)
                        for hd in range(4):
                            i = 4 * n + hd
                            last = pe.matmul(b_cum[:, chunk(hd)], columns[:, 1, i:i + 1].to_broadcast([P, P]),
                                             cst("causal"), start=True, stop=True)
                        ssd_pe.inc(last)
                    elif kind == "ssd_b":
                        ed, ec, v, v2, bt, hs = tmp2k[0], tmp2k[1], tmp1k[5], tmp1k[6], tmp1k[7], tmp1k[8]
                        pe.wait_ge(ssd_dve.sem, ssd_dve.at(l, 3 * n + 3))
                        for hd in range(4):
                            j, i = divmod(hd, 2)
                            o = core[3][64 * i:64 * i + 64, 256 * (n % 2) + P * j:256 * (n % 2) + P * j + P]
                            pe.matmul(o, v[:, chunk(hd, 64)], ed[:, chunk(hd)], start=True, stop=False)
                            pe.matmul(o, hs[:, chunk(hd, 64)], ec[:, chunk(hd)], start=False, stop=True)
                        for g in range(2):
                            last = pe.matmul(core[1][:, 256 + P * g:256 + P * g + P], bt[:, chunk(g)],
                                             v2[:, chunk(g)], start=True, stop=True)
                        ssd_pe.inc(last)
                    elif kind in ("ssd_stats", "ret_stats", "gla_stats"):
                        g = ("ssd_stats", "ret_stats", "gla_stats").index(kind)
                        pe.wait_ge(norm_sq.sem, norm_sq.at(l, g + 1))
                        ps = bank_of(step)
                        if g == 0:
                            for c in range(NCH):
                                for j in range(2):
                                    last = pe.matmul(ps[:, c:c + 1], ga[:, 2 + j, chunk(c)], one,
                                                     start=(j == 0), stop=(j == 1))
                        else:
                            raw, sq = (gb[:, 4:6, :], gb[:, 0:2, :]) if g == 1 else (None, ga[:, 0:2, :])
                            for c in range(NCH):
                                for j in range(2):
                                    i = 4 * c + 2 * j
                                    last = pe.matmul(ps[:, i:i + 2], sq[:, j, chunk(c)], cst("head2"),
                                                     start=True, stop=True)
                                    if g == 1:
                                        last = pe.matmul(ps[:, 32 + i:32 + i + 2], raw[:, j, chunk(c)], cst("head2"),
                                                         start=True, stop=True)
                        unit_done.inc(last)
                    elif kind == "ssd_norm":
                        pe.wait_ge(norm_rstd.sem, norm_rstd.at(l, 1))
                        for h in range(2):
                            ps = bank_of(step, h)
                            for c in range(4):
                                last = pe.matmul(ps[:, chunk(c)], stat[:, 0, 4 * h + c:4 * h + c + 1].to_broadcast([P, P]),
                                                 ident, start=True, stop=True)
                            unit_done.inc(last)
                    elif kind in ("ret_norm", "gla_norm"):
                        g = 1 if kind == "ret_norm" else 2
                        pe.wait_ge(norm_wide.sem, norm_wide.at(l, g))
                        u = 0
                        for j in range(2):
                            for h in range(2):
                                for s in ((1, 0) if g == 1 else (0,)):
                                    ps = bank_of(step, u)
                                    for c in range(4):
                                        i = 4 * (4 * h + c) + 2 * j
                                        wide = wide_stat(g, s).rearrange("p j t -> p (j t)")
                                        last = pe.matmul(ps[:, chunk(c)], wide[:, 64 * i:64 * i + P], ident,
                                                         start=True, stop=True)
                                    unit_done.inc(last)
                                    u += 1
                    elif kind == "ret_a":
                        pe.wait_ge(ret_dve.sem, ret_dve.at(l, 2 * n + 1))
                        if n == 0:
                            pe.wait_ge(raw_copied.sem, raw_copied.at(l, copied_count(13)))
                        for j in range(2):
                            transpose(core[2][:, chunk(j)], gb[:, 2 + j, chunk(n)])
                            transpose(core[2][:, chunk(2 + j)], gb[:, 4 + j, chunk(n)])
                        for j in range(2):
                            for i in range(2):
                                r = slice(64 * i, 64 * i + 64)
                                last = pe.matmul(core[i][:, chunk(j)], gb[r, 2 + j, chunk(n)], gb[r, j, chunk(n)],
                                                 start=True, stop=True)
                        ret_pe.inc(last)
                    elif kind == "ret_b":
                        m, kt, v, qg, hs = tmp2k[0], tmp1k[2], tmp1k[3], tmp1k[4], tmp1k[6]
                        pe.wait_ge(ret_act.sem, ret_act.at(l, 2 * n + 1))
                        pe.wait_ge(ret_dve.sem, ret_dve.at(l, 2 * n + 2))
                        for j in range(2):
                            o = core[3][:, 256 * (n % 2) + P * j:256 * (n % 2) + P * j + P]
                            pe.matmul(o, hs[:, chunk(j)], qg[:, chunk(j)], start=True, stop=False,
                                      skip_group_check=True)
                            for i in range(2):
                                hd = 2 * j + i
                                pe.matmul(o[64 * i:64 * i + 64], v[:, chunk(hd, 64)],
                                          m[:, chunk(hd)], start=False, stop=True,
                                          skip_group_check=True)
                        for j in range(2):
                            last = pe.matmul(core[1][:, 256 + P * j:256 + P * j + P], kt[:, chunk(j)], v[:, chunk(j)],
                                             start=True, stop=True)
                        ret_pe.inc(last)
                    elif kind == "gla_gate":
                        pe.wait_ge(lru_w_loaded.sem, lru_w_loaded.at(l, 9))
                        for h in range(2):
                            ps = bank_of(step, h)
                            unit_done.inc(pe.matmul(ps[:], gate_w[:], small[0:16, half_of(h)], start=True, stop=True))
                    elif kind == "gla_a":
                        qz = tmp2k[0]
                        pe.wait_ge(gla_dve.sem, gla_dve.at(l, 3 * n + 2))
                        transpose(core[2][:, 0:P], ga[:, 4, chunk(n)])
                        for j in range(2):
                            transpose(core[2][:, chunk(1 + j)], ga[:, 2 + j, chunk(n)])
                        for i in range(2):
                            last = pe.matmul(core[0][64 * i:64 * i + 64, 0:256],
                                             ga[:, 1, P * n + 64 * i:P * n + 64 * i + 64],
                                             qz[:].rearrange("p (h t) -> p h t", h=4)[:, :, chunk(i, 64)],
                                             start=True, stop=True)
                        gla_pe.inc(last)
                    elif kind in ("gla_b", "gla_c"):
                        m2, kt, v, hs = tmp2k[1], tmp1k[4], tmp1k[5], tmp1k[6]
                        i = 0 if kind == "gla_b" else 1
                        r = slice(64 * i, 64 * i + 64)
                        outs = (core[3], core[1])
                        if i == 0:
                            pe.wait_ge(gla_act.sem, gla_act.at(l, 2 * n + 1))
                            pe.wait_ge(gla_dve.sem, gla_dve.at(l, 3 * n + 3))
                            for j in range(2):
                                for s in range(2):
                                    hd = 2 * j + s
                                    pe.matmul(outs[j][64 * s:64 * s + 64, 0:P], v[:, chunk(hd, 64)], m2[:, chunk(hd)],
                                              start=True, stop=False, skip_group_check=True)
                        else:
                            pe.wait_ge(gla_dve.sem, gla_dve.at(l, 3 * n + 4))
                        for j in range(2):
                            pe.matmul(outs[j][:, r], hs[:, chunk(j)], ga[:, 0, P * n + 64 * i:P * n + 64 * i + 64],
                                      start=False, stop=True, skip_group_check=True)
                        o = core[0][:, 256:512] if i == 0 else core[2][:, 0:256]
                        gla_pe.inc(pe.matmul(o, kt[r, 0:P], v[r, :], start=True, stop=True))
                    elif kind == "lru":
                        pe.wait_ge(lru_xr.sem, lru_xr.at(l, n + 1))
                        u = 0
                        for h in range(2):
                            for m in range(2):
                                ps = bank_of(step, u)
                                unit_done.inc(pe.matmul(ps[:], lru_w[:, m, n, :], gb[:, 2 + n, half_of(h)],
                                                        start=True, stop=True))
                                u += 1

                with pe.Fori(0, KD // 2) as i:
                    for s in range(2):
                        pe.wait_ge(split_done.sem, split_done.at(l, i * 2 + (N_IN + s + 1)))
                        for h in range(2):
                            u = UNIT_OUT + 2 * s + h
                            ps = enter(i + u // 4, u % 4)
                            hi, lo = operand(h)
                            for k in range(KD):
                                pe.wait_ge(y_lo.sem, y_lo.at(l, 8 * h + k + 1))
                                pe.matmul(ps[:], w_hi[s][:, k, :], hi(k), start=(k == 0), stop=False)
                                pe.matmul(ps[:], w_hi[s][:, k, :], lo(k), start=False, stop=False)
                                last = pe.matmul(ps[:], w_lo[s][:, k, :], hi(k), start=False, stop=(k == KD - 1))
                            (tile_done if h else half_done).inc(last, KD // 2)

                def layer_norm(which, unit):
                    for h in range(2):
                        pe.wait_ge(sums_made.sem, sums_made.at(l, 16 * which + 15 + h))
                        for q in range(2):
                            ps = enter((unit + q) // 4, (unit + q) % 4)
                            for c in range(4):
                                last = pe.matmul(ps[:, c:c + 1], tmp[:, 2 * q + h, chunk(c)], one, start=True, stop=True)
                            unit_done.inc(last)
                        pe.wait_ge(ln_rstd.sem, ln_rstd.at(l, 2 * which + h + 1))
                        for q in range(2):
                            ps = enter((unit + 2 + q) // 4, (unit + 2 + q) % 4)
                            for c in range(4):
                                last = pe.matmul(ps[:, chunk(c)], stat[:, q, c:c + 1].to_broadcast([P, P]), ident,
                                                 start=True, stop=True)
                            unit_done.inc(last)
                        unit += 4

                layer_norm(0, UNIT_LN1)

                def ffn_part(unit4, t2, size, times):
                    with pe.Fori(0, size) as i:
                        for h in range(2):
                            hi, lo = operand(h)
                            for s in range(2):
                                if h == 0:
                                    pe.wait_ge(split_done.sem, split_done.at(l, (i + t2) * 2 + (s + 1)))
                                if h == 0 and s == 0:
                                    pe.wait_ge(h_lo.sem, h_lo.at(l, 24))
                                if h == 1 and s == 0:
                                    pe.wait_ge(h_lo.sem, h_lo.at(l, 32))
                                ps = enter(i + unit4, 2 * h + s)
                                (tile_done if h else half_done).inc(large(ps, s, KD, hi, lo), times * size)

                def ffn_down(unit4, t2, size, lo_count, times):
                    with pe.Fori(0, KD // 2) as i:
                        pe.wait_ge(up_lo.sem, lo_count)
                        for s in range(2):
                            pe.wait_ge(split_done.sem, split_done.at(l, (i + t2) * 2 + (s + 1)))
                            for h in range(2):
                                ps = enter(i + unit4, 2 * s + h)
                                last = large(ps, s, size, lambda k: act_hi[:, k, half_of(h)],
                                             lambda k: act_lo[:, k, half_of(h)])
                                (tile_done if h else half_done).inc(last, times * KD // 2)

                u4, t2 = UNIT_FFN // 4, (N_IN + KD) // 2
                with pe.Fori(0, FULL_PARTS) as part:
                    ffn_part(part * (PART + 4) + u4, part * (PART + 4) + t2, PART, FULL_PARTS)
                    ffn_down(part * (PART + 4) + (u4 + PART), part * (PART + 4) + (t2 + PART), PART,
                             up_lo.at(l, (part + 1) * (2 * PART)), FULL_PARTS)
                done = FULL_PARTS * (PART + 4)
                ffn_part(u4 + done, t2 + done, LAST_PART, 1)
                ffn_down(u4 + done + LAST_PART, t2 + done + LAST_PART, LAST_PART, up_lo.at(l, 2 * NF), 1)
                layer_norm(1, UNIT_LN2)

            pe.wait_ge(ax_ready.sem, ax_ready.at(DEPTH, 0))
            for n in range(2 * NCH):
                c, g = divmod(n, 2)
                pe.wait_ge(bank_free[n % 4].sem, bank_free[n % 4].at(DEPTH, n // 4))
                for i in range(4):
                    last = transpose(ring[n % 4][:, chunk(i)], ax[:, 4 * g + i, chunk(c)])
                unit_done.inc(last, 0)

        @block.scalar
        def _(act):
            def f(out_, in_, func, **k):
                return act.activation(out_, in_, func, **k)

            act.wait_ge(c_copied.sem, 1)
            c_tanh.inc(f(c_col[:, 1, :], c_col[:, 0, :], ACT.Tanh, scale=0.5), 1)
            for n in range(3, 19):
                h, k = divmod(n - 3, KD)
                act.wait_ge(unit_done.sem, n + 1)
                bank_free[n % 4].inc(f(ax[:, k, half_of(h)], ring[n % 4][:], ACT.Copy, scale=ALPHA), 0)
            act.sem_inc(ax_ready.sem, 15)
            act.drain().then_inc(ax_ready.sem, 1)
            act.wait_ge(angle_ready.sem, 1)
            f(angle[:, 2, :], angle[:, 0, :], ACT.Sin, scale=0.5)
            angle_sin.inc(f(angle[:, 3, :], angle[:, 0, :], ACT.Sin), 0)

            with act.Fori(0, DEPTH) as l:
                def wait(signal, n):
                    act.wait_ge(signal.sem, signal.at(l, n))

                def products(step, i=0):
                    u = UNIT[step] + i
                    if step[0] == "proj":
                        wait(tile_done if step[2] else half_done, step[1] + 1)
                    else:
                        wait(unit_done, MISC[step] + i + 1)
                    return ring[u % 4]

                def free(step, instruction, i=0):
                    bank_free[(UNIT[step] + i) % 4].inc(instruction)

                def split_h(first, scale, shift):
                    for h in range(2):
                        for k in range(KD):
                            n = 8 * h + k
                            if n >= 2:
                                wait(h_lo, first + n - 1)
                            args = dict(scale=scale[:, k:k + 1], bias=shift[:, k:k + 1])
                            f(tmp[:, 6 + n % 2, :], ax[:, k, half_of(h)], ACT.Identity, **args)
                            f(op_hi[:, k, half_of(h)], ax[:, k, half_of(h)], ACT.Identity, **args)
                            h_value.inc(act.drain())

                def weight_hi(tile, slot, n, times=1):
                    act.wait_ge(raw_loaded[slot].sem, raw_loaded[slot].at(l, n + 1))
                    act.wait_ge(tile_done.sem, tile_done.at(l, tile - 1))
                    w_hi_made.inc(f(w_hi[slot][:], w_raw[slot][:], ACT.Copy), times)

                for s in range(2):
                    weight_hi(s, s, 0)
                act.wait_ge(mod_first.sem, 1)
                wait(ax_ready, 0)
                split_h(0, mod_next[:, 8:16], mod_next[:, 0:8])

                copied = 0
                for step in ORDER:
                    kind, n = step[0], (step[1] if len(step) > 1 else 0)
                    if kind == "params":
                        ps = products(step)
                        free(step, f(par[:], ps[:, 0:N_ROWS], ACT.Copy))
                        wait(heads_loaded, 3)
                        f(head_par[:, 0:4], head_par[:, 0:4], ACT.Exp)
                        lam = col("lru_lambda")
                        act.drain()
                        first = ROWS["lru_lambda"][0]
                        lam = par[:, first:first + 2]
                        f(lru_col[:, 0, :], lam, ACT.Abs)
                        act.drain()
                        f(lru_col[:, 0, :], lru_col[:, 0, :], ACT.Exp, scale=-1.0)
                        par_copied.inc(act.drain())
                    elif kind == "small":
                        ps = products(step)
                        free(step, f(small[:, half_of(n)], ps[0:48, :], ACT.Copy))
                        small_copied.inc(act.drain())
                    elif kind == "dt":
                        wait(dt_x, 1)
                        f(columns[:, 1, :], columns[:, 0, :], ACT.Abs)
                        act.drain()
                        dt_exp.inc(f(columns[:, 1, :], columns[:, 1, :], ACT.Exp, scale=-1.0))
                    elif kind == "proj":
                        h = step[2]
                        if n == 2 and h == 0:
                            act.wait_ge(residual_saved.sem, residual_saved.at(l, 1))
                        if n == 16 and h == 0:
                            wait(y_final, 1)
                        if n == 22 and h == 0:
                            wait(y_final, 2)
                        ps = products(step)
                        if n in silu_tiles:
                            gate_tanh.inc(f(y[:, gate_slot[n], half_of(h)], ps[:], ACT.Tanh, scale=0.5))
                        elif n in gate_slot:
                            i = 2 * (n - 24) + h
                            if i:
                                wait(gelu_in, i)
                            gelu_sq.inc(f(tmp2k[4][:], ps[:], ACT.Square))
                            wait(gelu_in, i + 1)
                            gelu_tanh.inc(f(y[:, gate_slot[n], half_of(h)], y[:, gate_slot[n], half_of(h)],
                                            ACT.Tanh, scale=math.sqrt(2 / math.pi)))
                        else:
                            free(step, f(copied_to(n)[:, half_of(h)], ps[:], ACT.Copy))
                            raw_copied.inc(act.drain())
                        if h == 1:
                            weight_hi(n + 2, n % 2, n // 2 + 1)
                    elif kind == "conv":
                        wait(conv_done, n + 1)
                        conv_tanh.inc(f(conv_b[:], conv_a[:], ACT.Tanh))
                    elif kind == "ssd_a":
                        ed, ec, bt = tmp2k[0], tmp2k[1], tmp1k[7]
                        if n == 0:
                            wait(ssd_dve, 1)
                        wait(ssd_pe, 2 * n + 1)
                        f(bt[:], core[2][:, 256:512], ACT.Copy)
                        ssd_act.inc(f(ec[:], core[0][:], ACT.Exp))
                        wait(ssd_dve, 3 * n + 2)
                        f(ed[:], ed[:], ACT.Exp)
                        f(te[:], te[:], ACT.Exp)
                        ssd_act.inc(act.drain())
                    elif kind in ("ssd_stats", "ret_stats", "gla_stats"):
                        g = ("ssd_stats", "ret_stats", "gla_stats").index(kind)
                        if g == 0:
                            wait(norm_in, 1)
                        else:
                            act.drain()
                        raw, sq = ((y[:, 0:2, :], ga[:, 2:4, :]), (gb[:, 4:6, :], gb[:, 0:2, :]),
                                   (ga[:, 2:4, :], ga[:, 0:2, :]))[g]
                        for j in range(2):
                            last = f(sq[:, j, :], raw[:, j, :], ACT.Square)
                        norm_sq.inc(last)
                        wait(norm_var, g + 1)
                        norm_dev.inc(f(stat[:, 0, :], stat[:, 0, :], ACT.Sqrt, bias=eps))
                        if g:
                            wait(norm_rstd, g + 1)
                            for i in ((0, 1) if g == 1 else (0,)):
                                last = f(wide_stat(g, i).rearrange("p j (c f) -> p (j c) f", f=64),
                                         stat[:, i, :].unsqueeze(2).to_broadcast([P, 32, 64]), ACT.Copy)
                            norm_wide.inc(last)
                    elif kind == "ret_a":
                        wait(ret_pe, 2 * n + 1)
                        ret_act.inc(f(tmp1k[3][:], core[2][:, 256:512], ACT.Copy))
                    elif kind == "ret_b":
                        wait(ret_pe, 2 * n + 2)
                        for j in range(2):
                            last = f(gb[:, 4 + j, chunk(n)], core[3][:, 256 * (n % 2) + P * j:256 * (n % 2) + P * j + P],
                                     ACT.Copy)
                        ret_act.inc(last)
                    elif kind == "gla_gate":
                        wait(gla_gate_x, 1)
                        f(ga[:, 5, :], ga[:, 4, :], ACT.Abs)
                        act.drain()
                        f(ga[:, 5, :], ga[:, 5, :], ACT.Exp, scale=-1.0)
                        act.drain()
                        gla_gate_act.inc(f(ga[:, 5, :], ga[:, 5, :], ACT.Ln, bias=one))
                        wait(gla_cum, 1)
                        f(ga[:, 5, :], ga[:, 4, :], ACT.Exp, scale=1 / 16)
                        act.drain()
                        gla_gate_act.inc(f(ga[:, 4, :], ga[:, 4, :], ACT.Exp, scale=-1 / 16))
                    elif kind == "gla_a":
                        kt, v = tmp1k[4], tmp1k[5]
                        wait(gla_pe, 3 * n + 1)
                        f(kt[:, 0:P], core[2][:, 0:P], ACT.Copy)
                        gla_act.inc(f(v[:], core[2][:, P:3 * P], ACT.Copy))
                    elif kind == "gla_c":
                        wait(gla_pe, 3 * n + 3)
                        for j in range(2):
                            last = f(ga[:, 2 + j, chunk(n)], (core[3], core[1])[j][:, 0:P], ACT.Copy)
                        gla_act.inc(last)
                    elif kind == "lru":
                        e, g = gb[:, 4, :], gb[:, n, :]
                        fi = gb[:, 5, :]
                        ba, bx = col("lru_ba", n), lru_col[:, 3, n:n + 1]
                        if n:
                            wait(lru_dve, n)
                        for h in range(2):
                            ps = products(step, 2 * h)
                            free(step, f(e[:, half_of(h)], ps[:], ACT.Sigmoid, bias=ba), 2 * h)
                            ps = products(step, 2 * h + 1)
                            free(step, f(fi[:, half_of(h)], ps[:], ACT.Tanh, bias=bx, scale=0.5), 2 * h + 1)
                        act.drain()
                        lru_act.inc(f(g, e, ACT.Tanh, scale=lru_col[:, 1, n:n + 1]))
                        lru_act.inc(f(e, e, ACT.Exp, scale=lru_col[:, 2, n:n + 1]))
                        wait(lru_in, n + 1)
                        lru_act.inc(f(g, g, ACT.Sqrt))

                wait(y_final, 4)
                wait(tile_done, N_IN)
                residual_loaded.inc(act.dma_start(ax[:], residual.rearrange("k p t -> p k t")))
                for h in range(2):
                    for k in range(KD):
                        y_hi.inc(f(op_hi[:, k, half_of(h)], y[:, k, half_of(h)], ACT.Copy))

                def layer_norm(which, weight, bias, tile0, slot0):
                    for i in range(16):
                        d, h = divmod(i, 2)
                        if h == 1 and (which == 0 or d < KD - 2):
                            tile = tile0 + d + 2
                            weight_hi(tile, d % 2, slot0 + d // 2 + 1)
                        wait(z_made, 16 * which + i + 1)
                        if i >= 2:
                            wait(sums_made, 16 * which + i - 1)
                        z_sq.inc(f(tmp[:, 4 + i % 2, :], ax[:, d, half_of(h)], ACT.Square))
                    for h in range(2):
                        wait(ln_var, 2 * which + h + 1)
                        ln_dev.inc(f(stat[:, 1, 0:4], stat[:, 1, 0:4], ACT.Sqrt, bias=eps))
                        for k in range(KD):
                            wait(ln_norm, 16 * which + 8 * h + k + 1)
                            last = f(ax[:, k, half_of(h)], ax[:, k, half_of(h)], ACT.Identity,
                                     scale=weight[:, k:k + 1], bias=bias[:, k:k + 1])
                            if which:
                                ax_ready.inc(last)

                def rows(name):
                    first, count = ROWS[name]
                    return par[:, first:first + count]

                layer_norm(0, rows("ln1_w"), rows("ln1_b"), N_IN, N_IN // 2)
                act.drain()
                split_h(16, mod[:, 16:24], mod[:, 8:16])

                def ffn_part(t2, f0, size, times):
                    with act.Fori(0, size) as i:
                        for h in range(2):
                            act.wait_ge((tile_done if h else half_done).sem,
                                        (tile_done if h else half_done).at(l, (i + t2) * 2 + 1))
                            act.wait_ge(up_lo.sem, up_lo.at(l, (i + f0) * 2 + (h - 1)))
                            up_tanh.inc(f(tmp[:, h, :], ring[2 * h][:], ACT.Tanh, scale=0.5), times * size)
                            if h == 1:
                                for s in range(2):
                                    weight_hi((i + t2) * 2 + (2 + s), s, i + t2 + 1, times * size)
                            act.wait_ge(up_act.sem, up_act.at(l, (i + f0) * 2 + (h + 1)))
                            up_hi.inc(f(act_hi[:, bass.ds(i, 1), half_of(h)].rearrange("p a t -> p (a t)"),
                                        tmp[:, 4 + h, :], ACT.Copy), times * size)

                t2 = (N_IN + KD) // 2
                with act.Fori(0, FULL_PARTS) as part:
                    ffn_part(part * (PART + 4) + t2, part * PART, PART, FULL_PARTS)
                    with act.Fori(0, KD // 2) as i:
                        for s in range(2):
                            n2 = i + part * (PART + 4) + (t2 + PART)
                            weight_hi(n2 * 2 + (2 + s), s, n2 + 1, FULL_PARTS * KD // 2)
                ffn_part(t2 + FULL_PARTS * (PART + 4), FULL_PARTS * PART, LAST_PART, 1)
                t2 += FULL_PARTS * (PART + 4) + LAST_PART
                layer_norm(1, rows("ln2_w"), rows("ln2_b"), 2 * t2, t2)

            for n in range(2 * NCH):
                c, g = divmod(n, 2)
                act.wait_ge(unit_done.sem, unit_done.at(DEPTH, n + 1))
                f(x_rows[:, c, half_of(g)], ring[n % 4][:], ACT.Copy, scale=1 / ALPHA)
                bank_free[n % 4].inc(act.drain(), 0)
                out_copied.inc(act.drain(), 0)

        @block.vector
        def _(dve):
            def tt(out_, a_, b_, op):
                return dve.tensor_tensor(out_, a_, b_, op)

            def ts(out_, a_, s0, s1, op0, op1=ALU.bypass):
                return dve.tensor_scalar(out_, a_, s0, s1, op0, op1) if s1 is not None else \
                    dve.tensor_scalar(out_, a_, s0, None, op0)

            def stt(out_, a_, s, b_, op0, op1):
                return dve.scalar_tensor_tensor(out=out_, in0=a_, scalar=s, in1=b_, op0=op0, op1=op1)

            def log1p(e, s, z, p):
                ts(s, e, 2.0, None, ALU.add)
                dve.drain()
                dve.reciprocal(s, s)
                dve.drain()
                tt(s, e, s, ALU.mult)
                dve.drain()
                tt(z, s, s, ALU.mult)
                dve.drain()
                ts(p, z, 1 / 15, None, ALU.mult)
                for n in (13, 11, 9, 7, 5, 3):
                    dve.drain()
                    stt(p, p, 1 / n, z, ALU.add, ALU.mult)
                dve.drain()
                stt(s, p, 1.0, s, ALU.add, ALU.mult)
                dve.drain()
                ts(s, s, 2.0, None, ALU.mult)
                dve.drain()

            dve.sem_inc(up_lo.sem, 2)
            dve.wait_ge(unit_done.sem, 1)
            bank_free[0].inc(dve.tensor_copy(c_col[:, 0, :], ring[0][:, 0:KD]), 0)
            c_copied.inc(dve.drain(), 1)
            for l in range(DEPTH):
                dve.wait_ge(unit_done.sem, 2 + l)
                bank_free[1 + l].inc(dve.tensor_copy(b_ada[:, l, :], ring[1 + l][:, 0:48]), 0)
            dve.wait_ge(c_tanh.sem, 1)
            stt(c_col[:, 0, :], c_col[:, 1, :], 1.0, c_col[:, 0, :], ALU.add, ALU.mult)
            dve.drain()
            c_ready.inc(ts(c_col[:, 0, :], c_col[:, 0, :], 0.5, None, ALU.mult), 0)
            dve.wait_ge(pos_loaded.sem, 16)
            dve.wait_ge(const_loaded.sem, 64)
            dve.tensor_copy(angle[:, 1, :], angle[:, 0, :].bitcast(I32))
            dve.drain()
            ts(angle[:, 0, :], angle[:, 1, :], cst("freq"), None, ALU.mult)
            dve.drain()
            ts(angle[:, 1, :], angle[:, 0, :], 1 / TWO_PI, 12582912.0, ALU.mult, ALU.add)
            dve.drain()
            ts(angle[:, 1, :], angle[:, 1, :], -12582912.0, None, ALU.add)
            rest = TWO_PI
            for bits in (5, 14, None):
                part = rest if bits is None else math.floor(rest * 2 ** bits) / 2 ** bits
                rest -= part
                dve.drain()
                stt(angle[:, 0, :], angle[:, 1, :], -part, angle[:, 0, :], ALU.mult, ALU.add)
            dve.drain()
            angle_ready.inc(ts(angle[:, 0, :], angle[:, 0, :], 3.1415925, -3.1415925, ALU.min, ALU.max), 0)
            dve.wait_ge(angle_sin.sem, 1)
            tt(angle[:, 2, :], angle[:, 2, :], angle[:, 2, :], ALU.mult)
            dve.drain()
            rotary_made.inc(ts(angle[:, 2, :], angle[:, 2, :], -2.0, 1.0, ALU.mult, ALU.add), 0)
            dve.wait_ge(unit_done.sem, UNITS_0)
            bank_free[3].inc(tt(mod_next[:], ring[3][:, 0:16], b_ada[:, 0, 0:16], ALU.add), 0)
            dve.drain()
            mod_first.inc(ts(mod_next[:, 8:16], mod_next[:, 8:16], 1.0, 1 / ALPHA, ALU.add, ALU.mult), 0)

            with dve.Fori(0, DEPTH) as l:
                def wait(signal, n):
                    dve.wait_ge(signal.sem, signal.at(l, n))

                def products(step, i=0):
                    u = UNIT[step] + i
                    if step[0] == "proj":
                        wait(tile_done if step[2] else half_done, step[1] + 1)
                    elif step[0] == "ada":
                        wait(ada_sum_used, step[1] + 1)
                    else:
                        wait(unit_done, MISC[step] + i + 1)
                    return ring[u % 4]

                def free(step, instruction, i=0):
                    bank_free[(UNIT[step] + i) % 4].inc(instruction)

                def split_h(first):
                    for h in range(2):
                        for k in range(KD):
                            n = 8 * h + k
                            wait(h_value, first + n + 1)
                            h_lo.inc(tt(op_lo[:, k, half_of(h)], tmp[:, 6 + n % 2, :],
                                        op_hi[:, k, half_of(h)].bitcast(F32), ALU.subtract))

                split_h(0)

                def convolve(out_, in_, weight, bias):
                    ts(out_, in_, weight(0), bias, ALU.mult, ALU.add)
                    for s in range(1, 4):
                        dve.drain()
                        last = stt(out_[:, s:T], in_[:, 0:T - s], weight(s), out_[:, s:T], ALU.mult, ALU.add)
                    return last

                gate_n = 0
                for step in ORDER:
                    kind, n = step[0], (step[1] if len(step) > 1 else 0)
                    if kind == "params":
                        wait(par_copied, 1)
                        dve.tensor_copy(b_mod[:, 0:32], b_ada[:, bass.ds(l, 1), 16:48].rearrange("p a n -> p (a n)"))
                        dve.tensor_copy(b_mod[:, 32:48], b_ada[:, bass.ds((l + 1) % DEPTH, 1), 0:16]
                                        .rearrange("p a n -> p (a n)"))
                        for i in range(2):
                            r = slice(64 * i, 64 * i + 64)
                            dve.tensor_copy(head_par[r, 12:14], head_par[r, 8 + i:12:2])
                        for r, factor in ((slice(0, 36), 0.5), (slice(ROWS["ln1_w"][0], N_ROWS), ALPHA)):
                            ts(par[:, r], par[:, r], factor, None, ALU.mult)
                        log1p(*(lru_col[:, i, :] for i in (0, 1, 2, 3)))
                        lam = par[:, ROWS["lru_lambda"][0]:ROWS["lru_lambda"][0] + 2]
                        ts(lru_col[:, 0, :], lam, -1.0, 0.0, ALU.mult, ALU.max)
                        dve.drain()
                        tt(lru_col[:, 1, :], lru_col[:, 0, :], lru_col[:, 1, :], ALU.add)
                        dve.drain()
                        ts(lru_col[:, 1, :], lru_col[:, 1, :], 8.0, None, ALU.mult)
                        dve.drain()
                        ts(lru_col[:, 2, :], lru_col[:, 1, :], -1.0, None, ALU.mult)
                        first = ROWS["lru_bx"][0]
                        ts(lru_col[:, 3, :], par[:, first:first + 2], 0.5, None, ALU.mult)
                        par_ready.inc(dve.drain())
                    elif kind == "dt":
                        ps = products(step)
                        heads = lambda i: columns[:, i, :].rearrange("p (c h) -> p c h", h=4)
                        across = lambda r: head_par[:, r].unsqueeze(1).to_broadcast([P, NCH, 4])
                        free(step, tt(heads(0), ps[:, 0:32].rearrange("p (c h) -> p c h", h=4),
                                      across(slice(4, 8)), ALU.add))
                        dt_x.inc(dve.drain())
                        wait(dt_exp, 1)
                        log1p(columns[:, 1, :], columns[:, 2, :], columns[:, 3, :], columns[:, 4, :])
                        stt(columns[:, 0, :], columns[:, 0, :], 0.0, columns[:, 2, :], ALU.max, ALU.add)
                        dve.drain()
                        dt_ready.inc(stt(heads(1), heads(0), -1.0, across(slice(0, 4)), ALU.mult, ALU.mult))
                    elif kind == "dt_cum":
                        ps = products(step)
                        free(step, dve.tensor_copy(columns[:, 2, :], ps[:, 0:32]))
                    elif kind == "ada_sum":
                        wait(ada_loaded[1], n + 1)
                        wait(ada_sum_used, n)
                        ts(ada_sum[1][:], ada_raw[1][:, 0, :], c_col[:, 0, 4:5], None, ALU.mult)
                        for k in range(1, 4):
                            dve.drain()
                            last = stt(ada_sum[1][:], ada_raw[1][:, k, :], c_col[:, 0, 4 + k:5 + k], ada_sum[1][:],
                                       ALU.mult, ALU.add)
                        ada_raw_free[1].inc(last)
                        ada_summed[1].inc(dve.drain())
                    elif kind == "ada":
                        ps = products(step)
                        to, first = (mod, 2 * n) if n < 16 else (mod_next, 2 * n - 32)
                        free(step, tt(to[:, first:first + 2], ps[:, 0:2], b_mod[:, 2 * n:2 * n + 2], ALU.add))
                        if n == ADA_PAIRS - 1:
                            dve.drain()
                            ts(mod[:, 16:24], mod[:, 16:24], 1.0, 1 / ALPHA, ALU.add, ALU.mult)
                            ts(mod_next[:, 8:16], mod_next[:, 8:16], 1.0, 1 / ALPHA, ALU.add, ALU.mult)
                            ts(mod[:, 24:32], mod[:, 24:32], 0.5, None, ALU.mult)
                            dve.drain()
                    elif kind == "proj":
                        h = step[2]
                        if n in silu_tiles:
                            gate_n += 1
                            wait(gate_tanh, gate_n)
                            o = y[:, gate_slot[n], half_of(h)]
                            free(step, stt(o, o, 1.0, ring[UNIT[step] % 4][:], ALU.add, ALU.mult))
                        elif n in gate_slot:
                            i = 2 * (n - 24) + h
                            ps, o, sq = ring[UNIT[step] % 4], y[:, gate_slot[n], half_of(h)], tmp2k[4]
                            wait(gelu_sq, i + 1)
                            ts(sq[:], sq[:], 0.044715, 1.0, ALU.mult, ALU.add)
                            dve.drain()
                            gelu_in.inc(tt(o, sq[:], ps[:], ALU.mult))
                            wait(gelu_tanh, i + 1)
                            free(step, stt(o, o, 1.0, ps[:], ALU.add, ALU.mult))
                    elif kind == "conv":
                        wait(raw_copied, copied_count(n + 2))
                        conv_done.inc(convolve(conv_a[:], ga[:, n, :], lambda s: col("ssd_conv_w", 6 * (3 - s) + n),
                                               col("ssd_conv_b", n)))
                        wait(conv_tanh, n + 1)
                        stt(ga[:, n, :], conv_b[:], 1.0, conv_a[:], ALU.add, ALU.mult)
                        dve.drain()
                    elif kind == "ssd_zero":
                        dve.memset(tmp1k[8][:], 0.0)
                        ssd_dve.inc(dve.drain())
                    elif kind == "ssd_a":
                        ed, ec, g, v, v2 = tmp2k[0], tmp2k[1], tmp1k[4], tmp1k[5], tmp1k[6]
                        wait(ssd_act, 2 * n + 1)
                        by_head = lambda t, m: t.rearrange("p (h m) -> p h m", m=m)
                        cums = by_head(core[0][:], P)
                        for hd in range(4):
                            ts(ed[:, chunk(hd)], core[0][:, chunk(hd)], columns[:, 2, 4 * n + hd:4 * n + hd + 1], 0.0,
                               ALU.subtract, ALU.min)
                        dve.tensor_copy(te[:, 4:8], cums[:, :, P - 1])
                        tt(te[:, 0:4], cums[:, :, P - 1], columns[:, 2, 4 * n:4 * n + 4], ALU.subtract)
                        ssd_dve.inc(dve.drain())
                        tt(by_head(g[:], P), by_head(core[1][:, 0:256], P),
                           cst("causal").unsqueeze(1).to_broadcast([P, 2, P]), ALU.mult)
                        dt4 = columns[:, 0, 4 * n:4 * n + 4].unsqueeze(2).to_broadcast([P, 4, 64])
                        tt(by_head(v[:], 64), by_head(core[2][:, 0:256], 64), dt4, ALU.mult)
                        dve.drain()
                        wait(ssd_act, 2 * n + 2)
                        pair = lambda t: t.rearrange("p (g i m) -> p g i m", g=2, i=2)
                        for gr in range(2):
                            o = ed[:, 256 * gr:256 * gr + 256].rearrange("p (i m) -> p i m", i=2)
                            tt(o, o, g[:, chunk(gr)].unsqueeze(1).to_broadcast([P, 2, P]), ALU.mult)
                            o = ec[:, 256 * gr:256 * gr + 256].rearrange("p (i m) -> p i m", i=2)
                            tt(o, o, ga[:, 4 + gr, chunk(n)].unsqueeze(1).to_broadcast([P, 2, P]), ALU.mult)
                        tt(by_head(v2[:], 64), by_head(v[:], 64), te[:, 0:4].unsqueeze(2).to_broadcast([P, 4, 64]),
                           ALU.mult)
                        ssd_dve.inc(dve.drain())
                    elif kind == "ssd_b":
                        hs = tmp1k[8][:].rearrange("p (h m) -> p h m", m=64)
                        wait(ssd_pe, 2 * n + 2)
                        for j in range(2):
                            o = ga[:, j, chunk(n)]
                            stt(o, o, head_par[:, 12 + j:13 + j],
                                core[3][:, 256 * (n % 2) + P * j:256 * (n % 2) + P * j + P], ALU.mult, ALU.add)
                        tt(hs, hs, te[:, 4:8].unsqueeze(2).to_broadcast([P, 4, 64]), ALU.mult)
                        dve.drain()
                        tt(tmp1k[8][:], tmp1k[8][:], core[1][:, 256:512], ALU.add)
                        ssd_dve.inc(dve.drain())
                    elif kind == "ssd_stats":
                        for j in range(2):
                            tt(y[:, j, :], y[:, j, :], ga[:, j, :], ALU.mult)
                        norm_in.inc(dve.drain())
                        ps = products(step)
                        free(step, ts(stat[:, 0, 0:8], ps[:, 0:8], 1 / (4 * GW), None, ALU.mult))
                        norm_var.inc(dve.memset(stat[:, 0, 8:32], 1.0))
                        wait(norm_dev, 1)
                        norm_rstd.inc(dve.reciprocal(stat[:, 0, :], stat[:, 0, :]))
                    elif kind == "ssd_norm":
                        for h in range(2):
                            ps = products(step, h)
                            for j in range(2):
                                o = y[:, j, half_of(h)]
                                last = stt(o, o, col("ssd_norm_w", j), ps[:], ALU.mult, ALU.mult)
                            free(step, last, h)
                        y_final.inc(dve.drain())
                    elif kind == "rotate":
                        h = step[2]
                        if n == 0 and h == 0:
                            dve.wait_ge(rotary_loaded.sem, rotary_loaded.at(l, 1))
                        ps = products(step)
                        t_ = tmp2k[5]
                        o = gb[:, n, half_of(h)]
                        free(step, tt(t_[:], cos_sin[:, 1, half_of(h)], ps[:], ALU.mult))
                        tt(o, o, cos_sin[:, 0, half_of(h)], ALU.mult)
                        dve.drain()
                        rotate_lo.inc(tt(o, o, t_[:], ALU.add))
                        dve.drain()
                    elif kind == "ret_zero":
                        dve.memset(tmp1k[6][:], 0.0)
                        ret_dve.inc(dve.drain())
                    elif kind == "ret_a":
                        m, kt, qg = tmp2k[0], tmp1k[2], tmp1k[4]
                        wait(ret_act, 2 * n + 1)
                        by = lambda t, w: t.rearrange("p (h m) -> p h m", m=w)
                        for i in range(2):
                            tt(by(m[:], P)[:, i::2, :], by(core[i][:, 0:256], P), by(cst("ret_decay"), P)[:, i::2, :],
                               ALU.mult)
                        tt(by(kt[:], 64), by(core[2][:, 0:256], 64), cst("ret_end").unsqueeze(2).to_broadcast([P, 4, 64]),
                           ALU.mult)
                        tt(by(qg[:], P), gb[:, 0:2, chunk(n)], by(cst("ret_in"), P), ALU.mult)
                        ret_dve.inc(dve.drain())
                    elif kind == "ret_b":
                        st, hs = tmp1k[5], tmp1k[6]
                        wait(ret_pe, 2 * n + 2)
                        by = lambda t, w: t.rearrange("p (h m) -> p h m", m=w)
                        tt(by(st[:], P), by(core[1][:, 256:512], P), cst("block2").unsqueeze(1).to_broadcast([P, 2, P]),
                           ALU.mult)
                        dve.drain()
                        for j in range(2):
                            stt(hs[:, chunk(j)], hs[:, chunk(j)], cst("ret_chunk")[:, j:j + 1], st[:, chunk(j)],
                                ALU.mult, ALU.add)
                        ret_dve.inc(dve.drain())
                    elif kind == "ret_stats":
                        ps = products(step)
                        free_last = ts(stat[:, 1, :], ps[:, 32:64], 1 / 64, None, ALU.mult)
                        dve.drain()
                        tt(stat[:, 2, :], stat[:, 1, :], stat[:, 1, :], ALU.mult)
                        dve.drain()
                        free(step, stt(stat[:, 0, :], ps[:, 0:32], 1 / 64, stat[:, 2, :], ALU.mult, ALU.subtract))
                        norm_var.inc(dve.drain())
                        wait(norm_dev, 2)
                        norm_rstd.inc(dve.reciprocal(stat[:, 0, :], stat[:, 0, :]))
                    elif kind == "ret_norm":
                        u = 0
                        for j in range(2):
                            for h in range(2):
                                o = gb[:, 4 + j, half_of(h)]
                                ps = products(step, u)
                                free(step, tt(o, o, ps[:], ALU.subtract), u)
                                dve.drain()
                                ps = products(step, u + 1)
                                free(step, stt(o, o, col("ret_norm_w", j), ps[:], ALU.mult, ALU.mult), u + 1)
                                dve.drain()
                                tt(y[:, 2 + j, half_of(h)], y[:, 2 + j, half_of(h)], o, ALU.mult)
                                u += 2
                        y_final.inc(dve.drain())
                    elif kind == "gla_gate":
                        for h in range(2):
                            ps = products(step, h)
                            free(step, ts(ga[:, 4, half_of(h)], ps[:], col("gla_bg"), None, ALU.add), h)
                        gla_gate_x.inc(dve.drain())
                        wait(gla_gate_act, 1)
                        stt(ga[:, 4, :], ga[:, 4, :], 0.0, ga[:, 5, :], ALU.min, ALU.subtract)
                        dve.drain()
                        dve.memset(ga[:, 5, :], 1.0)
                        dve.drain()
                        dve.memset(ga[:, 5, 0:T:64], 0.0)
                        dve.drain()
                        gla_cum.inc(dve.tensor_tensor_scan(ga[:, 4, :], ga[:, 5, :], ga[:, 4, :], 0.0, ALU.mult, ALU.add))
                        wait(gla_gate_act, 2)
                        wait(raw_copied, copied_count(19))
                        stt(ga[:, 0, :], ga[:, 0, :], 32 ** -0.5, ga[:, 5, :], ALU.mult, ALU.mult)
                        tt(ga[:, 1, :], ga[:, 1, :], ga[:, 4, :], ALU.mult)
                        dve.drain()
                        by = lambda t: t.rearrange("p (c t) -> p c t", t=64)
                        tt(by(ga[:, 4, :]), by(ga[:, 1, :]),
                           by(ga[:, 5, :])[:, :, 63:64].to_broadcast([P, T // 64, 64]), ALU.mult)
                        dve.drain()
                    elif kind == "gla_zero":
                        dve.memset(tmp1k[6][:], 0.0)
                        dve.memset(tmp2k[1][:], 0.0)
                        gla_dve.inc(dve.drain())
                    elif kind == "gla_a":
                        qz, m2 = tmp2k[0], tmp2k[1]
                        by = lambda t: t.rearrange("p (h t) -> p h t", h=4)
                        tt(by(qz[:]), ga[:, 0, chunk(n)].unsqueeze(1).to_broadcast([P, 4, P]),
                           cst("head4").unsqueeze(2).to_broadcast([P, 4, P]), ALU.mult)
                        gla_dve.inc(dve.drain())
                        wait(gla_pe, 3 * n + 1)
                        for i in range(2):
                            r = slice(64 * i, 64 * i + 64)
                            tt(by(m2[r, :])[:, :, chunk(i, 64)], by(core[0][r, 0:256]),
                               cst("causal64", r).unsqueeze(1).to_broadcast([64, 4, 64]), ALU.mult)
                        gla_dve.inc(dve.drain())
                    elif kind in ("gla_b", "gla_c"):
                        st, hs = tmp1k[7], tmp1k[6]
                        i = 0 if kind == "gla_b" else 1
                        wait(gla_pe, 3 * n + 2 + i)
                        states = core[0][:, 256:512] if i == 0 else core[2][:, 0:256]
                        tt(st[:], states, cst("block4"), ALU.mult)
                        dve.drain()
                        end = P * n + 64 * i + 63
                        stt(hs[:], hs[:], ga[:, 5, end:end + 1], st[:], ALU.mult, ALU.add)
                        if i == 0:
                            gla_dve.inc(dve.drain())
                        else:
                            dve.drain()
                    elif kind == "gla_stats":
                        ps = products(step)
                        free(step, ts(stat[:, 0, :], ps[:, 0:32], 1 / 64, None, ALU.mult))
                        norm_var.inc(dve.drain())
                        wait(norm_dev, 3)
                        norm_rstd.inc(dve.reciprocal(stat[:, 0, :], stat[:, 0, :]))
                    elif kind == "gla_norm":
                        u = 0
                        for j in range(2):
                            for h in range(2):
                                o = ga[:, 2 + j, half_of(h)]
                                ps = products(step, u)
                                free(step, stt(o, o, col("gla_norm_w", j), ps[:], ALU.mult, ALU.mult), u)
                                dve.drain()
                                tt(y[:, 6 + j, half_of(h)], y[:, 6 + j, half_of(h)], o, ALU.mult)
                                u += 1
                        y_final.inc(dve.drain())
                    elif kind == "lru":
                        xr, e, fi, g = gb[:, 2 + n, :], gb[:, 4, :], gb[:, 5, :], gb[:, n, :]
                        wait(raw_copied, copied_count(22 + n))
                        lru_xr.inc(convolve(xr, g, lambda s: col("lru_conv_w", 2 * (3 - s) + n), col("lru_conv_b", n)))
                        wait(lru_act, 3 * n + 1)
                        stt(fi, fi, 1.0, xr, ALU.add, ALU.mult)
                        dve.drain()
                        wait(lru_act, 3 * n + 2)
                        tt(xr, e, e, ALU.mult)
                        dve.drain()
                        lru_in.inc(stt(g, xr, 1.0, g, ALU.add, ALU.mult))
                        wait(lru_act, 3 * n + 3)
                        tt(fi, fi, g, ALU.mult)
                        dve.drain()
                        lru_dve.inc(dve.tensor_tensor_scan(g, e, fi, 0.0, ALU.mult, ALU.add))

                for j in range(2):
                    stt(y[:, 4 + j, :], gb[:, j, :], 0.25, y[:, 4 + j, :], ALU.mult, ALU.mult)
                y_final.inc(dve.drain())
                for h in range(2):
                    for k in range(KD):
                        wait(y_hi, 8 * h + k + 1)
                        y_lo.inc(tt(op_lo[:, k, half_of(h)], y[:, k, half_of(h)],
                                    op_hi[:, k, half_of(h)].bitcast(F32), ALU.subtract))

                def add_products(d, h, bank, signal, tile, gate):
                    dve.wait_ge(signal.sem, signal.at(l, tile))
                    o = ax[:, d, half_of(h)]
                    return stt(o, ring[bank][:], gate[:, d:d + 1], o, ALU.mult, ALU.add)

                def layer_norm(which, unit, misc, bank0, tile0, gate):
                    def add_square(i):
                        d, h = divmod(i, 2)
                        wait(z_sq, 16 * which + i + 1)
                        q = tmp[:, 2 + h, :]
                        if d == 0:
                            sums_made.inc(dve.tensor_copy(q, tmp[:, 4 + i % 2, :]))
                        else:
                            sums_made.inc(tt(q, q, tmp[:, 4 + i % 2, :], ALU.add))

                    for i in range(16):
                        d, h = divmod(i, 2)
                        bank = (bank0 + i) % 4
                        bank_free[bank].inc(add_products(d, h, bank, tile_done if h else half_done, tile0 + d + 1, gate))
                        z_made.inc(dve.drain())
                        o = tmp[:, h, :]
                        if d == 0:
                            dve.tensor_copy(o, ax[:, d, half_of(h)])
                        else:
                            tt(o, o, ax[:, d, half_of(h)], ALU.add)
                        if i:
                            add_square(i - 1)
                    add_square(15)
                    for h in range(2):
                        wait(unit_done, misc + 1)
                        ps = ring[unit % 4]
                        bank_free[unit % 4].inc(ts(stat[:, 0, 0:4], ps[:, 0:4], 1 / D, None, ALU.mult))
                        dve.drain()
                        tt(stat[:, 2, 0:4], stat[:, 0, 0:4], stat[:, 0, 0:4], ALU.mult)
                        dve.drain()
                        wait(unit_done, misc + 2)
                        ps = ring[(unit + 1) % 4]
                        bank_free[(unit + 1) % 4].inc(stt(stat[:, 1, 0:4], ps[:, 0:4], 1 / D, stat[:, 2, 0:4],
                                                          ALU.mult, ALU.subtract))
                        ln_var.inc(dve.drain())
                        wait(ln_dev, 2 * which + h + 1)
                        ln_rstd.inc(dve.reciprocal(stat[:, 1, 0:4], stat[:, 1, 0:4]))
                        wait(unit_done, misc + 4)
                        mean, rstd = ring[(unit + 2) % 4], ring[(unit + 3) % 4]
                        for k in range(KD):
                            o = ax[:, k, half_of(h)]
                            last = tt(o, o, mean[:], ALU.subtract)
                            if k == KD - 1:
                                bank_free[(unit + 2) % 4].inc(last)
                            dve.drain()
                            tt(o, o, rstd[:], ALU.mult)
                            ln_norm.inc(dve.drain())
                        bank_free[(unit + 3) % 4].inc(dve.drain())
                        unit, misc = unit + 4, misc + 4

                dve.wait_ge(residual_loaded.sem, residual_loaded.at(l, 1))
                layer_norm(0, UNIT_LN1, MISC_LN1, UNIT_OUT % 4, N_IN, mod[:, 0:8])
                split_h(16)

                def ffn_part(t2, f0, size, times):
                    with dve.Fori(0, size) as i:
                        for h in range(2):
                            n = (i + f0) * 2 + (h + 1)
                            dve.wait_ge(up_tanh.sem, up_tanh.at(l, n))
                            bank_free[2 * h].inc(stt(tmp[:, 2 + h, :], tmp[:, h, :], 1.0, ring[2 * h][:],
                                                     ALU.add, ALU.mult), times * size)
                            done = tile_done if h else half_done
                            dve.drain()
                            dve.wait_ge(done.sem, done.at(l, (i + t2) * 2 + 2))
                            bank_free[2 * h + 1].inc(tt(tmp[:, 4 + h, :], tmp[:, 2 + h, :], ring[2 * h + 1][:],
                                                        ALU.mult), times * size)
                            up_act.inc(dve.drain(), times * size)
                            dve.wait_ge(up_hi.sem, up_hi.at(l, n))
                            hidden = lambda t: t[:, bass.ds(i, 1), half_of(h)].rearrange("p a t -> p (a t)")
                            up_lo.inc(tt(hidden(act_lo), tmp[:, 4 + h, :], hidden(act_hi).bitcast(F32),
                                         ALU.subtract), times * size)

                t2 = (N_IN + KD) // 2
                with dve.Fori(0, FULL_PARTS) as part:
                    ffn_part(part * (PART + 4) + t2, part * PART, PART, FULL_PARTS)
                    for d in range(KD):
                        for h in range(2):
                            bank = (2 * d + h) % 4
                            bank_free[bank].inc(add_products(
                                d, h, bank, tile_done if h else half_done,
                                (part * (PART + 4) + (t2 + PART)) * 2 + (d + 1), mod[:, 24:32]), FULL_PARTS)
                t2 += FULL_PARTS * (PART + 4)
                ffn_part(t2, FULL_PARTS * PART, LAST_PART, 1)
                layer_norm(1, UNIT_LN2, MISC_LN2, 0, 2 * (t2 + LAST_PART), mod[:, 24:32])

        wrong = [(s.name, s.layer, s.counted) for s in Signal.all if s.layer and s.layer != s.counted]
        assert not wrong, wrong


_INS = ["x", "c", "positions", "w_ada", "b_ada", "w_in", "ssd_conv_w", "ssd_conv_b", "ssd_dt_bias", "ssd_a_log",
        "ssd_d", "ssd_norm_w", "ret_norm_w", "lru_conv_w", "lru_conv_b", "lru_wa", "lru_ba", "lru_wx", "lru_bx",
        "lru_lambda", "gla_wg2", "gla_bg", "gla_norm_w", "w_out", "ln1_w", "ln1_b", "ffn_w_up", "ffn_w_down",
        "ln2_w", "ln2_b"]


def kernel(**inputs):
    import numpy as _np
    import concourse.bacc as _bacc
    from concourse import mybir as _mybir
    from concourse.bass_utils import run_bass_kernel_spmd as _run

    nc = _bacc.Bacc("TRN2", target_bir_lowering=False, num_devices=1)
    arrays, args = {}, {}
    for name in _INS + ["const"]:
        v = constants() if name == "const" else _np.ascontiguousarray(inputs[name])
        arrays[f"in_{name}"] = v
        args[name] = nc.dram_tensor(f"in_{name}", v.shape, _mybir.dt.from_np(v.dtype), kind="ExternalInput").ap()
    out = nc.dram_tensor("out_0", (1, T, D), _mybir.dt.float32, kind="ExternalOutput").ap()
    nc.disable_value_cache = True
    build(nc, args, out)
    return _run(nc, [arrays], core_ids=[0]).results[0]["out_0"]
```

```python
import math
from contextlib import ExitStack

import numpy as np

import concourse.bass as bass
import concourse.mybir as mybir

F32 = mybir.dt.float32
F32R = mybir.dt.float32r
I32 = mybir.dt.int32
ALU = mybir.AluOpType
ACT = mybir.ActivationFunctionType

P = 128
D = 1024
T = 1024
DEPTH = 2
KD = D // P
HALF = 512
GW = 256
CH = 128
NCH = T // CH
XBC = 768
D_FF = 2816
NF = D_FF // P
PART = 6
ALPHA = (2 * DEPTH) ** 0.25
EPS = 1e-5
TWO_PI = 2 * math.pi

COL_Z, COL_XBC, COL_DT = 0, 256, 1024
COL_RET = 1028
COL_LRU_GATE, COL_LRU_X = 2052, 2308
COL_GLA_QKV, COL_GLOW, COL_GLA_R = 2564, 3076, 3092

IN_SEGMENTS = [(COL_Z, 8), (COL_RET, 8), (COL_GLA_QKV, 4), (COL_GLA_R, 2), (COL_LRU_X, 2), (COL_LRU_GATE, 2)]
N_IN = sum(n for _, n in IN_SEGMENTS)
FULL_PARTS = NF // PART
LAST_PART = NF - FULL_PARTS * PART
N_TILES = N_IN + KD + 2 * NF + (FULL_PARTS + 1) * KD
ADA_PAIRS = 24

ROWS = {}
_n = 0
for _name, _count in [("ssd_conv_w", 24), ("ssd_conv_b", 6), ("ssd_norm_w", 2), ("ret_norm_w", 2),
                      ("gla_norm_w", 2), ("lru_conv_w", 8), ("lru_conv_b", 2), ("lru_ba", 2),
                      ("lru_bx", 2), ("lru_lambda", 2), ("gla_bg", 1), ("ln1_w", 8), ("ln1_b", 8),
                      ("ln2_w", 8), ("ln2_b", 8)]:
    ROWS[_name] = (_n, _count)
    _n += _count
N_ROWS = _n

CONST = {}
_n = 0
for _name, _count in [("ident", 128), ("causal", 128), ("perm", 128), ("ret_decay", 512),
                      ("ret_in", 256), ("block2", 128), ("block4", 256), ("causal64", 64),
                      ("ret_end", 4), ("head4", 4), ("ret_chunk", 2), ("freq", 1), ("eps", 1),
                      ("head2", 2), ("one", 1)]:
    CONST[_name] = (_n, _count)
    _n += _count
N_CONST = _n


def constants():
    c = np.zeros((P, N_CONST), np.float64)
    p = np.arange(P)

    def put(name, value):
        a, n = CONST[name]
        c[:, a:a + n] = np.asarray(value).reshape(P, n)

    gamma = 1.0 - 2.0 ** (-5.0 - np.arange(4))
    put("ident", np.eye(P))
    put("causal", p[:, None] <= p[None, :])
    perm = np.zeros((P, P))
    for m in range(P):
        perm[m + 32 if m % 64 < 32 else m - 32, m] = -1.0 if m % 64 < 32 else 1.0
    put("perm", perm)
    lag = p[None, :] - p[:, None]
    put("ret_decay", np.stack([np.where(lag >= 0, g ** np.maximum(lag, 0), 0) * 0.125 for g in gamma], 1))
    put("ret_in", np.stack([gamma[2 * j + p // 64][:, None] ** (p + 1.0) for j in range(2)], 1))
    put("block2", p[:, None] // 64 == p[None, :] // 64)
    put("block4", p[:, None] // 32 == np.arange(256)[None, :] // 64)
    put("causal64", p[:, None] % 64 <= np.arange(64)[None, :])
    put("ret_end", 0.125 * gamma[None, :] ** (127.0 - p[:, None]))
    put("head4", p[:, None] // 32 == np.arange(4)[None, :])
    put("ret_chunk", np.stack([gamma[2 * j + p // 64] ** 128.0 for j in range(2)], 1))
    put("freq", 10000.0 ** (-(p % 32) / 32.0))
    put("eps", np.full(P, EPS))
    put("head2", p[:, None] // 64 == np.arange(2)[None, :])
    put("one", np.ones(P))
    return c.astype(np.float32)


def mixer_order():
    order = [("params",), ("small", 0), ("small", 1)]

    def tile(t):
        group = [("proj", t, 0), ("proj", t, 1)]
        if t < ADA_PAIRS:
            group = [("ada_sum", t)] + group + [("ada", t)]
        return group

    def spread(units, groups):
        halves = sum(u[0] == "proj" for u in units)
        n, seen, out = 0, 0, []
        for u in units:
            out.append(u)
            if u[0] == "proj":
                seen += 1
                want = len(groups) * seen // halves
                out += sum(groups[n:want], [])
                n = want
        return out

    for t in range(8):
        order += tile(t)
        if t == 0:
            order += [("dt",), ("dt_cum",)]
        if 2 <= t:
            order.append(("conv", t - 2))
    def pipelined(name):
        groups = [[(name + "_zero",), (name + "_pre", 0), (name + "_mid", 0)]]
        for c in range(NCH):
            more = c + 1 < NCH
            groups.append([(name + "_pre", c + 1)] * more + [(name + "_b", c)] + [(name + "_mid", c + 1)] * more)
        return groups

    order += tile(8)
    units = []
    for t in range(9, 15):
        units += tile(t)
        if t <= 12:
            units += [("rotate", t - 9, 0), ("rotate", t - 9, 1)]
    order += spread(units, pipelined("ssd"))
    order += [("ssd_gate",)]
    ret = pipelined("ret")
    t15, t16 = tile(15), tile(16)
    order += t15[:2] + ret[0] + t15[2:3] + [("ssd_stats",)] + t15[3:] + ret[1]
    order += t16[:2] + [("ssd_norm",)] + ret[2] + t16[2:] + [("gla_gate",)]
    units = []
    for t in range(17, 20):
        units += tile(t)
    order += spread(units, ret[3:]) + [("ret_square",), ("gla_scale",)]
    gla = [[("gla_c", c - 1)] * (c > 0) + [("gla_b", c)] * (c < NCH) +
           [("gla_pre", c + 1), ("gla_mid", c + 1)] * (c + 1 < NCH) for c in range(NCH + 1)]
    t20, t21, t22, t23, t24 = (tile(t) for t in range(20, 25))
    order += t20[:2] + [("gla_zero",), ("gla_pre", 0), ("gla_mid", 0)] + t20[2:3] + [("ret_stats",)] + t20[3:] + gla[0]
    order += t21[:2] + [("ret_norm",)] + gla[1] + t21[2:] + gla[2]
    order += t22[:2] + gla[3] + t22[2:] + [("lru_conv", 0)] + gla[4]
    order += t23[:2] + [("lru", 0)] + gla[5] + t23[2:] + [("lru_gate", 0), ("lru_conv", 1)] + gla[6]
    order += t24[:1] + [("lru_scan", 0)] + gla[7] + [("lru", 1)] + t24[1:] + gla[8]
    order += [("gla_square",), ("lru_gate", 1), ("proj", 25, 0), ("lru_scan", 1), ("lru_out", 0), ("lru_out", 1),
              ("lru_out", 2), ("gla_stats",)]
    order += [("y_split", k) for k in range(6)]
    order += [("proj", 25, 1), ("lru_out", 3), ("gla_norm", 0), ("y_split", 6), ("y_split", 7), ("gla_norm", 1)]
    order += [("y_split", k) for k in range(8, 16)]
    return order


ORDER = mixer_order()
UNITS_OF = {"params": 1, "small": 1, "dt": 1, "dt_cum": 1, "proj": 1, "ada": 1, "rotate": 1,
            "ssd_stats": 1, "ssd_norm": 2, "ret_stats": 1, "ret_norm": 8, "gla_stats": 1, "gla_norm": 2,
            "gla_gate": 2, "lru": 4}
UNIT = {}
_n = 0
for _step in ORDER:
    UNIT[_step] = _n
    _n += UNITS_OF.get(_step[0], 0)
UNIT_OUT = _n
MISC = {}
_n = 0
for _step in ORDER:
    MISC[_step] = _n
    _n += 0 if _step[0] in ("proj", "ada") else UNITS_OF.get(_step[0], 0)
MISC_LN1 = _n
MISC_LN2 = MISC_LN1 + 8
N_MISC = MISC_LN2 + 8
UNIT_LN1 = UNIT_OUT + 2 * KD
UNIT_FFN = UNIT_LN1 + 8
UNIT_LN2 = UNIT_FFN + 4 * NF + 2 * KD * (FULL_PARTS + 1)
UNITS = UNIT_LN2 + 8
UNITS_0 = 20
assert UNIT_FFN % 4 == 0 and UNIT_LN2 % 4 == 0 and UNITS % 4 == 0 and UNITS_0 % 4 == 0


class Signal:

    all = []

    def __init__(self, ctx, nc, name, layer, before=0, step=1):
        self.sem = ctx.enter_context(nc.semaphore(name))
        self.name, self.layer, self.before, self.step = name, layer, before, step
        self.counted = 0
        Signal.all.append(self)

    def inc(self, instruction, times=1):
        self.counted += times
        instruction.then_inc(self.sem, self.step)

    def at(self, l, n):
        return l * (self.layer * self.step) + n * self.step + self.before * self.step


def build(nc, a, out):
    Signal.all = []
    ctx = ExitStack()
    with ctx:
        KB = 1024
        place_at = [(nc.sbuf_base + 63) // 64 * 64]

        def region(size):
            offset = place_at[0]
            place_at[0] += (size + 31) // 32 * 32
            assert place_at[0] <= nc.sbuf_usable_end, place_at[0] - nc.sbuf_usable_end
            return offset

        def place(name, shape, dt=F32, at=None):
            if at is None:
                at = region(4 * int(np.prod(shape[1:])))
            return nc.alloc_sbuf_tensor_at(name, shape, dt, offset=at)

        op_hi = place("op_hi", [P, KD, T], F32R)
        op_lo = place("op_lo", [P, KD, T], F32R)
        ada_first = nc.alloc_sbuf_tensor_at("ada_first", [P, KD, 2 * D], F32, offset=place_at[0] - 64 * KB)
        w_raw = [place(f"w_raw{i}", [P, KD, P]) for i in range(2)]
        w_hi = [place(f"w_hi{i}", [P, KD, P], F32R) for i in range(2)]
        w_lo = [place(f"w_lo{i}", [P, KD, P], F32R) for i in range(2)]
        ada_raw = [place(f"ada_raw{i}", [P, 4, 256]) for i in range(2)]
        ada_sum = [place(f"ada_sum{i}", [P, 256]) for i in range(2)]
        X = region(32 * KB)
        Y = region(48 * KB)
        TMP = region(16 * KB)
        ax = place("ax", [P, KD, T], at=X)
        act_hi = place("act_hi", [P, PART, T], F32R, at=Y)
        act_lo = place("act_lo", [P, PART, T], F32R, at=Y + 24 * KB)
        x_rows = place("x_rows", [P, 8, D], at=Y)
        angle = place("angle", [P, 4, T], at=Y + 32 * KB)
        ga = place("ga", [P, 6, T], at=X)
        gb = place("gb", [P, 6, T], at=X + 24 * KB)
        y = place("y", [P, 8, T], at=Y + 16 * KB)
        cos_sin = place("cos_sin", [P, 2, T], at=Y + 32 * KB)
        small_hi = place("small_hi", [P, KD * 48 + 80], F32R, at=Y + 40 * KB)
        small_lo = place("small_lo", [P, KD * 48 + 80], F32R, at=Y + 42 * KB)
        tmp = place("tmp", [P, 8, HALF], at=TMP)
        small = place("small", [48, T], at=TMP)
        tmp2k = [place(f"tmp2k{i}", [P, HALF], at=TMP + (4 + 2 * i) * KB) for i in range(6)]
        tmp1k = [place(f"tmp1k{i}", [P, 256], at=TMP + (4 + i) * KB) for i in range(12)]
        gla_m = [tmp2k[1], place("gla_m1", [P, HALF], at=TMP)]
        gla_v = [tmp1k[5], place("gla_v1", [P, 256], at=TMP + 3 * KB)]
        gla_k = tmp1k[4]
        gla_h = [tmp1k[6], tmp1k[7], tmp1k[10]]
        gla_st = [tmp1k[11], place("gla_st1", [P, 256], at=TMP + 2 * KB)]
        conv_a = place("conv_a", [P, T], at=TMP + 4 * KB)
        conv_b = place("conv_b", [P, T], at=TMP + 8 * KB)
        const = place("consts", [P, N_CONST])
        par = place("par", [P, N_ROWS])
        par_rows = place("par_rows", [N_ROWS, P])
        b_ada = place("b_ada_columns", [P, DEPTH, 48])
        b_ada_rows = place("b_ada_rows", [48, DEPTH, P])
        mod = place("mod", [P, 32])
        mod_next = place("mod_next", [P, 16])
        b_mod = place("b_mod", [P, 48])
        c_rows = place("c_rows", [KD, P])
        c_col = place("c_col", [P, 2, KD])
        lru_w = place("lru_w", [P, 2, 2, P])
        gate_w = place("gate_w", [16, P])
        head_par = place("head_par", [P, 14])
        columns = place("columns", [P, 5, 32])
        lru_col = place("lru_col", [P, 6, 2])
        stat = place("stat", [P, 4, 32])
        te = place("te", [P, 8])

        ring = [ctx.enter_context(nc.psum_tensor(f"ring{i}", [P, HALF], F32)) for i in range(4)]
        core = [ctx.enter_context(nc.psum_tensor(f"core{i}", [P, HALF], F32)) for i in range(4)]
        residual = nc.dram_tensor("residual", (KD, P, T), F32, kind="Internal").ap()
        rotary = nc.dram_tensor("rotary", (2, P, T), F32, kind="Internal").ap()

        def signal(name, layer, before=0, step=1):
            return Signal(ctx, nc, name, layer, before, step)

        const_loaded = signal("const_loaded", 0, 4, 16)
        x_loaded = [signal(f"x_loaded{i}", 0, 1, 16) for i in range(4)]
        pos_loaded = signal("pos_loaded", 0, 1, 16)
        rows_loaded = signal("rows_loaded", 15, 0, 16)
        heads_loaded = signal("heads_loaded", 3, 0, 16)
        lru_w_loaded = signal("lru_w_loaded", 9, 0, 16)
        small_loaded = signal("small_loaded", 2, 0, 16)
        raw_loaded = [signal(f"raw_loaded{i}", N_TILES // 2, 0, 16) for i in range(2)]
        raw_free = [signal(f"raw_free{i}", N_TILES // 2, 1) for i in range(2)]
        split_done = signal("split_done", N_TILES)
        half_done = signal("half_done", N_TILES)
        tile_done = signal("tile_done", N_TILES, 2)
        small_split = signal("small_split", 1)
        zeroed = signal("zeroed", 0, 1)
        pool_passed = signal("pool_passed", 0)
        ada_first_loaded = [signal(f"ada_first_loaded{i}", 0, 1, 16) for i in range(4)]
        ada_loaded = [signal(f"ada_loaded{i}", ADA_PAIRS, 0, 16) for i in range(2)]
        ada_raw_free = [signal(f"ada_raw_free{i}", ADA_PAIRS + 1 - i, 1) for i in range(2)]
        ada_summed = [signal(f"ada_summed{i}", ADA_PAIRS) for i in range(2)]
        ada_sum_used = signal("ada_sum_used", ADA_PAIRS, 1)
        w_hi_made = signal("w_hi_made", N_TILES)
        residual_saved = signal("residual_saved", 1, 0, 16)
        residual_loaded = signal("residual_loaded", 1, 0, 16)
        rotary_saved = signal("rotary_saved", 0, 1, 16)
        rotary_loaded = signal("rotary_loaded", 1, 0, 16)
        bank_free = [signal(f"bank_free{i}", UNITS // 4, UNITS_0 // 4) for i in range(4)]
        unit_done = signal("unit_done", N_MISC, UNITS_0)
        ax_ready = signal("ax_ready", 16, 16)
        h_value = signal("h_value", 32)
        y_hi = signal("y_hi", 16)
        gate_tanh = signal("gate_tanh", 12)
        raw_copied = signal("raw_copied", 36)
        conv_tanh = signal("conv_tanh", 6)
        small_copied = signal("small_copied", 2)
        par_copied = signal("par_copied", 1)
        dt_exp = signal("dt_exp", 1)
        ssd_copied = signal("ssd_copied", NCH)
        ssd_exp = signal("ssd_exp", NCH)
        ret_v = signal("ret_v", NCH)
        gla_kv = signal("gla_kv", NCH)
        gla_out = signal("gla_out", NCH)
        gla_gate_act = signal("gla_gate_act", 2)
        norm_sq = signal("norm_sq", 3)
        norm_dev = signal("norm_dev", 3)
        norm_wide = signal("norm_wide", 2)
        lru_act = signal("lru_act", 6)
        gelu_sq = signal("gelu_sq", 4)
        gelu_tanh = signal("gelu_tanh", 4)
        z_sq = signal("z_sq", 32)
        ln_dev = signal("ln_dev", 4)
        up_tanh = signal("up_tanh", 2 * NF)
        up_hi = signal("up_hi", 2 * NF)
        c_copied = signal("c_copied", 0, 1)
        c_tanh = signal("c_tanh", 0, 1)
        angle_sin = signal("angle_sin", 0, 1)
        out_copied = signal("out_copied", 0, 16)
        h_lo = signal("h_lo", 32)
        y_lo = signal("y_lo", 16)
        y_final = signal("y_final", 2)
        lru_final = signal("lru_final", 4)
        gla_final = signal("gla_final", 4)
        par_ready = signal("par_ready", 1)
        conv_done = signal("conv_done", 6)
        dt_x = signal("dt_x", 1)
        dt_ready = signal("dt_ready", 1)
        ssd_exponents = signal("ssd_exponents", NCH)
        ssd_banks_read = signal("ssd_banks_read", NCH)
        ssd_operands = signal("ssd_operands", NCH)
        ssd_state = signal("ssd_state", NCH + 1)
        rotate_lo = signal("rotated", 8)
        ret_operands = signal("ret_operands", NCH)
        ret_state = signal("ret_state", NCH + 1)
        gla_zeroed = signal("gla_zeroed", 1)
        gla_masked = signal("gla_masked", NCH)
        gla_state = signal("gla_state", NCH)
        gla_gate_x = signal("gla_gate_x", 1)
        gla_cum = signal("gla_cum", 1)
        norm_in = signal("norm_in", 1)
        norm_var = signal("norm_var", 3)
        norm_rstd = signal("norm_rstd", 3)
        lru_xr = signal("lru_xr", 2)
        lru_dve = signal("lru_dve", 2)
        lru_in = signal("lru_in", 2)
        gelu_in = signal("gelu_in", 4)
        z_made = signal("z_made", 32)
        sums_made = signal("sums_made", 32)
        ln_var = signal("ln_var", 4)
        ln_rstd = signal("ln_rstd", 4)
        ln_norm = signal("ln_norm", 32)
        up_act = signal("up_act", 2 * NF)
        up_lo = signal("up_lo", 2 * NF, 2)
        c_ready = signal("c_ready", 0, 1)
        mod_first = signal("mod_first", 0, 1)
        angle_ready = signal("angle_ready", 0, 1)
        rotary_made = signal("rotary_made", 0, 1)
        ssd_pre_done = signal("ssd_pre_done", NCH)
        ssd_b_done = signal("ssd_b_done", NCH)
        ret_pre_done = signal("ret_pre_done", NCH)
        ret_b_done = signal("ret_b_done", NCH)
        gla_pre_done = signal("gla_pre_done", NCH)
        gla_b_done = signal("gla_b_done", NCH)
        gla_c_done = signal("gla_c_done", NCH)
        out_saved = signal("out_saved", 0, 8, 16)

        def cst(name, rows=slice(None)):
            first, n = CONST[name]
            return const[rows, first:first + n]

        def col(name, i=0):
            first, _ = ROWS[name]
            return par[:, first + i:first + i + 1]

        ident, eps, one = cst("ident"), cst("eps"), cst("one")

        def chunk(c, n=CH):
            return slice(c * n, (c + 1) * n)

        def half_of(h):
            return slice(h * HALF, (h + 1) * HALF)

        gate_slot = {0: 0, 1: 1, 14: 2, 15: 3, 20: 6, 21: 7, 24: 4, 25: 5}
        silu_tiles = [0, 1, 14, 15, 20, 21]
        copied_tiles = [t for t in range(N_IN) if t not in gate_slot]

        def copied_to(t):
            if t < 8:
                return ga[:, t - 2, :]
            if t < 14:
                return gb[:, t - 8, :]
            if t < 20:
                return ga[:, t - 16, :]
            return gb[:, t - 22, :]

        def copied_count(t):
            return 2 * copied_tiles.index(t) + 2

        def wide_stat(g, s):
            return gb[:, 2 * s:2 * s + 2, :] if g == 1 else ga[:, 0:2, :]

        block = ctx.enter_context(nc.Block())

        @block.sync
        def _(sp):
            const_loaded.inc(sp.dma_start(const[:], a["const"]))
            const_loaded.inc(sp.dma_start(c_rows[:], a["c"].rearrange("b (k p) -> (b k) p", p=P)))
            for l in range(DEPTH):
                const_loaded.inc(sp.dma_start(b_ada_rows[:, l, :], a["b_ada"][l, :].rearrange("(k p) -> k p", p=P)))
            for i in range(4):
                x_loaded[i].inc(sp.dma_start(
                    x_rows[:, 2 * i:2 * i + 2, :],
                    a["x"][0, 256 * i:256 * i + 256, :].rearrange("(k p) d -> p k d", p=P)))
            pos_loaded.inc(sp.dma_start(angle[:, 0, :].bitcast(I32), a["positions"][0, :].partition_broadcast(P)))

            for i in range(4):
                ada_first_loaded[i].inc(sp.dma_start(
                    ada_first[:, :, 512 * i:512 * i + 512],
                    a["w_ada"][0, :, 512 * i:512 * i + 512].rearrange("(k p) n -> p k n", p=P)))
            sp.wait_ge(rotary_made.sem, 1)
            rotary_saved.inc(sp.dma_start(rotary.rearrange("a p t -> p a t"), angle[:, 2:4, :]))
            sp.wait_ge(rotary_saved.sem, 16)

            with sp.Fori(0, DEPTH) as l:
                def layer_of(name, at=None):
                    return a[name][bass.ds(l if at is None else at, 1)]

                def load_tile(slot, n, name, row0, rows, col0, times=1):
                    sp.wait_ge(raw_free[slot].sem, raw_free[slot].at(l, n))
                    src = layer_of(name).rearrange("a m n -> (a m) n")[bass.ds(row0, rows * P), bass.ds(col0, P)]
                    raw_loaded[slot].inc(sp.dma_start(w_raw[slot][:, 0:rows, :],
                                                      src.rearrange("(k p) n -> p k n", p=P)), times)

                def load_ada_pair(pair, layer, col0, times=1):
                    for q in range(2):
                        src = layer_of("w_ada", layer).rearrange("a m n -> (a m) n")[
                            512 * q:512 * q + 512, bass.ds(col0, 256)]
                        sp.wait_ge(ada_raw_free[q].sem, ada_raw_free[q].at(l, pair + (1 - q)))
                        ada_loaded[q].inc(sp.dma_start(ada_raw[q][:], src.rearrange("(k p) n -> p k n", p=P)), times)

                sp.wait_ge(ada_raw_free[0].sem, ada_raw_free[0].at(l, 0))
                src = layer_of("w_in").rearrange("a (k p) n -> p (a k) n", p=P)
                small_raw = ada_raw[0][:].rearrange("p a b -> p (a b)")[:, 0:KD * 48].rearrange("p (k n) -> p k n", n=48)
                small_loaded.inc(sp.dma_start(small_raw[:, :, 0:16], src[:, :, COL_GLOW:COL_GLOW + 16]))
                small_loaded.inc(sp.dma_start(small_raw[:, :, 32:36], src[:, :, COL_DT:COL_DT + 4]))
                load_tile(0, 0, "w_in", 0, KD, 0)
                for name, (first, count) in ROWS.items():
                    v = layer_of(name)
                    v = v.rearrange("a c (k p) -> (a c k) p", p=P) if len(v.shape) == 3 else \
                        v.rearrange("a (k p) -> (a k) p", p=P)
                    rows_loaded.inc(sp.dma_start(par_rows[first:first + count, :], v))
                load_tile(1, 0, "w_in", 0, KD, P)
                for i, name in enumerate(("ssd_a_log", "ssd_dt_bias", "ssd_d")):
                    heads_loaded.inc(sp.dma_start(head_par[:, 4 * i:4 * i + 4],
                                                  layer_of(name).rearrange("a h -> (a h)").partition_broadcast(P)))
                sp.wait_ge(zeroed.sem, 1)
                for m, name in enumerate(("lru_wa", "lru_wx")):
                    for k in range(4):
                        r = slice(64 * (k % 2), 64 * (k % 2) + 64)
                        lru_w_loaded.inc(sp.dma_start(lru_w[r, m, k // 2, r],
                                                      layer_of(name).rearrange("a k i j -> (a k) i j")[k]))
                lru_w_loaded.inc(sp.dma_start(gate_w[:], layer_of("gla_wg2").rearrange("a r n -> (a r) n")))
                sp.wait_ge(ax_ready.sem, ax_ready.at(l, 0))
                residual_saved.inc(sp.dma_start(residual.rearrange("k p t -> p k t"), ax[:]))
                sp.wait_ge(tile_done.sem, tile_done.at(l, 0))
                rotary_loaded.inc(sp.dma_start(cos_sin[:], rotary.rearrange("a p t -> p a t")))

                def ada_source(pair):
                    return (None, 2048 + 256 * pair) if pair < 16 else ((l + 1) % DEPTH, 256 * (pair - 16))

                t = 0
                for first, count in IN_SEGMENTS:
                    skip = 2 if t == 0 else 0
                    if t == 0:
                        for s in range(2):
                            load_ada_pair(s, *ada_source(s))
                    with sp.Fori(skip // 2, count // 2) as i:
                        for s in range(2):
                            load_tile(s, i + t // 2, "w_in", 0, KD, i * (2 * P) + (first + s * P),
                                      (count - skip) // 2)
                            if t < ADA_PAIRS:
                                layer, col0 = ada_source(t + s)
                                load_ada_pair(i * 2 + (t + s), layer, i * 512 + col0, (count - skip) // 2)
                    t += count
                with sp.Fori(0, KD // 2) as i:
                    for s in range(2):
                        load_tile(s, i + t // 2, "w_out", 0, KD, i * (2 * P) + s * P, KD // 2)
                t += KD

                def load_part(t2, f0, size, times):
                    with sp.Fori(0, size) as i:
                        load_tile(0, i + t2, "ffn_w_up", 0, KD, (i + f0) * P, times * size)
                        load_tile(1, i + t2, "ffn_w_up", 0, KD, (i + (f0 + NF)) * P, times * size)
                    with sp.Fori(0, KD // 2) as i:
                        for s in range(2):
                            load_tile(s, i + (t2 + size), "ffn_w_down", f0 * P, size, i * (2 * P) + s * P,
                                      times * KD // 2)

                with sp.Fori(0, FULL_PARTS) as part:
                    load_part(part * (PART + KD // 2) + t // 2, part * PART, PART, FULL_PARTS)
                load_part(FULL_PARTS * (PART + KD // 2) + t // 2, FULL_PARTS * PART, LAST_PART, 1)

            for c in range(NCH):
                sp.wait_ge(out_copied.sem, 2 * c + 2)
                out_saved.inc(sp.dma_start(out[0, chunk(c), :], x_rows[:, c, :]))
            sp.wait_ge(out_saved.sem, 16 * NCH)

        @block.gpsimd
        def _(pool):
            zeroed.inc(pool.memset(lru_w[:], 0.0))
            for s in range(2):
                pool.sem_inc(raw_free[s].sem, 1)
                pool.sem_inc(ada_raw_free[s].sem, 1)
            pool.wait_ge(c_ready.sem, 1)
            with pool.Fori(0, DEPTH) as l:
                def split(slot, tile, rows, times=1):
                    pool.wait_ge(w_hi_made.sem, w_hi_made.at(l, tile + 1))
                    raw_free[slot].inc(pool.tensor_tensor(
                        w_lo[slot][:, 0:rows, :], w_raw[slot][:, 0:rows, :],
                        w_hi[slot][:, 0:rows, :].bitcast(F32), ALU.subtract), times)
                    split_done.inc(pool.drain(), times)

                def sum_ada(pair, times):
                    raw = ada_raw[0]
                    pool.wait_ge(ada_loaded[0].sem, ada_loaded[0].at(l, pair + 1))
                    pool.tensor_tensor(raw[:], raw[:], c_col[:, 0, 0:4].unsqueeze(2).to_broadcast([P, 4, 256]), ALU.mult)
                    pool.drain()
                    pool.tensor_tensor(raw[:, 0:2, :], raw[:, 0:2, :], raw[:, 2:4, :], ALU.add)
                    pool.drain()
                    pool.wait_ge(ada_sum_used.sem, ada_sum_used.at(l, pair))
                    ada_raw_free[0].inc(pool.tensor_tensor(ada_sum[0][:], raw[:, 0, :], raw[:, 1, :], ALU.add), times)
                    ada_summed[0].inc(pool.drain(), times)

                pool.wait_ge(small_loaded.sem, small_loaded.at(l, 2))
                pool.wait_ge(tile_done.sem, tile_done.at(l, 0))
                pool.wait_ge(rotary_saved.sem, 16)
                small_raw = ada_raw[0][:].rearrange("p a b -> p (a b)")[:, 0:KD * 48].rearrange("p (k n) -> p k n", n=48)
                parts = [t[:, 0:KD * 48].rearrange("p (k n) -> p k n", n=48) for t in (small_hi, small_lo)]
                pool.sem_inc(pool_passed.sem, 1)
                pool.memset(small_hi[:].bitcast(F32), 0.0)
                pool.memset(small_lo[:].bitcast(F32), 0.0)
                pool.drain()
                for r in (slice(0, 16), slice(32, 36)):
                    pool.tensor_copy(parts[0][:, :, r], small_raw[:, :, r])
                pool.drain()
                for r in (slice(0, 16), slice(32, 36)):
                    last = pool.tensor_tensor(parts[1][:, :, r], small_raw[:, :, r],
                                              parts[0][:, :, r].bitcast(F32), ALU.subtract)
                ada_raw_free[0].inc(last)
                small_split.inc(pool.drain())

                with pool.Fori(0, ADA_PAIRS // 2) as i:
                    for s in range(2):
                        split(s, i * 2 + s, KD, ADA_PAIRS // 2)
                        sum_ada(i * 2 + s, ADA_PAIRS // 2)
                with pool.Fori(ADA_PAIRS // 2, (N_IN + KD) // 2) as i:
                    for s in range(2):
                        split(s, i * 2 + s, KD, (N_IN + KD - ADA_PAIRS) // 2)

                def split_part(t2, size, times):
                    with pool.Fori(0, size) as i:
                        for s in range(2):
                            split(s, (i + t2) * 2 + s, KD, times * size)
                    with pool.Fori(0, KD // 2) as i:
                        for s in range(2):
                            split(s, (i + (t2 + size)) * 2 + s, size, times * KD // 2)

                with pool.Fori(0, FULL_PARTS) as part:
                    split_part(part * (PART + KD // 2) + (N_IN + KD) // 2, PART, FULL_PARTS)
                split_part(FULL_PARTS * (PART + KD // 2) + (N_IN + KD) // 2, LAST_PART, 1)

        @block.tensor
        def _(pe):
            pe.sem_inc(tile_done.sem, 2)
            pe.sem_inc(ada_sum_used.sem, 1)

            def transpose(out_, in_):
                return pe.transpose(out_, in_, ident[0:in_.shape[0], 0:in_.shape[0]])

            pe.wait_ge(const_loaded.sem, 64)
            n = 0
            unit_done.counted = 0
            last = transpose(ring[0][:, 0:KD], c_rows[:])
            unit_done.inc(last, 0)
            for l in range(DEPTH):
                unit_done.inc(transpose(ring[1 + l][:, 0:48], b_ada_rows[:, l, :]), 0)
            for n in range(3, 19):
                h, k = divmod(n - 3, KD)
                if n >= 4:
                    pe.wait_ge(bank_free[n % 4].sem, n // 4)
                if k == 0:
                    for i in (2 * h, 2 * h + 1):
                        pe.wait_ge(x_loaded[i].sem, 16)
                for i in range(4):
                    last = transpose(ring[n % 4][:, chunk(i)], x_rows[:, 4 * h + i, chunk(k)])
                unit_done.inc(last, 0)
            pe.wait_ge(bank_free[3].sem, 19 // 4)
            pe.wait_ge(c_ready.sem, 1)
            for n in range(2 * KD):
                if n % 4 == 0:
                    pe.wait_ge(ada_first_loaded[n // 4].sem, 16)
                for k in range(KD):
                    last = pe.matmul(ring[3][:, n:n + 1], ada_first[:, k, chunk(n)], c_col[:, 0, k:k + 1],
                                     start=(k == 0), stop=(k == KD - 1))
            unit_done.inc(last, 0)

            with pe.Fori(0, DEPTH) as l:
                def enter(unit4, bank):
                    pe.wait_ge(bank_free[bank].sem, bank_free[bank].at(l, unit4))
                    return ring[bank]

                def bank_of(step, i=0):
                    u = UNIT[step] + i
                    return enter(u // 4, u % 4)

                def large(ps, slot, rows, hi, lo):
                    for k in range(rows):
                        pe.matmul(ps[:], w_hi[slot][:, k, :], hi(k), start=(k == 0), stop=False)
                        pe.matmul(ps[:], w_hi[slot][:, k, :], lo(k), start=False, stop=False)
                        last = pe.matmul(ps[:], w_lo[slot][:, k, :], hi(k), start=False, stop=(k == rows - 1))
                    return last

                def operand(h):
                    return (lambda k: op_hi[:, k, half_of(h)]), (lambda k: op_lo[:, k, half_of(h)])

                for step in ORDER:
                    kind, n = step[0], (step[1] if len(step) > 1 else 0)
                    if kind == "params":
                        pe.wait_ge(rows_loaded.sem, rows_loaded.at(l, 15))
                        ps = bank_of(step)
                        unit_done.inc(transpose(ps[:, 0:N_ROWS], par_rows[:]))
                    elif kind == "small":
                        if n == 0:
                            pe.wait_ge(small_split.sem, small_split.at(l, 1))
                        ps = bank_of(step)
                        hi, lo = operand(n)
                        for k in range(KD):
                            pe.wait_ge(h_lo.sem, h_lo.at(l, 8 * n + k + 1))
                            w_h, w_l = (t[:, k * 48:k * 48 + P] for t in (small_hi, small_lo))
                            pe.matmul(ps[:], w_h, hi(k), start=(k == 0), stop=False)
                            pe.matmul(ps[:], w_h, lo(k), start=False, stop=False)
                            last = pe.matmul(ps[:], w_l, hi(k), start=False, stop=(k == KD - 1))
                        unit_done.inc(last)
                    elif kind == "proj":
                        h = step[2]
                        if h == 0:
                            pe.wait_ge(split_done.sem, split_done.at(l, n + 1))
                        ps = bank_of(step)
                        last = large(ps, n % 2, KD, *operand(h))
                        (tile_done if h else half_done).inc(last)
                    elif kind == "ada":
                        for q in range(2):
                            pe.wait_ge(ada_summed[q].sem, ada_summed[q].at(l, n + 1))
                        ps = bank_of(step)
                        for i in range(2):
                            for q in range(2):
                                last = pe.matmul(ps[:, i:i + 1], ada_sum[q][:, chunk(i)], one,
                                                 start=(q == 0), stop=(q == 1))
                        ada_sum_used.inc(last)
                    elif kind == "dt":
                        pe.wait_ge(small_copied.sem, small_copied.at(l, 2))
                        ps = bank_of(step)
                        for c in range(NCH):
                            last = pe.matmul(ps[:, 4 * c:4 * c + 4], small[32:36, chunk(c)], ident[32:36, 32:36],
                                             start=True, stop=True)
                        unit_done.inc(last)
                    elif kind == "dt_cum":
                        pe.wait_ge(dt_ready.sem, dt_ready.at(l, 1))
                        ps = bank_of(step)
                        unit_done.inc(pe.matmul(ps[:, 0:32], cst("causal"), columns[:, 1, :], start=True, stop=True))
                    elif kind == "rotate":
                        h = step[2]
                        pe.wait_ge(raw_copied.sem, raw_copied.at(l, copied_count(8 + n) - 1 + h))
                        ps = bank_of(step)
                        unit_done.inc(pe.matmul(ps[:], cst("perm"), gb[:, n, half_of(h)], start=True, stop=True))
                    elif kind == "ssd_pre":
                        if n == 0:
                            pe.wait_ge(ssd_state.sem, ssd_state.at(l, 1))
                        else:
                            pe.wait_ge(ssd_banks_read.sem, ssd_banks_read.at(l, n))
                        b_cum, b_g, b_t, _ = core
                        for j in range(2):
                            transpose(b_t[:, chunk(j)], ga[:, j, chunk(n)])
                            transpose(b_t[:, chunk(2 + j)], ga[:, 2 + j, chunk(n)])
                        for g in range(2):
                            pe.matmul(b_g[:, chunk(g)], ga[:, 2 + g, chunk(n)], ga[:, 4 + g, chunk(n)],
                                      start=True, stop=True)
                        for hd in range(4):
                            i = 4 * n + hd
                            last = pe.matmul(b_cum[:, chunk(hd)], columns[:, 1, i:i + 1].to_broadcast([P, P]),
                                             cst("causal"), start=True, stop=True)
                        ssd_pre_done.inc(last)
                    elif kind == "ssd_b":
                        ed, ec, v, v2, bt, hs = tmp2k[0], tmp2k[1], tmp1k[5], tmp1k[6], tmp1k[7], tmp1k[8]
                        pe.wait_ge(ssd_operands.sem, ssd_operands.at(l, n + 1))
                        pe.wait_ge(ssd_state.sem, ssd_state.at(l, n + 1))
                        for hd in range(4):
                            j, i = divmod(hd, 2)
                            o = core[3][64 * i:64 * i + 64, chunk(j)]
                            pe.matmul(o, v[:, chunk(hd, 64)], ed[:, chunk(hd)], start=True, stop=False)
                            pe.matmul(o, hs[:, chunk(hd, 64)], ec[:, chunk(hd)], start=False, stop=True)
                        for g in range(2):
                            last = pe.matmul(core[3][:, chunk(2 + g)], bt[:, chunk(g)],
                                             v2[:, chunk(g)], start=True, stop=True)
                        ssd_b_done.inc(last)
                    elif kind in ("ssd_stats", "ret_stats", "gla_stats"):
                        g = ("ssd_stats", "ret_stats", "gla_stats").index(kind)
                        pe.wait_ge(norm_sq.sem, norm_sq.at(l, g + 1))
                        ps = bank_of(step)
                        if g == 0:
                            for c in range(NCH):
                                for j in range(2):
                                    last = pe.matmul(ps[:, c:c + 1], ga[:, 2 + j, chunk(c)], one,
                                                     start=(j == 0), stop=(j == 1))
                        else:
                            raw, sq = (gb[:, 4:6, :], gb[:, 0:2, :]) if g == 1 else (None, ga[:, 0:2, :])
                            for c in range(NCH):
                                for j in range(2):
                                    i = 4 * c + 2 * j
                                    last = pe.matmul(ps[:, i:i + 2], sq[:, j, chunk(c)], cst("head2"),
                                                     start=True, stop=True)
                                    if g == 1:
                                        last = pe.matmul(ps[:, 32 + i:32 + i + 2], raw[:, j, chunk(c)], cst("head2"),
                                                         start=True, stop=True)
                        unit_done.inc(last)
                    elif kind == "ssd_norm":
                        pe.wait_ge(norm_rstd.sem, norm_rstd.at(l, 1))
                        for h in range(2):
                            ps = bank_of(step, h)
                            for c in range(4):
                                last = transpose(ps[:, chunk(c)],
                                                 stat[:, 0, 4 * h + c:4 * h + c + 1].to_broadcast([P, P]))
                            unit_done.inc(last)
                    elif kind in ("ret_norm", "gla_norm"):
                        g = 1 if kind == "ret_norm" else 2
                        pe.wait_ge(norm_wide.sem, norm_wide.at(l, g))
                        u = 0
                        for h in ((0, 1) if g == 1 else (n,)):
                            for j in range(2):
                                for s in ((1, 0) if g == 1 else (0,)):
                                    ps = bank_of(step, u)
                                    for c in range(4):
                                        i = 4 * (4 * h + c) + 2 * j
                                        wide = wide_stat(g, s).rearrange("p j t -> p (j t)")
                                        last = transpose(ps[:, chunk(c)], wide[:, 64 * i:64 * i + P])
                                    unit_done.inc(last)
                                    u += 1
                    elif kind == "ret_pre":
                        if n:
                            pe.wait_ge(ret_operands.sem, ret_operands.at(l, n))
                        else:
                            pe.wait_ge(ret_state.sem, ret_state.at(l, 1))
                            pe.wait_ge(raw_copied.sem, raw_copied.at(l, copied_count(13)))
                        for j in range(2):
                            transpose(core[2][:, chunk(j)], gb[:, 2 + j, chunk(n)])
                            transpose(core[2][:, chunk(2 + j)], gb[:, 4 + j, chunk(n)])
                        for j in range(2):
                            for i in range(2):
                                r = slice(64 * i, 64 * i + 64)
                                last = pe.matmul(core[i][:, chunk(j)], gb[r, 2 + j, chunk(n)], gb[r, j, chunk(n)],
                                                 start=True, stop=True)
                        ret_pre_done.inc(last)
                    elif kind == "ret_b":
                        m, kt, v, qg, hs = tmp2k[0], tmp1k[2], tmp1k[3], tmp1k[4], tmp1k[6]
                        pe.wait_ge(ret_operands.sem, ret_operands.at(l, n + 1))
                        pe.wait_ge(ret_state.sem, ret_state.at(l, n + 1))
                        for j in range(2):
                            o = core[3][:, chunk(j)]
                            pe.matmul(o, hs[:, chunk(j)], qg[:, chunk(j)], start=True, stop=False,
                                      skip_group_check=True)
                            for i in range(2):
                                hd = 2 * j + i
                                pe.matmul(o[64 * i:64 * i + 64], v[:, chunk(hd, 64)],
                                          m[:, chunk(hd)], start=False, stop=True,
                                          skip_group_check=True)
                        for j in range(2):
                            last = pe.matmul(core[3][:, chunk(2 + j)], kt[:, chunk(j)], v[:, chunk(j)],
                                             start=True, stop=True)
                        ret_b_done.inc(last)
                    elif kind == "gla_gate":
                        pe.wait_ge(lru_w_loaded.sem, lru_w_loaded.at(l, 9))
                        for h in range(2):
                            ps = bank_of(step, h)
                            unit_done.inc(pe.matmul(ps[:], gate_w[:], small[0:16, half_of(h)], start=True, stop=True))
                    elif kind == "gla_pre":
                        qz = tmp2k[0]
                        if n:
                            pe.wait_ge(gla_masked.sem, gla_masked.at(l, n))
                            pe.wait_ge(gla_kv.sem, gla_kv.at(l, n))
                        else:
                            pe.wait_ge(gla_zeroed.sem, gla_zeroed.at(l, 1))
                        transpose(core[2][:, 0:P], ga[:, 4, chunk(n)])
                        for j in range(2):
                            transpose(core[2][:, chunk(1 + j)], ga[:, 2 + j, chunk(n)])
                        for i in range(2):
                            last = pe.matmul(core[0][64 * i:64 * i + 64, 0:256],
                                             ga[:, 1, P * n + 64 * i:P * n + 64 * i + 64],
                                             qz[:].rearrange("p (h t) -> p h t", h=4)[:, :, chunk(i, 64)],
                                             start=True, stop=True)
                        gla_pre_done.inc(last)
                    elif kind == "gla_b":
                        pe.wait_ge(gla_kv.sem, gla_kv.at(l, n + 1))
                        if n:
                            pe.wait_ge(gla_state.sem, gla_state.at(l, n))
                        for i in range(2):
                            last = pe.matmul(core[1][:, chunk(i, 256)], gla_k[:, chunk(i)], gla_v[n % 2][:],
                                             start=True, stop=True)
                        gla_b_done.inc(last)
                    elif kind == "gla_c":
                        pe.wait_ge(gla_masked.sem, gla_masked.at(l, n + 1))
                        pe.wait_ge(gla_state.sem, gla_state.at(l, n + 1))
                        if n:
                            pe.wait_ge(gla_out.sem, gla_out.at(l, n))
                        for j in range(2):
                            o = core[3][:, chunk(j)]
                            for i in range(2):
                                pe.matmul(o[:, chunk(i, 64)], gla_h[(2 * n + i) % 3][:, chunk(j)],
                                          ga[:, 0, P * n + 64 * i:P * n + 64 * i + 64],
                                          start=(i == 0), stop=False, skip_group_check=True)
                            for i in range(2):
                                hd = 2 * j + i
                                last = pe.matmul(o[64 * i:64 * i + 64], gla_v[n % 2][:, chunk(hd, 64)],
                                                 gla_m[n % 2][:, chunk(hd)], start=False, stop=True,
                                                 skip_group_check=True)
                        gla_c_done.inc(last)
                    elif kind == "lru":
                        pe.wait_ge(lru_xr.sem, lru_xr.at(l, n + 1))
                        u = 0
                        for h in range(2):
                            for m in range(2):
                                ps = bank_of(step, u)
                                unit_done.inc(pe.matmul(ps[:], lru_w[:, m, n, :], gb[:, 2 + n, half_of(h)],
                                                        start=True, stop=True))
                                u += 1

                with pe.Fori(0, KD // 2) as i:
                    for s in range(2):
                        pe.wait_ge(split_done.sem, split_done.at(l, i * 2 + (N_IN + s + 1)))
                        for h in range(2):
                            u = UNIT_OUT + 2 * s + h
                            ps = enter(i + u // 4, u % 4)
                            hi, lo = operand(h)
                            for k in range(KD):
                                pe.wait_ge(y_lo.sem, y_lo.at(l, 8 * h + k + 1))
                                pe.matmul(ps[:], w_hi[s][:, k, :], hi(k), start=(k == 0), stop=False)
                                pe.matmul(ps[:], w_hi[s][:, k, :], lo(k), start=False, stop=False)
                                last = pe.matmul(ps[:], w_lo[s][:, k, :], hi(k), start=False, stop=(k == KD - 1))
                            (tile_done if h else half_done).inc(last, KD // 2)

                def layer_norm(which, unit):
                    for h in range(2):
                        pe.wait_ge(sums_made.sem, sums_made.at(l, 16 * which + 15 + h))
                        for q in range(2):
                            ps = enter((unit + q) // 4, (unit + q) % 4)
                            for c in range(4):
                                last = pe.matmul(ps[:, c:c + 1], tmp[:, 2 * q + h, chunk(c)], one, start=True, stop=True)
                            unit_done.inc(last)
                        pe.wait_ge(ln_rstd.sem, ln_rstd.at(l, 2 * which + h + 1))
                        for q in range(2):
                            ps = enter((unit + 2 + q) // 4, (unit + 2 + q) % 4)
                            for c in range(4):
                                last = transpose(ps[:, chunk(c)], stat[:, q, c:c + 1].to_broadcast([P, P]))
                            unit_done.inc(last)
                        unit += 4

                layer_norm(0, UNIT_LN1)

                def ffn_part(unit4, t2, size, times):
                    with pe.Fori(0, size) as i:
                        for h in range(2):
                            hi, lo = operand(h)
                            for s in range(2):
                                if h == 0:
                                    pe.wait_ge(split_done.sem, split_done.at(l, (i + t2) * 2 + (s + 1)))
                                if h == 0 and s == 0:
                                    pe.wait_ge(h_lo.sem, h_lo.at(l, 24))
                                if h == 1 and s == 0:
                                    pe.wait_ge(h_lo.sem, h_lo.at(l, 32))
                                ps = enter(i + unit4, 2 * h + s)
                                (tile_done if h else half_done).inc(large(ps, s, KD, hi, lo), times * size)

                def ffn_down(unit4, t2, size, lo_count, times):
                    with pe.Fori(0, KD // 2) as i:
                        pe.wait_ge(up_lo.sem, lo_count)
                        for s in range(2):
                            pe.wait_ge(split_done.sem, split_done.at(l, (i + t2) * 2 + (s + 1)))
                            for h in range(2):
                                ps = enter(i + unit4, 2 * s + h)
                                last = large(ps, s, size, lambda k: act_hi[:, k, half_of(h)],
                                             lambda k: act_lo[:, k, half_of(h)])
                                (tile_done if h else half_done).inc(last, times * KD // 2)

                u4, t2 = UNIT_FFN // 4, (N_IN + KD) // 2
                with pe.Fori(0, FULL_PARTS) as part:
                    ffn_part(part * (PART + 4) + u4, part * (PART + 4) + t2, PART, FULL_PARTS)
                    ffn_down(part * (PART + 4) + (u4 + PART), part * (PART + 4) + (t2 + PART), PART,
                             up_lo.at(l, (part + 1) * (2 * PART)), FULL_PARTS)
                done = FULL_PARTS * (PART + 4)
                ffn_part(u4 + done, t2 + done, LAST_PART, 1)
                ffn_down(u4 + done + LAST_PART, t2 + done + LAST_PART, LAST_PART, up_lo.at(l, 2 * NF), 1)
                layer_norm(1, UNIT_LN2)

            pe.wait_ge(ax_ready.sem, ax_ready.at(DEPTH, 0))
            for n in range(2 * NCH):
                c, g = divmod(n, 2)
                pe.wait_ge(bank_free[n % 4].sem, bank_free[n % 4].at(DEPTH, n // 4))
                for i in range(4):
                    last = transpose(ring[n % 4][:, chunk(i)], ax[:, 4 * g + i, chunk(c)])
                unit_done.inc(last, 0)

        @block.scalar
        def _(act):
            def f(out_, in_, func, **k):
                return act.activation(out_, in_, func, **k)

            act.wait_ge(c_copied.sem, 1)
            c_tanh.inc(f(c_col[:, 1, :], c_col[:, 0, :], ACT.Tanh, scale=0.5), 1)
            for n in range(3, 19):
                h, k = divmod(n - 3, KD)
                act.wait_ge(unit_done.sem, n + 1)
                bank_free[n % 4].inc(f(ax[:, k, half_of(h)], ring[n % 4][:], ACT.Copy, scale=ALPHA), 0)
            act.sem_inc(ax_ready.sem, 15)
            act.drain().then_inc(ax_ready.sem, 1)
            act.wait_ge(angle_ready.sem, 1)
            f(angle[:, 2, :], angle[:, 0, :], ACT.Sin, scale=0.5)
            angle_sin.inc(f(angle[:, 3, :], angle[:, 0, :], ACT.Sin), 0)

            with act.Fori(0, DEPTH) as l:
                def wait(signal, n):
                    act.wait_ge(signal.sem, signal.at(l, n))

                def products(step, i=0):
                    u = UNIT[step] + i
                    if step[0] == "proj":
                        wait(tile_done if step[2] else half_done, step[1] + 1)
                    else:
                        wait(unit_done, MISC[step] + i + 1)
                    return ring[u % 4]

                def free(step, instruction, i=0):
                    bank_free[(UNIT[step] + i) % 4].inc(instruction)

                def split_h(first, scale, shift):
                    for h in range(2):
                        for k in range(KD):
                            n = 8 * h + k
                            if n >= 2:
                                wait(h_lo, first + n - 1)
                            args = dict(scale=scale[:, k:k + 1], bias=shift[:, k:k + 1])
                            f(tmp[:, 6 + n % 2, :], ax[:, k, half_of(h)], ACT.Identity, **args)
                            f(op_hi[:, k, half_of(h)], ax[:, k, half_of(h)], ACT.Identity, **args)
                            h_value.inc(act.drain())

                def weight_hi(tile, slot, n, times=1):
                    act.wait_ge(raw_loaded[slot].sem, raw_loaded[slot].at(l, n + 1))
                    act.wait_ge(tile_done.sem, tile_done.at(l, tile - 1))
                    w_hi_made.inc(f(w_hi[slot][:], w_raw[slot][:], ACT.Copy), times)

                for s in range(2):
                    weight_hi(s, s, 0)
                act.wait_ge(mod_first.sem, 1)
                wait(ax_ready, 0)
                split_h(0, mod_next[:, 8:16], mod_next[:, 0:8])

                copied = 0
                for step in ORDER:
                    kind, n = step[0], (step[1] if len(step) > 1 else 0)
                    if kind == "params":
                        ps = products(step)
                        free(step, f(par[:], ps[:, 0:N_ROWS], ACT.Copy))
                        wait(heads_loaded, 3)
                        f(head_par[:, 0:4], head_par[:, 0:4], ACT.Exp)
                        lam = col("lru_lambda")
                        act.drain()
                        first = ROWS["lru_lambda"][0]
                        lam = par[:, first:first + 2]
                        f(lru_col[:, 0, :], lam, ACT.Abs)
                        act.drain()
                        f(lru_col[:, 0, :], lru_col[:, 0, :], ACT.Exp, scale=-1.0)
                        par_copied.inc(act.drain())
                    elif kind == "small":
                        ps = products(step)
                        free(step, f(small[:, half_of(n)], ps[0:48, :], ACT.Copy))
                        small_copied.inc(act.drain())
                    elif kind == "dt":
                        wait(dt_x, 1)
                        f(columns[:, 1, :], columns[:, 0, :], ACT.Abs)
                        act.drain()
                        dt_exp.inc(f(columns[:, 1, :], columns[:, 1, :], ACT.Exp, scale=-1.0))
                    elif kind == "proj":
                        h = step[2]
                        if n == 2 and h == 0:
                            act.wait_ge(residual_saved.sem, residual_saved.at(l, 1))
                        if n == 16 and h == 0:
                            wait(y_final, 1)
                        if n == 22 and h == 0:
                            wait(y_final, 2)
                        ps = products(step)
                        if n in silu_tiles:
                            gate_tanh.inc(f(y[:, gate_slot[n], half_of(h)], ps[:], ACT.Tanh, scale=0.5))
                        elif n in gate_slot:
                            i = 2 * (n - 24) + h
                            if i:
                                wait(gelu_in, i)
                            gelu_sq.inc(f(tmp2k[4][:], ps[:], ACT.Square))
                            wait(gelu_in, i + 1)
                            gelu_tanh.inc(f(y[:, gate_slot[n], half_of(h)], y[:, gate_slot[n], half_of(h)],
                                            ACT.Tanh, scale=math.sqrt(2 / math.pi)))
                        else:
                            free(step, f(copied_to(n)[:, half_of(h)], ps[:], ACT.Copy))
                            raw_copied.inc(act.drain())
                        if h == 1:
                            weight_hi(n + 2, n % 2, n // 2 + 1)
                    elif kind == "conv":
                        wait(conv_done, n + 1)
                        conv_tanh.inc(f(conv_b[:], conv_a[:], ACT.Tanh))
                    elif kind == "ssd_mid":
                        ed, ec, bt = tmp2k[0], tmp2k[1], tmp1k[7]
                        if n == 0:
                            wait(ssd_state, 1)
                        else:
                            wait(ssd_b_done, n)
                        wait(ssd_pre_done, n + 1)
                        f(bt[:], core[2][:, 256:512], ACT.Copy)
                        ssd_copied.inc(f(ec[:], core[0][:], ACT.Exp))
                        wait(ssd_exponents, n + 1)
                        f(ed[:], ed[:], ACT.Exp)
                        f(te[:], te[:], ACT.Exp)
                        ssd_exp.inc(act.drain())
                    elif kind in ("ssd_gate", "ret_square", "gla_square"):
                        g = ("ssd_gate", "ret_square", "gla_square").index(kind)
                        if g == 0:
                            wait(norm_in, 1)
                        elif g == 1:
                            wait(ret_state, NCH + 1)
                        else:
                            act.drain()
                        raw, sq = ((y[:, 0:2, :], ga[:, 2:4, :]), (gb[:, 4:6, :], gb[:, 0:2, :]),
                                   (ga[:, 2:4, :], ga[:, 0:2, :]))[g]
                        for j in range(2):
                            last = f(sq[:, j, :], raw[:, j, :], ACT.Square)
                        norm_sq.inc(last)
                    elif kind in ("ssd_stats", "ret_stats", "gla_stats"):
                        g = ("ssd_stats", "ret_stats", "gla_stats").index(kind)
                        wait(norm_var, g + 1)
                        norm_dev.inc(f(stat[:, 0, :], stat[:, 0, :], ACT.Sqrt, bias=eps))
                        if g:
                            wait(norm_rstd, g + 1)
                            for i in ((0, 1) if g == 1 else (0,)):
                                last = f(wide_stat(g, i).rearrange("p j (c f) -> p (j c) f", f=64),
                                         stat[:, i, :].unsqueeze(2).to_broadcast([P, 32, 64]), ACT.Copy)
                            norm_wide.inc(last)
                    elif kind == "ret_mid":
                        if n:
                            wait(ret_b_done, n)
                        wait(ret_pre_done, n + 1)
                        ret_v.inc(f(tmp1k[3][:], core[2][:, 256:512], ACT.Copy))
                    elif kind == "gla_gate":
                        wait(gla_gate_x, 1)
                        f(ga[:, 5, :], ga[:, 4, :], ACT.Abs)
                        act.drain()
                        f(ga[:, 5, :], ga[:, 5, :], ACT.Exp, scale=-1.0)
                        act.drain()
                        gla_gate_act.inc(f(ga[:, 5, :], ga[:, 5, :], ACT.Ln, bias=one))
                        wait(gla_cum, 1)
                        f(ga[:, 5, :], ga[:, 4, :], ACT.Exp, scale=1 / 16)
                        act.drain()
                        gla_gate_act.inc(f(ga[:, 4, :], ga[:, 4, :], ACT.Exp, scale=-1 / 16))
                    elif kind == "gla_mid":
                        if n >= 2:
                            wait(gla_c_done, n - 1)
                        wait(gla_pre_done, n + 1)
                        for i in range(2):
                            r = slice(64 * i, 64 * i + 64)
                            f(gla_k[r, chunk(i)], core[2][r, 0:P], ACT.Copy)
                        gla_kv.inc(f(gla_v[n % 2][:], core[2][:, P:3 * P], ACT.Copy))
                    elif kind == "gla_c":
                        wait(gla_c_done, n + 1)
                        gla_out.inc(f(ga[:, 2:4, chunk(n)], core[3][:, 0:256].rearrange("p (j t) -> p j t", j=2),
                                      ACT.Copy))
                    elif kind == "lru":
                        e, g = gb[:, 4, :], gb[:, n, :]
                        fi = gb[:, 5, :]
                        ba, bx = col("lru_ba", n), lru_col[:, 3, n:n + 1]
                        if n:
                            wait(lru_dve, n)
                        for h in range(2):
                            ps = products(step, 2 * h)
                            free(step, f(e[:, half_of(h)], ps[:], ACT.Sigmoid, bias=ba), 2 * h)
                            ps = products(step, 2 * h + 1)
                            free(step, f(fi[:, half_of(h)], ps[:], ACT.Tanh, bias=bx, scale=0.5), 2 * h + 1)
                        act.drain()
                        lru_act.inc(f(g, e, ACT.Tanh, scale=lru_col[:, 1, n:n + 1]))
                        lru_act.inc(f(e, e, ACT.Exp, scale=lru_col[:, 2, n:n + 1]))
                    elif kind == "lru_gate":
                        wait(lru_in, n + 1)
                        lru_act.inc(f(gb[:, n, :], gb[:, n, :], ACT.Sqrt))
                    elif kind == "y_split":
                        h, k = divmod(n, KD)
                        if k == 0:
                            wait(tile_done if h else half_done, N_IN)
                        if n == 0:
                            wait(y_final, 2)
                        if k in (4, 5):
                            wait(lru_final, 2 * (k - 4) + h + 1)
                        if k in (6, 7):
                            wait(gla_final, 2 * h + k - 5)
                        if n == 8:
                            wait(gla_final, 4)
                            residual_loaded.inc(act.dma_start(ax[:], residual.rearrange("k p t -> p k t")))
                        y_hi.inc(f(op_hi[:, k, half_of(h)], y[:, k, half_of(h)], ACT.Copy))

                def layer_norm(which, weight, bias, tile0, slot0):
                    for i in range(16):
                        d, h = divmod(i, 2)
                        if h == 1 and (which == 0 or d < KD - 2):
                            tile = tile0 + d + 2
                            weight_hi(tile, d % 2, slot0 + d // 2 + 1)
                        wait(z_made, 16 * which + i + 1)
                        if i >= 2:
                            wait(sums_made, 16 * which + i - 1)
                        z_sq.inc(f(tmp[:, 4 + i % 2, :], ax[:, d, half_of(h)], ACT.Square))
                    for h in range(2):
                        wait(ln_var, 2 * which + h + 1)
                        ln_dev.inc(f(stat[:, 1, 0:4], stat[:, 1, 0:4], ACT.Sqrt, bias=eps))
                        for k in range(KD):
                            wait(ln_norm, 16 * which + 8 * h + k + 1)
                            last = f(ax[:, k, half_of(h)], ax[:, k, half_of(h)], ACT.Identity,
                                     scale=weight[:, k:k + 1], bias=bias[:, k:k + 1])
                            if which:
                                ax_ready.inc(last)

                def rows(name):
                    first, count = ROWS[name]
                    return par[:, first:first + count]

                layer_norm(0, rows("ln1_w"), rows("ln1_b"), N_IN, N_IN // 2)
                act.drain()
                split_h(16, mod[:, 16:24], mod[:, 8:16])

                def ffn_part(t2, f0, size, times):
                    with act.Fori(0, size) as i:
                        for h in range(2):
                            act.wait_ge((tile_done if h else half_done).sem,
                                        (tile_done if h else half_done).at(l, (i + t2) * 2 + 1))
                            act.wait_ge(up_lo.sem, up_lo.at(l, (i + f0) * 2 + (h - 1)))
                            up_tanh.inc(f(tmp[:, h, :], ring[2 * h][:], ACT.Tanh, scale=0.5), times * size)
                            if h == 1:
                                for s in range(2):
                                    weight_hi((i + t2) * 2 + (2 + s), s, i + t2 + 1, times * size)
                            act.wait_ge(up_act.sem, up_act.at(l, (i + f0) * 2 + (h + 1)))
                            up_hi.inc(f(act_hi[:, bass.ds(i, 1), half_of(h)].rearrange("p a t -> p (a t)"),
                                        tmp[:, 4 + h, :], ACT.Copy), times * size)

                t2 = (N_IN + KD) // 2
                with act.Fori(0, FULL_PARTS) as part:
                    ffn_part(part * (PART + 4) + t2, part * PART, PART, FULL_PARTS)
                    with act.Fori(0, KD // 2) as i:
                        for s in range(2):
                            n2 = i + part * (PART + 4) + (t2 + PART)
                            weight_hi(n2 * 2 + (2 + s), s, n2 + 1, FULL_PARTS * KD // 2)
                ffn_part(t2 + FULL_PARTS * (PART + 4), FULL_PARTS * PART, LAST_PART, 1)
                t2 += FULL_PARTS * (PART + 4) + LAST_PART
                layer_norm(1, rows("ln2_w"), rows("ln2_b"), 2 * t2, t2)

            for n in range(2 * NCH):
                c, g = divmod(n, 2)
                act.wait_ge(unit_done.sem, unit_done.at(DEPTH, n + 1))
                f(x_rows[:, c, half_of(g)], ring[n % 4][:], ACT.Copy, scale=1 / ALPHA)
                bank_free[n % 4].inc(act.drain(), 0)
                out_copied.inc(act.drain(), 0)

        @block.vector
        def _(dve):
            def tt(out_, a_, b_, op):
                return dve.tensor_tensor(out_, a_, b_, op)

            def ts(out_, a_, s0, s1, op0, op1=ALU.bypass):
                return dve.tensor_scalar(out_, a_, s0, s1, op0, op1) if s1 is not None else \
                    dve.tensor_scalar(out_, a_, s0, None, op0)

            def stt(out_, a_, s, b_, op0, op1):
                return dve.scalar_tensor_tensor(out=out_, in0=a_, scalar=s, in1=b_, op0=op0, op1=op1)

            def log1p(e, s, z, p):
                ts(s, e, 2.0, None, ALU.add)
                dve.drain()
                dve.reciprocal(s, s)
                dve.drain()
                tt(s, e, s, ALU.mult)
                dve.drain()
                tt(z, s, s, ALU.mult)
                dve.drain()
                ts(p, z, 1 / 15, None, ALU.mult)
                for n in (13, 11, 9, 7, 5, 3):
                    dve.drain()
                    stt(p, p, 1 / n, z, ALU.add, ALU.mult)
                dve.drain()
                stt(s, p, 1.0, s, ALU.add, ALU.mult)
                dve.drain()
                ts(s, s, 2.0, None, ALU.mult)
                dve.drain()

            dve.sem_inc(up_lo.sem, 2)
            dve.wait_ge(unit_done.sem, 1)
            bank_free[0].inc(dve.tensor_copy(c_col[:, 0, :], ring[0][:, 0:KD]), 0)
            c_copied.inc(dve.drain(), 1)
            for l in range(DEPTH):
                dve.wait_ge(unit_done.sem, 2 + l)
                bank_free[1 + l].inc(dve.tensor_copy(b_ada[:, l, :], ring[1 + l][:, 0:48]), 0)
            dve.wait_ge(c_tanh.sem, 1)
            stt(c_col[:, 0, :], c_col[:, 1, :], 1.0, c_col[:, 0, :], ALU.add, ALU.mult)
            dve.drain()
            c_ready.inc(ts(c_col[:, 0, :], c_col[:, 0, :], 0.5, None, ALU.mult), 0)
            dve.wait_ge(pos_loaded.sem, 16)
            dve.wait_ge(const_loaded.sem, 64)
            dve.tensor_copy(angle[:, 1, :], angle[:, 0, :].bitcast(I32))
            dve.drain()
            ts(angle[:, 0, :], angle[:, 1, :], cst("freq"), None, ALU.mult)
            dve.drain()
            ts(angle[:, 1, :], angle[:, 0, :], 1 / TWO_PI, 12582912.0, ALU.mult, ALU.add)
            dve.drain()
            ts(angle[:, 1, :], angle[:, 1, :], -12582912.0, None, ALU.add)
            rest = TWO_PI
            for bits in (5, 14, None):
                part = rest if bits is None else math.floor(rest * 2 ** bits) / 2 ** bits
                rest -= part
                dve.drain()
                stt(angle[:, 0, :], angle[:, 1, :], -part, angle[:, 0, :], ALU.mult, ALU.add)
            dve.drain()
            angle_ready.inc(ts(angle[:, 0, :], angle[:, 0, :], 3.1415925, -3.1415925, ALU.min, ALU.max), 0)
            dve.wait_ge(angle_sin.sem, 1)
            tt(angle[:, 2, :], angle[:, 2, :], angle[:, 2, :], ALU.mult)
            dve.drain()
            rotary_made.inc(ts(angle[:, 2, :], angle[:, 2, :], -2.0, 1.0, ALU.mult, ALU.add), 0)
            dve.wait_ge(unit_done.sem, UNITS_0)
            bank_free[3].inc(tt(mod_next[:], ring[3][:, 0:16], b_ada[:, 0, 0:16], ALU.add), 0)
            dve.drain()
            mod_first.inc(ts(mod_next[:, 8:16], mod_next[:, 8:16], 1.0, 1 / ALPHA, ALU.add, ALU.mult), 0)

            with dve.Fori(0, DEPTH) as l:
                def wait(signal, n):
                    dve.wait_ge(signal.sem, signal.at(l, n))

                def products(step, i=0):
                    u = UNIT[step] + i
                    if step[0] == "proj":
                        wait(tile_done if step[2] else half_done, step[1] + 1)
                    elif step[0] == "ada":
                        wait(ada_sum_used, step[1] + 1)
                    else:
                        wait(unit_done, MISC[step] + i + 1)
                    return ring[u % 4]

                def free(step, instruction, i=0):
                    bank_free[(UNIT[step] + i) % 4].inc(instruction)

                def split_h(first):
                    for h in range(2):
                        for k in range(KD):
                            n = 8 * h + k
                            wait(h_value, first + n + 1)
                            h_lo.inc(tt(op_lo[:, k, half_of(h)], tmp[:, 6 + n % 2, :],
                                        op_hi[:, k, half_of(h)].bitcast(F32), ALU.subtract))

                split_h(0)

                def convolve(out_, in_, weight, bias):
                    ts(out_, in_, weight(0), bias, ALU.mult, ALU.add)
                    for s in range(1, 4):
                        dve.drain()
                        last = stt(out_[:, s:T], in_[:, 0:T - s], weight(s), out_[:, s:T], ALU.mult, ALU.add)
                    return last

                gate_n = 0
                for step in ORDER:
                    kind, n = step[0], (step[1] if len(step) > 1 else 0)
                    if kind == "params":
                        wait(par_copied, 1)
                        dve.tensor_copy(b_mod[:, 0:32], b_ada[:, bass.ds(l, 1), 16:48].rearrange("p a n -> p (a n)"))
                        dve.tensor_copy(b_mod[:, 32:48], b_ada[:, bass.ds((l + 1) % DEPTH, 1), 0:16]
                                        .rearrange("p a n -> p (a n)"))
                        for i in range(2):
                            r = slice(64 * i, 64 * i + 64)
                            dve.tensor_copy(head_par[r, 12:14], head_par[r, 8 + i:12:2])
                        for r, factor in ((slice(0, 36), 0.5), (slice(ROWS["ln1_w"][0], N_ROWS), ALPHA)):
                            ts(par[:, r], par[:, r], factor, None, ALU.mult)
                        log1p(*(lru_col[:, i, :] for i in (0, 1, 2, 3)))
                        lam = par[:, ROWS["lru_lambda"][0]:ROWS["lru_lambda"][0] + 2]
                        ts(lru_col[:, 0, :], lam, -1.0, 0.0, ALU.mult, ALU.max)
                        dve.drain()
                        tt(lru_col[:, 1, :], lru_col[:, 0, :], lru_col[:, 1, :], ALU.add)
                        dve.drain()
                        ts(lru_col[:, 1, :], lru_col[:, 1, :], 8.0, None, ALU.mult)
                        dve.drain()
                        ts(lru_col[:, 2, :], lru_col[:, 1, :], -1.0, None, ALU.mult)
                        first = ROWS["lru_bx"][0]
                        ts(lru_col[:, 3, :], par[:, first:first + 2], 0.5, None, ALU.mult)
                        par_ready.inc(dve.drain())
                    elif kind == "dt":
                        ps = products(step)
                        heads = lambda i: columns[:, i, :].rearrange("p (c h) -> p c h", h=4)
                        across = lambda r: head_par[:, r].unsqueeze(1).to_broadcast([P, NCH, 4])
                        free(step, tt(heads(0), ps[:, 0:32].rearrange("p (c h) -> p c h", h=4),
                                      across(slice(4, 8)), ALU.add))
                        dt_x.inc(dve.drain())
                        wait(dt_exp, 1)
                        log1p(columns[:, 1, :], columns[:, 2, :], columns[:, 3, :], columns[:, 4, :])
                        stt(columns[:, 0, :], columns[:, 0, :], 0.0, columns[:, 2, :], ALU.max, ALU.add)
                        dve.drain()
                        dt_ready.inc(stt(heads(1), heads(0), -1.0, across(slice(0, 4)), ALU.mult, ALU.mult))
                    elif kind == "dt_cum":
                        ps = products(step)
                        free(step, dve.tensor_copy(columns[:, 2, :], ps[:, 0:32]))
                    elif kind == "ada_sum":
                        wait(ada_loaded[1], n + 1)
                        wait(ada_sum_used, n)
                        ts(ada_sum[1][:], ada_raw[1][:, 0, :], c_col[:, 0, 4:5], None, ALU.mult)
                        for k in range(1, 4):
                            dve.drain()
                            last = stt(ada_sum[1][:], ada_raw[1][:, k, :], c_col[:, 0, 4 + k:5 + k], ada_sum[1][:],
                                       ALU.mult, ALU.add)
                        ada_raw_free[1].inc(last)
                        ada_summed[1].inc(dve.drain())
                    elif kind == "ada":
                        ps = products(step)
                        to, first = (mod, 2 * n) if n < 16 else (mod_next, 2 * n - 32)
                        free(step, tt(to[:, first:first + 2], ps[:, 0:2], b_mod[:, 2 * n:2 * n + 2], ALU.add))
                        if n == ADA_PAIRS - 1:
                            dve.drain()
                            ts(mod[:, 16:24], mod[:, 16:24], 1.0, 1 / ALPHA, ALU.add, ALU.mult)
                            ts(mod_next[:, 8:16], mod_next[:, 8:16], 1.0, 1 / ALPHA, ALU.add, ALU.mult)
                            ts(mod[:, 24:32], mod[:, 24:32], 0.5, None, ALU.mult)
                            dve.drain()
                    elif kind == "proj":
                        h = step[2]
                        if n in silu_tiles:
                            gate_n += 1
                            wait(gate_tanh, gate_n)
                            o = y[:, gate_slot[n], half_of(h)]
                            free(step, stt(o, o, 1.0, ring[UNIT[step] % 4][:], ALU.add, ALU.mult))
                        elif n in gate_slot:
                            i = 2 * (n - 24) + h
                            ps, o, sq = ring[UNIT[step] % 4], y[:, gate_slot[n], half_of(h)], tmp2k[4]
                            wait(gelu_sq, i + 1)
                            ts(sq[:], sq[:], 0.044715, 1.0, ALU.mult, ALU.add)
                            dve.drain()
                            gelu_in.inc(tt(o, sq[:], ps[:], ALU.mult))
                            wait(gelu_tanh, i + 1)
                            free(step, stt(o, o, 1.0, ps[:], ALU.add, ALU.mult))
                    elif kind == "conv":
                        wait(raw_copied, copied_count(n + 2))
                        conv_done.inc(convolve(conv_a[:], ga[:, n, :], lambda s: col("ssd_conv_w", 6 * (3 - s) + n),
                                               col("ssd_conv_b", n)))
                        wait(conv_tanh, n + 1)
                        stt(ga[:, n, :], conv_b[:], 1.0, conv_a[:], ALU.add, ALU.mult)
                        dve.drain()
                    elif kind == "ssd_zero":
                        dve.memset(tmp1k[8][:], 0.0)
                        ssd_state.inc(dve.drain())
                    elif kind == "ssd_mid":
                        ed, ec, g, v, v2 = tmp2k[0], tmp2k[1], tmp1k[4], tmp1k[5], tmp1k[6]
                        by_head = lambda t, m: t.rearrange("p (h m) -> p h m", m=m)
                        cums = by_head(core[0][:], P)
                        wait(ssd_pre_done, n + 1)
                        tt(by_head(g[:], P), by_head(core[1][:, 0:256], P),
                           cst("causal").unsqueeze(1).to_broadcast([P, 2, P]), ALU.mult)
                        wait(ssd_copied, n + 1)
                        for hd in range(4):
                            ts(ed[:, chunk(hd)], core[0][:, chunk(hd)], columns[:, 2, 4 * n + hd:4 * n + hd + 1], 0.0,
                               ALU.subtract, ALU.min)
                        dve.tensor_copy(te[:, 4:8], cums[:, :, P - 1])
                        tt(te[:, 0:4], cums[:, :, P - 1], columns[:, 2, 4 * n:4 * n + 4], ALU.subtract)
                        ssd_exponents.inc(dve.drain())
                        dt4 = columns[:, 0, 4 * n:4 * n + 4].unsqueeze(2).to_broadcast([P, 4, 64])
                        tt(by_head(v[:], 64), by_head(core[2][:, 0:256], 64), dt4, ALU.mult)
                        ssd_banks_read.inc(dve.drain())
                        for gr in range(2):
                            o = ec[:, chunk(gr, 256)].rearrange("p (i m) -> p i m", i=2)
                            tt(o, o, ga[:, 4 + gr, chunk(n)].unsqueeze(1).to_broadcast([P, 2, P]), ALU.mult)
                        wait(ssd_exp, n + 1)
                        for gr in range(2):
                            o = ed[:, chunk(gr, 256)].rearrange("p (i m) -> p i m", i=2)
                            tt(o, o, g[:, chunk(gr)].unsqueeze(1).to_broadcast([P, 2, P]), ALU.mult)
                        tt(by_head(v2[:], 64), by_head(v[:], 64), te[:, 0:4].unsqueeze(2).to_broadcast([P, 4, 64]),
                           ALU.mult)
                        ssd_operands.inc(dve.drain())
                    elif kind == "ssd_b":
                        hs = tmp1k[8][:].rearrange("p (h m) -> p h m", m=64)
                        wait(ssd_b_done, n + 1)
                        tt(hs, hs, te[:, 4:8].unsqueeze(2).to_broadcast([P, 4, 64]), ALU.mult)
                        dve.drain()
                        tt(tmp1k[8][:], tmp1k[8][:], core[3][:, 256:512], ALU.add)
                        for j in range(2):
                            o = ga[:, j, chunk(n)]
                            stt(o, o, head_par[:, 12 + j:13 + j], core[3][:, chunk(j)], ALU.mult, ALU.add)
                        ssd_state.inc(dve.drain())
                    elif kind == "ssd_gate":
                        for j in range(2):
                            tt(y[:, j, :], y[:, j, :], ga[:, j, :], ALU.mult)
                        norm_in.inc(dve.drain())
                    elif kind == "ssd_stats":
                        ps = products(step)
                        free(step, ts(stat[:, 0, 0:8], ps[:, 0:8], 1 / (4 * GW), None, ALU.mult))
                        norm_var.inc(dve.memset(stat[:, 0, 8:32], 1.0))
                        wait(norm_dev, 1)
                        norm_rstd.inc(dve.reciprocal(stat[:, 0, :], stat[:, 0, :]))
                    elif kind == "ssd_norm":
                        for h in range(2):
                            ps = products(step, h)
                            for j in range(2):
                                o = y[:, j, half_of(h)]
                                last = stt(o, o, col("ssd_norm_w", j), ps[:], ALU.mult, ALU.mult)
                            free(step, last, h)
                        y_final.inc(dve.drain())
                    elif kind == "rotate":
                        h = step[2]
                        if n == 0 and h == 0:
                            dve.wait_ge(rotary_loaded.sem, rotary_loaded.at(l, 1))
                        ps = products(step)
                        t_ = tmp2k[5]
                        o = gb[:, n, half_of(h)]
                        free(step, tt(t_[:], cos_sin[:, 1, half_of(h)], ps[:], ALU.mult))
                        tt(o, o, cos_sin[:, 0, half_of(h)], ALU.mult)
                        dve.drain()
                        rotate_lo.inc(tt(o, o, t_[:], ALU.add))
                        dve.drain()
                    elif kind == "ret_zero":
                        dve.memset(tmp1k[6][:], 0.0)
                        ret_state.inc(dve.drain())
                    elif kind == "ret_mid":
                        m, kt, qg = tmp2k[0], tmp1k[2], tmp1k[4]
                        by = lambda t, w: t.rearrange("p (h m) -> p h m", m=w)
                        tt(by(qg[:], P), gb[:, 0:2, chunk(n)], by(cst("ret_in"), P), ALU.mult)
                        wait(ret_pre_done, n + 1)
                        for i in range(2):
                            tt(by(m[:], P)[:, i::2, :], by(core[i][:, 0:256], P), by(cst("ret_decay"), P)[:, i::2, :],
                               ALU.mult)
                        wait(ret_v, n + 1)
                        tt(by(kt[:], 64), by(core[2][:, 0:256], 64), cst("ret_end").unsqueeze(2).to_broadcast([P, 4, 64]),
                           ALU.mult)
                        ret_operands.inc(dve.drain())
                    elif kind == "ret_b":
                        st, hs = tmp1k[5], tmp1k[6]
                        wait(ret_b_done, n + 1)
                        by = lambda t, w: t.rearrange("p (h m) -> p h m", m=w)
                        tt(by(st[:], P), by(core[3][:, 256:512], P), cst("block2").unsqueeze(1).to_broadcast([P, 2, P]),
                           ALU.mult)
                        dve.tensor_copy(gb[:, 4:6, chunk(n)], by(core[3][:, 0:256], P))
                        dve.drain()
                        for j in range(2):
                            stt(hs[:, chunk(j)], hs[:, chunk(j)], cst("ret_chunk")[:, j:j + 1], st[:, chunk(j)],
                                ALU.mult, ALU.add)
                        ret_state.inc(dve.drain())
                    elif kind == "ret_stats":
                        ps = products(step)
                        free_last = ts(stat[:, 1, :], ps[:, 32:64], 1 / 64, None, ALU.mult)
                        dve.drain()
                        tt(stat[:, 2, :], stat[:, 1, :], stat[:, 1, :], ALU.mult)
                        dve.drain()
                        free(step, stt(stat[:, 0, :], ps[:, 0:32], 1 / 64, stat[:, 2, :], ALU.mult, ALU.subtract))
                        norm_var.inc(dve.drain())
                        wait(norm_dev, 2)
                        norm_rstd.inc(dve.reciprocal(stat[:, 0, :], stat[:, 0, :]))
                    elif kind == "ret_norm":
                        u = 0
                        for h in range(2):
                            for j in range(2):
                                o = gb[:, 4 + j, half_of(h)]
                                ps = products(step, u)
                                free(step, tt(o, o, ps[:], ALU.subtract), u)
                                dve.drain()
                                ps = products(step, u + 1)
                                free(step, stt(o, o, col("ret_norm_w", j), ps[:], ALU.mult, ALU.mult), u + 1)
                                dve.drain()
                                tt(y[:, 2 + j, half_of(h)], y[:, 2 + j, half_of(h)], o, ALU.mult)
                                u += 2
                        y_final.inc(dve.drain())
                    elif kind == "gla_gate":
                        for h in range(2):
                            ps = products(step, h)
                            free(step, ts(ga[:, 4, half_of(h)], ps[:], col("gla_bg"), None, ALU.add), h)
                        gla_gate_x.inc(dve.drain())
                        wait(gla_gate_act, 1)
                        stt(ga[:, 4, :], ga[:, 4, :], 0.0, ga[:, 5, :], ALU.min, ALU.subtract)
                        dve.drain()
                        dve.memset(ga[:, 5, :], 1.0)
                        dve.drain()
                        dve.memset(ga[:, 5, 0:T:64], 0.0)
                        dve.drain()
                        gla_cum.inc(dve.tensor_tensor_scan(ga[:, 4, :], ga[:, 5, :], ga[:, 4, :], 0.0, ALU.mult, ALU.add))
                    elif kind == "gla_scale":
                        wait(gla_gate_act, 2)
                        wait(raw_copied, copied_count(19))
                        stt(ga[:, 0, :], ga[:, 0, :], 32 ** -0.5, ga[:, 5, :], ALU.mult, ALU.mult)
                        tt(ga[:, 1, :], ga[:, 1, :], ga[:, 4, :], ALU.mult)
                        dve.drain()
                        by = lambda t: t.rearrange("p (c t) -> p c t", t=64)
                        tt(by(ga[:, 4, :]), by(ga[:, 1, :]),
                           by(ga[:, 5, :])[:, :, 63:64].to_broadcast([P, T // 64, 64]), ALU.mult)
                        dve.drain()
                    elif kind in ("gla_zero", "gla_mid"):
                        by = lambda t: t.rearrange("p (h t) -> p h t", h=4)
                        if kind == "gla_zero":
                            for t in (gla_h[0], gla_k, *gla_m):
                                dve.memset(t[:], 0.0)
                        else:
                            if n >= 2:
                                wait(gla_c_done, n - 1)
                            wait(gla_pre_done, n + 1)
                            for i in range(2):
                                r = slice(64 * i, 64 * i + 64)
                                tt(by(gla_m[n % 2][r, :])[:, :, chunk(i, 64)], by(core[0][r, 0:256]),
                                   cst("causal64", r).unsqueeze(1).to_broadcast([64, 4, 64]), ALU.mult)
                        c = 0 if kind == "gla_zero" else n + 1
                        if c < NCH:
                            tt(by(tmp2k[0][:]), ga[:, 0, chunk(c)].unsqueeze(1).to_broadcast([P, 4, P]),
                               cst("head4").unsqueeze(2).to_broadcast([P, 4, P]), ALU.mult)
                        (gla_zeroed if kind == "gla_zero" else gla_masked).inc(dve.drain())
                    elif kind == "gla_b":
                        wait(gla_b_done, n + 1)
                        for i in range(2):
                            tt(gla_st[i][:], core[1][:, chunk(i, 256)], cst("block4"), ALU.mult)
                        for i in range(2):
                            dve.drain()
                            end = P * n + 64 * i + 63
                            stt(gla_h[(2 * n + i + 1) % 3][:], gla_h[(2 * n + i) % 3][:], ga[:, 5, end:end + 1],
                                gla_st[i][:], ALU.mult, ALU.add)
                        gla_state.inc(dve.drain())
                    elif kind == "gla_stats":
                        ps = products(step)
                        free(step, ts(stat[:, 0, :], ps[:, 0:32], 1 / 64, None, ALU.mult))
                        norm_var.inc(dve.drain())
                        wait(norm_dev, 3)
                        norm_rstd.inc(dve.reciprocal(stat[:, 0, :], stat[:, 0, :]))
                    elif kind == "gla_norm":
                        for j in range(2):
                            o = ga[:, 2 + j, half_of(n)]
                            ps = products(step, j)
                            free(step, stt(o, o, col("gla_norm_w", j), ps[:], ALU.mult, ALU.mult), j)
                            dve.drain()
                            gla_final.inc(tt(y[:, 6 + j, half_of(n)], y[:, 6 + j, half_of(n)], o, ALU.mult))
                    elif kind == "lru_conv":
                        wait(raw_copied, copied_count(22 + n))
                        lru_xr.inc(convolve(gb[:, 2 + n, :], gb[:, n, :], lambda s: col("lru_conv_w", 2 * (3 - s) + n),
                                            col("lru_conv_b", n)))
                    elif kind == "lru_gate":
                        xr, e, fi, g = gb[:, 2 + n, :], gb[:, 4, :], gb[:, 5, :], gb[:, n, :]
                        wait(lru_act, 3 * n + 1)
                        stt(fi, fi, 1.0, xr, ALU.add, ALU.mult)
                        dve.drain()
                        wait(lru_act, 3 * n + 2)
                        tt(xr, e, e, ALU.mult)
                        dve.drain()
                        lru_in.inc(stt(g, xr, 1.0, g, ALU.add, ALU.mult))
                    elif kind == "lru_scan":
                        e, fi, g = gb[:, 4, :], gb[:, 5, :], gb[:, n, :]
                        wait(lru_act, 3 * n + 3)
                        tt(fi, fi, g, ALU.mult)
                        dve.drain()
                        lru_dve.inc(dve.tensor_tensor_scan(g, e, fi, 0.0, ALU.mult, ALU.add))
                    elif kind == "lru_out":
                        j, h = divmod(n, 2)
                        o = y[:, 4 + j, half_of(h)]
                        dve.drain()
                        lru_final.inc(stt(o, gb[:, j, half_of(h)], 0.25, o, ALU.mult, ALU.mult))
                    elif kind == "y_split":
                        h, k = divmod(n, KD)
                        wait(y_hi, n + 1)
                        y_lo.inc(tt(op_lo[:, k, half_of(h)], y[:, k, half_of(h)],
                                    op_hi[:, k, half_of(h)].bitcast(F32), ALU.subtract))

                def add_products(d, h, bank, signal, tile, gate):
                    dve.wait_ge(signal.sem, signal.at(l, tile))
                    o = ax[:, d, half_of(h)]
                    return stt(o, ring[bank][:], gate[:, d:d + 1], o, ALU.mult, ALU.add)

                def layer_norm(which, unit, misc, bank0, tile0, gate):
                    def add_square(i):
                        d, h = divmod(i, 2)
                        wait(z_sq, 16 * which + i + 1)
                        q = tmp[:, 2 + h, :]
                        if d == 0:
                            sums_made.inc(dve.tensor_copy(q, tmp[:, 4 + i % 2, :]))
                        else:
                            sums_made.inc(tt(q, q, tmp[:, 4 + i % 2, :], ALU.add))

                    for i in range(16):
                        d, h = divmod(i, 2)
                        bank = (bank0 + i) % 4
                        bank_free[bank].inc(add_products(d, h, bank, tile_done if h else half_done, tile0 + d + 1, gate))
                        z_made.inc(dve.drain())
                        o = tmp[:, h, :]
                        if d == 0:
                            dve.tensor_copy(o, ax[:, d, half_of(h)])
                        else:
                            tt(o, o, ax[:, d, half_of(h)], ALU.add)
                        if i:
                            add_square(i - 1)
                    add_square(15)
                    for h in range(2):
                        wait(unit_done, misc + 1)
                        ps = ring[unit % 4]
                        bank_free[unit % 4].inc(ts(stat[:, 0, 0:4], ps[:, 0:4], 1 / D, None, ALU.mult))
                        dve.drain()
                        tt(stat[:, 2, 0:4], stat[:, 0, 0:4], stat[:, 0, 0:4], ALU.mult)
                        dve.drain()
                        wait(unit_done, misc + 2)
                        ps = ring[(unit + 1) % 4]
                        bank_free[(unit + 1) % 4].inc(stt(stat[:, 1, 0:4], ps[:, 0:4], 1 / D, stat[:, 2, 0:4],
                                                          ALU.mult, ALU.subtract))
                        ln_var.inc(dve.drain())
                        wait(ln_dev, 2 * which + h + 1)
                        ln_rstd.inc(dve.reciprocal(stat[:, 1, 0:4], stat[:, 1, 0:4]))
                        wait(unit_done, misc + 4)
                        mean, rstd = ring[(unit + 2) % 4], ring[(unit + 3) % 4]
                        for k in range(KD):
                            o = ax[:, k, half_of(h)]
                            last = tt(o, o, mean[:], ALU.subtract)
                            if k == KD - 1:
                                bank_free[(unit + 2) % 4].inc(last)
                            dve.drain()
                            tt(o, o, rstd[:], ALU.mult)
                            ln_norm.inc(dve.drain())
                        bank_free[(unit + 3) % 4].inc(dve.drain())
                        unit, misc = unit + 4, misc + 4

                dve.wait_ge(residual_loaded.sem, residual_loaded.at(l, 1))
                layer_norm(0, UNIT_LN1, MISC_LN1, UNIT_OUT % 4, N_IN, mod[:, 0:8])
                split_h(16)

                def ffn_part(t2, f0, size, times):
                    with dve.Fori(0, size) as i:
                        for h in range(2):
                            n = (i + f0) * 2 + (h + 1)
                            dve.wait_ge(up_tanh.sem, up_tanh.at(l, n))
                            bank_free[2 * h].inc(stt(tmp[:, 2 + h, :], tmp[:, h, :], 1.0, ring[2 * h][:],
                                                     ALU.add, ALU.mult), times * size)
                            done = tile_done if h else half_done
                            dve.drain()
                            dve.wait_ge(done.sem, done.at(l, (i + t2) * 2 + 2))
                            bank_free[2 * h + 1].inc(tt(tmp[:, 4 + h, :], tmp[:, 2 + h, :], ring[2 * h + 1][:],
                                                        ALU.mult), times * size)
                            up_act.inc(dve.drain(), times * size)
                            dve.wait_ge(up_hi.sem, up_hi.at(l, n))
                            hidden = lambda t: t[:, bass.ds(i, 1), half_of(h)].rearrange("p a t -> p (a t)")
                            up_lo.inc(tt(hidden(act_lo), tmp[:, 4 + h, :], hidden(act_hi).bitcast(F32),
                                         ALU.subtract), times * size)

                t2 = (N_IN + KD) // 2
                with dve.Fori(0, FULL_PARTS) as part:
                    ffn_part(part * (PART + 4) + t2, part * PART, PART, FULL_PARTS)
                    for d in range(KD):
                        for h in range(2):
                            bank = (2 * d + h) % 4
                            bank_free[bank].inc(add_products(
                                d, h, bank, tile_done if h else half_done,
                                (part * (PART + 4) + (t2 + PART)) * 2 + (d + 1), mod[:, 24:32]), FULL_PARTS)
                t2 += FULL_PARTS * (PART + 4)
                ffn_part(t2, FULL_PARTS * PART, LAST_PART, 1)
                layer_norm(1, UNIT_LN2, MISC_LN2, 0, 2 * (t2 + LAST_PART), mod[:, 24:32])

        wrong = [(s.name, s.layer, s.counted) for s in Signal.all if s.layer and s.layer != s.counted]
        assert not wrong, wrong


_INS = ["x", "c", "positions", "w_ada", "b_ada", "w_in", "ssd_conv_w", "ssd_conv_b", "ssd_dt_bias", "ssd_a_log",
        "ssd_d", "ssd_norm_w", "ret_norm_w", "lru_conv_w", "lru_conv_b", "lru_wa", "lru_ba", "lru_wx", "lru_bx",
        "lru_lambda", "gla_wg2", "gla_bg", "gla_norm_w", "w_out", "ln1_w", "ln1_b", "ffn_w_up", "ffn_w_down",
        "ln2_w", "ln2_b"]


def kernel(**inputs):
    import numpy as _np
    import concourse.bacc as _bacc
    from concourse import mybir as _mybir
    from concourse.bass_utils import run_bass_kernel_spmd as _run

    nc = _bacc.Bacc("TRN2", target_bir_lowering=False, num_devices=1)
    arrays, args = {}, {}
    for name in _INS + ["const"]:
        v = constants() if name == "const" else _np.ascontiguousarray(inputs[name])
        arrays[f"in_{name}"] = v
        args[name] = nc.dram_tensor(f"in_{name}", v.shape, _mybir.dt.from_np(v.dtype), kind="ExternalInput").ap()
    out = nc.dram_tensor("out_0", (1, T, D), _mybir.dt.float32, kind="ExternalOutput").ap()
    nc.disable_value_cache = True
    build(nc, args, out)
    return _run(nc, [arrays], core_ids=[0]).results[0]["out_0"]
```

```python
import math
from contextlib import ExitStack

import numpy as np

import concourse.bass as bass
import concourse.mybir as mybir

F32 = mybir.dt.float32
F32R = mybir.dt.float32r
I32 = mybir.dt.int32
ALU = mybir.AluOpType
ACT = mybir.ActivationFunctionType

P = 128
D = 1024
T = 1024
DEPTH = 2
KD = D // P
HALF = 512
GW = 256
CH = 128
NCH = T // CH
XBC = 768
D_FF = 2816
NF = D_FF // P
PART = 6
ALPHA = (2 * DEPTH) ** 0.25
EPS = 1e-5
TWO_PI = 2 * math.pi

COL_Z, COL_XBC, COL_DT = 0, 256, 1024
COL_RET = 1028
COL_LRU_GATE, COL_LRU_X = 2052, 2308
COL_GLA_QKV, COL_GLOW, COL_GLA_R = 2564, 3076, 3092

IN_SEGMENTS = [(COL_Z, 8), (COL_RET, 8), (COL_GLA_QKV, 4), (COL_GLA_R, 2), (COL_LRU_X, 2), (COL_LRU_GATE, 2)]
N_IN = sum(n for _, n in IN_SEGMENTS)
FULL_PARTS = NF // PART
LAST_PART = NF - FULL_PARTS * PART
N_TILES = N_IN + KD + 2 * NF + (FULL_PARTS + 1) * KD
ADA_PAIRS = 24

ROWS = {}
_n = 0
for _name, _count in [("ssd_conv_w", 24), ("ssd_conv_b", 6), ("ssd_norm_w", 2), ("ret_norm_w", 2),
                      ("gla_norm_w", 2), ("lru_conv_w", 8), ("lru_conv_b", 2), ("lru_ba", 2),
                      ("lru_bx", 2), ("lru_lambda", 2), ("gla_bg", 1), ("ln1_w", 8), ("ln1_b", 8),
                      ("ln2_w", 8), ("ln2_b", 8)]:
    ROWS[_name] = (_n, _count)
    _n += _count
N_ROWS = _n

CONST = {}
_n = 0
for _name, _count in [("ident", 128), ("causal", 128), ("perm", 128), ("ret_decay", 512),
                      ("ret_in", 256), ("block2", 128), ("block4", 256), ("causal64", 64),
                      ("ret_end", 4), ("head4", 4), ("ret_chunk", 2), ("freq", 1), ("eps", 1),
                      ("head2", 2), ("one", 1)]:
    CONST[_name] = (_n, _count)
    _n += _count
N_CONST = _n


def constants():
    c = np.zeros((P, N_CONST), np.float64)
    p = np.arange(P)

    def put(name, value):
        a, n = CONST[name]
        c[:, a:a + n] = np.asarray(value).reshape(P, n)

    gamma = 1.0 - 2.0 ** (-5.0 - np.arange(4))
    put("ident", np.eye(P))
    put("causal", p[:, None] <= p[None, :])
    perm = np.zeros((P, P))
    for m in range(P):
        perm[m + 32 if m % 64 < 32 else m - 32, m] = -1.0 if m % 64 < 32 else 1.0
    put("perm", perm)
    lag = p[None, :] - p[:, None]
    put("ret_decay", np.stack([np.where(lag >= 0, g ** np.maximum(lag, 0), 0) * 0.125 for g in gamma], 1))
    put("ret_in", np.stack([gamma[2 * j + p // 64][:, None] ** (p + 1.0) for j in range(2)], 1))
    put("block2", p[:, None] // 64 == p[None, :] // 64)
    put("block4", p[:, None] // 32 == np.arange(256)[None, :] // 64)
    put("causal64", p[:, None] % 64 <= np.arange(64)[None, :])
    put("ret_end", 0.125 * gamma[None, :] ** (127.0 - p[:, None]))
    put("head4", p[:, None] // 32 == np.arange(4)[None, :])
    put("ret_chunk", np.stack([gamma[2 * j + p // 64] ** 128.0 for j in range(2)], 1))
    put("freq", 10000.0 ** (-(p % 32) / 32.0))
    put("eps", np.full(P, EPS))
    put("head2", p[:, None] // 64 == np.arange(2)[None, :])
    put("one", np.ones(P))
    return c.astype(np.float32)


def mixer_order():
    order = [("params",), ("small", 0), ("small", 1)]

    def tile(t):
        group = [("proj", t, 0), ("proj", t, 1)]
        if t < ADA_PAIRS:
            group = [("ada_sum", t)] + group + [("ada", t)]
        return group

    def spread(units, groups):
        halves = sum(u[0] == "proj" for u in units)
        n, seen, out = 0, 0, []
        for u in units:
            out.append(u)
            if u[0] == "proj":
                seen += 1
                want = len(groups) * seen // halves
                out += sum(groups[n:want], [])
                n = want
        return out

    for t in range(8):
        order += tile(t)
        if t == 0:
            order.append(("dt",))
        if t == 3:
            order.append(("dt_cum",))
        if 2 <= t:
            order.append(("conv", t - 2))
    def pipelined(name):
        groups = [[(name + "_zero",), (name + "_pre", 0), (name + "_mid", 0)]]
        for c in range(NCH):
            more = c + 1 < NCH
            groups.append([(name + "_pre", c + 1)] * more + [(name + "_b", c)] + [(name + "_mid", c + 1)] * more)
        return groups

    order += tile(8)
    units = []
    for t in range(9, 15):
        units += tile(t)
        if t <= 12:
            units += [("rotate", t - 9, 0), ("rotate", t - 9, 1)]
    order += spread(units, pipelined("ssd"))
    order += [("ssd_gate",)]
    ret = pipelined("ret")
    t15, t16 = tile(15), tile(16)
    order += t15[:2] + ret[0][:1] + t15[2:3] + ret[0][1:] + [("ssd_stats",)] + t15[3:]
    order += t16[:2] + [("ssd_norm",)] + ret[1] + t16[2:] + ret[2] + [("gla_gate",)]
    units = []
    for t in range(17, 20):
        units += tile(t)
    ret[4] = ret[4] + [("gla_cum",)]
    order += spread(units, ret[3:]) + [("ret_square",), ("gla_scale",)]
    gla = [[("gla_c", c - 1)] * (c > 0) + [("gla_b", c)] * (c < NCH) +
           [("gla_pre", c + 1), ("gla_mid", c + 1)] * (c + 1 < NCH) for c in range(NCH + 1)]
    t20, t21, t22, t23, t24 = (tile(t) for t in range(20, 25))
    order += t20[:2] + [("gla_zero",)] + t20[2:3] + [("gla_pre", 0), ("gla_mid", 0), ("ret_stats",)] + t20[3:] + gla[0]
    order += t21[:2] + [("ret_norm",)] + gla[1] + t21[2:] + gla[2]
    order += t22[:2] + gla[3] + t22[2:] + [("lru_conv", 0)] + gla[4]
    order += t23[:2] + [("lru", 0)] + gla[5] + t23[2:] + [("lru_gate", 0), ("lru_conv", 1)] + gla[6]
    order += t24[:1] + [("lru_scan", 0)] + gla[7] + [("lru", 1)] + t24[1:] + gla[8]
    order += [("gla_square",), ("lru_gate", 1), ("proj", 25, 0), ("gla_stats",), ("lru_scan", 1), ("lru_out", 0),
              ("lru_out", 1), ("lru_out", 2)]
    order += [("y_split", k) for k in range(6)]
    order += [("proj", 25, 1), ("lru_out", 3), ("gla_norm", 0), ("y_split", 6), ("y_split", 7), ("gla_norm", 1)]
    order += [("y_split", k) for k in range(8, 16)]
    return order


ORDER = mixer_order()
UNITS_OF = {"params": 1, "small": 1, "dt": 1, "dt_cum": 1, "proj": 1, "ada": 1, "rotate": 1,
            "ssd_stats": 1, "ssd_norm": 2, "ret_stats": 1, "ret_norm": 8, "gla_stats": 1,
            "gla_gate": 2, "lru": 4}
UNIT = {}
_n = 0
for _step in ORDER:
    UNIT[_step] = _n
    _n += UNITS_OF.get(_step[0], 0)
UNIT_OUT = _n
MISC = {}
_n = 0
for _step in ORDER:
    MISC[_step] = _n
    _n += 0 if _step[0] in ("proj", "ada") else UNITS_OF.get(_step[0], 0)
N_MISC = _n
UNIT_FFN = UNIT_OUT + 2 * KD
UNITS = UNIT_FFN + 4 * NF + 2 * KD * (FULL_PARTS + 1)
UNITS_0 = 20
assert UNIT_FFN % 4 == 0 and UNITS % 4 == 0 and UNITS_0 % 4 == 0
NORM_UNITS = [divmod(i, 2) for i in range(2 * KD - 4)] + [(KD - 2, 0), (KD - 1, 0), (KD - 2, 1), (KD - 1, 1)]


class Signal:

    all = []

    def __init__(self, ctx, nc, name, layer, before=0, step=1):
        self.sem = ctx.enter_context(nc.semaphore(name))
        self.name, self.layer, self.before, self.step = name, layer, before, step
        self.counted = 0
        Signal.all.append(self)

    def inc(self, instruction, times=1):
        self.counted += times
        instruction.then_inc(self.sem, self.step)

    def at(self, l, n):
        return l * (self.layer * self.step) + n * self.step + self.before * self.step


def build(nc, a, out):
    Signal.all = []
    ctx = ExitStack()
    with ctx:
        KB = 1024
        place_at = [(nc.sbuf_base + 63) // 64 * 64]

        def region(size):
            offset = place_at[0]
            place_at[0] += (size + 31) // 32 * 32
            assert place_at[0] <= nc.sbuf_usable_end, place_at[0] - nc.sbuf_usable_end
            return offset

        def place(name, shape, dt=F32, at=None):
            if at is None:
                at = region(4 * int(np.prod(shape[1:])))
            return nc.alloc_sbuf_tensor_at(name, shape, dt, offset=at)

        op_hi = place("op_hi", [P, KD, T], F32R)
        op_lo = place("op_lo", [P, KD, T], F32R)
        ada_first = nc.alloc_sbuf_tensor_at("ada_first", [P, KD, 2 * D], F32, offset=place_at[0] - 64 * KB)
        w_raw = [place(f"w_raw{i}", [P, KD, P]) for i in range(2)]
        w_hi = [place(f"w_hi{i}", [P, KD, P], F32R) for i in range(2)]
        w_lo = [place(f"w_lo{i}", [P, KD, P], F32R) for i in range(2)]
        ada_raw = [place(f"ada_raw{i}", [P, 4, 256]) for i in range(2)]
        ada_sum = [place(f"ada_sum{i}", [P, 256]) for i in range(2)]
        X = region(32 * KB)
        Y = region(48 * KB)
        TMP = region(16 * KB)
        ax = place("ax", [P, KD, T], at=X)
        act_hi = place("act_hi", [P, PART, T], F32R, at=Y)
        act_lo = place("act_lo", [P, PART, T], F32R, at=Y + 24 * KB)
        x_rows = place("x_rows", [P, 8, D], at=Y)
        angle = place("angle", [P, 4, T], at=Y + 32 * KB)
        ga = place("ga", [P, 6, T], at=X)
        gb = place("gb", [P, 6, T], at=X + 24 * KB)
        y = place("y", [P, 8, T], at=Y + 16 * KB)
        cos_sin = place("cos_sin", [P, 2, T], at=Y + 32 * KB)
        small_hi = place("small_hi", [P, KD * 48 + 80], F32R, at=Y + 40 * KB)
        small_lo = place("small_lo", [P, KD * 48 + 80], F32R, at=Y + 42 * KB)
        tmp = place("tmp", [P, 8, HALF], at=TMP)
        small = place("small", [48, T], at=TMP)
        tmp2k = [place(f"tmp2k{i}", [P, HALF], at=TMP + (4 + 2 * i) * KB) for i in range(6)]
        tmp1k = [place(f"tmp1k{i}", [P, 256], at=TMP + (4 + i) * KB) for i in range(12)]
        gla_m = [tmp2k[1], place("gla_m1", [P, HALF], at=TMP)]
        gla_v = [tmp1k[5], place("gla_v1", [P, 256], at=TMP + 3 * KB)]
        gla_k = tmp1k[4]
        gla_h = [tmp1k[6], tmp1k[7], tmp1k[10]]
        gla_st = [tmp1k[11], place("gla_st1", [P, 256], at=TMP + 2 * KB)]
        conv_a = place("conv_a", [P, T], at=TMP + 4 * KB)
        conv_b = place("conv_b", [P, T], at=TMP + 8 * KB)
        const = place("consts", [P, N_CONST])
        par = place("par", [P, N_ROWS])
        par_rows = place("par_rows", [N_ROWS, P])
        b_ada = place("b_ada_columns", [P, DEPTH, 48])
        b_ada_rows = place("b_ada_rows", [48, DEPTH, P])
        mod = place("mod", [P, 32])
        mod_next = place("mod_next", [P, 16])
        fold = place("fold", [P, 4, KD])
        b_mod = place("b_mod", [P, 48])
        c_rows = place("c_rows", [KD, P])
        c_col = place("c_col", [P, 2, KD])
        lru_w = place("lru_w", [P, 2, 2, P])
        gate_w = place("gate_w", [16, P])
        head_par = place("head_par", [P, 14])
        columns = place("columns", [P, 5, 32])
        lru_col = place("lru_col", [P, 6, 2])
        stat = place("stat", [P, 4, 32])
        te = place("te", [P, 8])

        ring = [ctx.enter_context(nc.psum_tensor(f"ring{i}", [P, HALF], F32)) for i in range(4)]
        core = [ctx.enter_context(nc.psum_tensor(f"core{i}", [P, HALF], F32)) for i in range(4)]
        residual = nc.dram_tensor("residual", (KD, P, T), F32, kind="Internal").ap()
        rotary = nc.dram_tensor("rotary", (2, P, T), F32, kind="Internal").ap()

        def signal(name, layer, before=0, step=1):
            return Signal(ctx, nc, name, layer, before, step)

        const_loaded = signal("const_loaded", 0, 4, 16)
        x_loaded = [signal(f"x_loaded{i}", 0, 1, 16) for i in range(4)]
        pos_loaded = signal("pos_loaded", 0, 1, 16)
        rows_loaded = signal("rows_loaded", 15, 0, 16)
        heads_loaded = signal("heads_loaded", 3, 0, 16)
        lru_w_loaded = signal("lru_w_loaded", 9, 0, 16)
        small_loaded = signal("small_loaded", 2, 0, 16)
        raw_loaded = [signal(f"raw_loaded{i}", N_TILES // 2, 0, 16) for i in range(2)]
        raw_free = [signal(f"raw_free{i}", N_TILES // 2, 1) for i in range(2)]
        split_done = signal("split_done", N_TILES)
        half_done = signal("half_done", N_TILES)
        tile_done = signal("tile_done", N_TILES, 2)
        small_split = signal("small_split", 1)
        zeroed = signal("zeroed", 0, 1)
        pool_passed = signal("pool_passed", 0)
        ada_first_loaded = [signal(f"ada_first_loaded{i}", 0, 1, 16) for i in range(4)]
        ada_loaded = [signal(f"ada_loaded{i}", ADA_PAIRS, 0, 16) for i in range(2)]
        ada_raw_free = [signal(f"ada_raw_free{i}", ADA_PAIRS + 1 - i, 1) for i in range(2)]
        ada_summed = [signal(f"ada_summed{i}", ADA_PAIRS) for i in range(2)]
        ada_sum_used = signal("ada_sum_used", ADA_PAIRS, 1)
        w_hi_made = signal("w_hi_made", N_TILES)
        residual_saved = signal("residual_saved", 2, 0, 16)
        residual_loaded = signal("residual_loaded", 1, 0, 16)
        rotary_saved = signal("rotary_saved", 0, 1, 16)
        rotary_loaded = signal("rotary_loaded", 1, 0, 16)
        bank_free = [signal(f"bank_free{i}", UNITS // 4, UNITS_0 // 4) for i in range(4)]
        unit_done = signal("unit_done", N_MISC, UNITS_0)
        ax_half1 = signal("ax_half1", 1, 1)
        h_value = signal("h_value", 32, 16)
        y_hi = signal("y_hi", 16)
        gate_tanh = signal("gate_tanh", 12)
        raw_copied = signal("raw_copied", 36)
        conv_tanh = signal("conv_tanh", 6)
        small_copied = signal("small_copied", 2)
        par_copied = signal("par_copied", 1)
        dt_exp = signal("dt_exp", 1)
        ssd_copied = signal("ssd_copied", NCH)
        ssd_exp = signal("ssd_exp", NCH)
        ret_v = signal("ret_v", NCH)
        gla_kv = signal("gla_kv", NCH)
        gla_out = signal("gla_out", NCH)
        gla_gate_act = signal("gla_gate_act", 2)
        norm_sq = signal("norm_sq", 3)
        norm_dev = signal("norm_dev", 3)
        norm_wide = signal("norm_wide", 2)
        lru_act = signal("lru_act", 6)
        gelu_sq = signal("gelu_sq", 4)
        gelu_tanh = signal("gelu_tanh", 4)
        z_sq = signal("z_sq", 32)
        ln_dev = signal("ln_dev", 4)
        up_tanh = signal("up_tanh", 2 * NF)
        up_hi = signal("up_hi", 2 * NF)
        c_copied = signal("c_copied", 0, 1)
        c_tanh = signal("c_tanh", 0, 1)
        angle_sin = signal("angle_sin", 0, 1)
        out_copied = [signal(f"out_copied{i}", 0, NCH) for i in range(2)]
        ax_half0 = signal("ax_half0", 1, 1)
        h_lo = signal("h_lo", 32, 16)
        y_lo = signal("y_lo", 16)
        y_final = signal("y_final", 2)
        lru_final = signal("lru_final", 4)
        gla_final = signal("gla_final", 4)
        par_ready = signal("par_ready", 1)
        conv_done = signal("conv_done", 6)
        dt_x = signal("dt_x", 1)
        dt_ready = signal("dt_ready", 1)
        ssd_exponents = signal("ssd_exponents", NCH)
        ssd_banks_read = signal("ssd_banks_read", NCH)
        ssd_operands = signal("ssd_operands", NCH)
        ssd_state = signal("ssd_state", NCH + 1)
        ret_operands = signal("ret_operands", NCH)
        ret_state = signal("ret_state", NCH + 1)
        gla_zeroed = signal("gla_zeroed", 1)
        gla_masked = signal("gla_masked", NCH)
        gla_state = signal("gla_state", NCH)
        gla_gate_x = signal("gla_gate_x", 1)
        gla_cum = signal("gla_cum", 1)
        norm_in = signal("norm_in", 1)
        norm_var = signal("norm_var", 3)
        norm_rstd = signal("norm_rstd", 3)
        lru_xr = signal("lru_xr", 2)
        lru_dve = signal("lru_dve", 2)
        lru_in = signal("lru_in", 2)
        gelu_in = signal("gelu_in", 4)
        z_made = signal("z_made", 32)
        sums_made = signal("sums_made", 32)
        ln_var = signal("ln_var", 4)
        ln_rstd = signal("ln_rstd", 4)
        ln_norm = signal("ln_norm", 32)
        up_act = signal("up_act", 2 * NF)
        up_lo = signal("up_lo", 2 * NF, 2)
        c_ready = signal("c_ready", 0, 1)
        ada_first_summed = signal("ada_first_summed", 0, 4)
        mod_first = signal("mod_first", 0, 1)
        angle_ready = signal("angle_ready", 0, 1)
        rotary_made = signal("rotary_made", 0, 1)
        ssd_pre_done = signal("ssd_pre_done", NCH)
        ssd_b_done = signal("ssd_b_done", NCH)
        ret_pre_done = signal("ret_pre_done", NCH)
        ret_b_done = signal("ret_b_done", NCH)
        gla_pre_done = signal("gla_pre_done", NCH)
        gla_b_done = signal("gla_b_done", NCH)
        gla_c_done = signal("gla_c_done", NCH)
        gla_spread = signal("gla_spread", 4)
        ln_summed = signal("ln_summed", 4)
        ln_spread = signal("ln_spread", 4)
        out_saved = signal("out_saved", 0, 8, 16)

        def cst(name, rows=slice(None)):
            first, n = CONST[name]
            return const[rows, first:first + n]

        def col(name, i=0):
            first, _ = ROWS[name]
            return par[:, first + i:first + i + 1]

        ident, eps, one = cst("ident"), cst("eps"), cst("one")

        def chunk(c, n=CH):
            return slice(c * n, (c + 1) * n)

        def half_of(h):
            return slice(h * HALF, (h + 1) * HALF)

        gate_slot = {0: 0, 1: 1, 14: 2, 15: 3, 20: 6, 21: 7, 24: 4, 25: 5}
        silu_tiles = [0, 1, 14, 15, 20, 21]
        copied_tiles = [t for t in range(N_IN) if t not in gate_slot]

        def copied_to(t):
            if t < 8:
                return ga[:, t - 2, :]
            if t < 14:
                return gb[:, t - 8, :]
            if t < 20:
                return ga[:, t - 16, :]
            return gb[:, t - 22, :]

        def copied_count(t):
            return 2 * copied_tiles.index(t) + 2

        def wide_stat(g, s):
            return gb[:, 2 * s:2 * s + 2, :] if g == 1 else ga[:, 0:2, :]

        block = ctx.enter_context(nc.Block())

        @block.sync
        def _(sp):
            const_loaded.inc(sp.dma_start(const[:], a["const"]))
            const_loaded.inc(sp.dma_start(c_rows[:], a["c"].rearrange("b (k p) -> (b k) p", p=P)))
            for l in range(DEPTH):
                const_loaded.inc(sp.dma_start(b_ada_rows[:, l, :], a["b_ada"][l, :].rearrange("(k p) -> k p", p=P)))
            pos_loaded.inc(sp.dma_start(angle[:, 0, :].bitcast(I32), a["positions"][0, :].partition_broadcast(P)))
            for i in range(4):
                x_loaded[i].inc(sp.dma_start(
                    x_rows[:, 2 * i:2 * i + 2, :],
                    a["x"][0, 256 * i:256 * i + 256, :].rearrange("(k p) d -> p k d", p=P)))

            for i in range(4):
                ada_first_loaded[i].inc(sp.dma_start(
                    ada_first[:, :, 512 * i:512 * i + 512],
                    a["w_ada"][0, :, 512 * i:512 * i + 512].rearrange("(k p) n -> p k n", p=P)))
            def load_head(l, layer):
                sp.wait_ge(ada_raw_free[0].sem, ada_raw_free[0].at(l, 0))
                w_in = a["w_in"][bass.ds(layer, 1)].rearrange("a (k p) n -> p (a k) n", p=P)
                small_raw = ada_raw[0][:].rearrange("p a b -> p (a b)")[:, 0:KD * 48].rearrange("p (k n) -> p k n", n=48)
                small_loaded.inc(sp.dma_start(small_raw[:, :, 0:16], w_in[:, :, COL_GLOW:COL_GLOW + 16]))
                small_loaded.inc(sp.dma_start(small_raw[:, :, 32:36], w_in[:, :, COL_DT:COL_DT + 4]))
                for s in range(2):
                    sp.wait_ge(raw_free[s].sem, raw_free[s].at(l, 0))
                    raw_loaded[s].inc(sp.dma_start(w_raw[s][:], w_in[:, :, chunk(s)]))

            load_head(0, 0)
            for counted in (small_loaded, *raw_loaded):
                counted.counted = 0
            sp.wait_ge(rotary_made.sem, 1)
            rotary_saved.inc(sp.dma_start(rotary.rearrange("a p t -> p a t"), angle[:, 2:4, :]))
            sp.wait_ge(rotary_saved.sem, 16)

            with sp.Fori(0, DEPTH) as l:
                def layer_of(name, at=None):
                    return a[name][bass.ds(l if at is None else at, 1)]

                def load_tile(slot, n, name, row0, rows, col0, times=1):
                    sp.wait_ge(raw_free[slot].sem, raw_free[slot].at(l, n))
                    src = layer_of(name).rearrange("a m n -> (a m) n")[bass.ds(row0, rows * P), bass.ds(col0, P)]
                    raw_loaded[slot].inc(sp.dma_start(w_raw[slot][:, 0:rows, :],
                                                      src.rearrange("(k p) n -> p k n", p=P)), times)

                def load_ada_pair(pair, layer, col0, times=1):
                    for q in range(2):
                        src = layer_of("w_ada", layer).rearrange("a m n -> (a m) n")[
                            512 * q:512 * q + 512, bass.ds(col0, 256)]
                        sp.wait_ge(ada_raw_free[q].sem, ada_raw_free[q].at(l, pair + (1 - q)))
                        ada_loaded[q].inc(sp.dma_start(ada_raw[q][:], src.rearrange("(k p) n -> p k n", p=P)), times)

                for name, (first, count) in ROWS.items():
                    v = layer_of(name)
                    v = v.rearrange("a c (k p) -> (a c k) p", p=P) if len(v.shape) == 3 else \
                        v.rearrange("a (k p) -> (a k) p", p=P)
                    rows_loaded.inc(sp.dma_start(par_rows[first:first + count, :], v))
                for i, name in enumerate(("ssd_a_log", "ssd_dt_bias", "ssd_d")):
                    heads_loaded.inc(sp.dma_start(head_par[:, 4 * i:4 * i + 4],
                                                  layer_of(name).rearrange("a h -> (a h)").partition_broadcast(P)))
                sp.wait_ge(zeroed.sem, 1)
                for m, name in enumerate(("lru_wa", "lru_wx")):
                    for k in range(4):
                        r = slice(64 * (k % 2), 64 * (k % 2) + 64)
                        lru_w_loaded.inc(sp.dma_start(lru_w[r, m, k // 2, r],
                                                      layer_of(name).rearrange("a k i j -> (a k) i j")[k]))
                lru_w_loaded.inc(sp.dma_start(gate_w[:], layer_of("gla_wg2").rearrange("a r n -> (a r) n")))
                for h, half in enumerate((ax_half0, ax_half1)):
                    sp.wait_ge(half.sem, half.at(l, 0))
                    residual_saved.inc(sp.dma_start(residual[:, :, half_of(h)].rearrange("k p t -> p k t"),
                                                    ax[:, :, half_of(h)]))
                sp.wait_ge(tile_done.sem, tile_done.at(l, 0))
                rotary_loaded.inc(sp.dma_start(cos_sin[:], rotary.rearrange("a p t -> p a t")))

                def ada_source(pair):
                    return (None, 2048 + 256 * pair) if pair < 16 else ((l + 1) % DEPTH, 256 * (pair - 16))

                t = 0
                for first, count in IN_SEGMENTS:
                    skip = 2 if t == 0 else 0
                    if t == 0:
                        for s in range(2):
                            load_ada_pair(s, *ada_source(s))
                    with sp.Fori(skip // 2, count // 2) as i:
                        for s in range(2):
                            load_tile(s, i + t // 2, "w_in", 0, KD, i * (2 * P) + (first + s * P),
                                      (count - skip) // 2)
                            if t < ADA_PAIRS:
                                layer, col0 = ada_source(t + s)
                                load_ada_pair(i * 2 + (t + s), layer, i * 512 + col0, (count - skip) // 2)
                    t += count
                with sp.Fori(0, KD // 2) as i:
                    for s in range(2):
                        load_tile(s, i + t // 2, "w_out", 0, KD, i * (2 * P) + s * P, KD // 2)
                t += KD

                def load_part(t2, f0, size, times):
                    with sp.Fori(0, size) as i:
                        load_tile(0, i + t2, "ffn_w_up", 0, KD, (i + f0) * P, times * size)
                        load_tile(1, i + t2, "ffn_w_up", 0, KD, (i + (f0 + NF)) * P, times * size)
                    with sp.Fori(0, KD // 2) as i:
                        for s in range(2):
                            load_tile(s, i + (t2 + size), "ffn_w_down", f0 * P, size, i * (2 * P) + s * P,
                                      times * KD // 2)

                with sp.Fori(0, FULL_PARTS) as part:
                    load_part(part * (PART + KD // 2) + t // 2, part * PART, PART, FULL_PARTS)
                load_part(FULL_PARTS * (PART + KD // 2) + t // 2, FULL_PARTS * PART, LAST_PART, 1)
                load_head(l + 1, (l + 1) % DEPTH)

            for c in range(NCH):
                for done in out_copied:
                    sp.wait_ge(done.sem, c + 1)
                out_saved.inc(sp.dma_start(out[0, chunk(c), :], x_rows[:, c, :]))
            sp.wait_ge(out_saved.sem, 16 * NCH)

        @block.gpsimd
        def _(pool):
            zeroed.inc(pool.memset(lru_w[:], 0.0))
            for s in range(2):
                pool.sem_inc(raw_free[s].sem, 1)
                pool.sem_inc(ada_raw_free[s].sem, 1)
            pool.wait_ge(c_ready.sem, 1)

            def split(l, slot, tile, rows, times=1):
                pool.wait_ge(w_hi_made.sem, w_hi_made.at(l, tile + 1))
                raw_free[slot].inc(pool.tensor_tensor(
                    w_lo[slot][:, 0:rows, :], w_raw[slot][:, 0:rows, :],
                    w_hi[slot][:, 0:rows, :].bitcast(F32), ALU.subtract), times)
                split_done.inc(pool.drain(), times)

            def split_small(l, times=1):
                pool.wait_ge(small_loaded.sem, small_loaded.at(l, 2))
                small_raw = ada_raw[0][:].rearrange("p a b -> p (a b)")[:, 0:KD * 48].rearrange("p (k n) -> p k n", n=48)
                parts = [t[:, 0:KD * 48].rearrange("p (k n) -> p k n", n=48) for t in (small_hi, small_lo)]
                pool.sem_inc(pool_passed.sem, 1)
                pool.memset(small_hi[:].bitcast(F32), 0.0)
                pool.memset(small_lo[:].bitcast(F32), 0.0)
                pool.drain()
                for r in (slice(0, 16), slice(32, 36)):
                    pool.tensor_copy(parts[0][:, :, r], small_raw[:, :, r])
                pool.drain()
                for r in (slice(0, 16), slice(32, 36)):
                    last = pool.tensor_tensor(parts[1][:, :, r], small_raw[:, :, r],
                                              parts[0][:, :, r].bitcast(F32), ALU.subtract)
                ada_raw_free[0].inc(last, times)
                small_split.inc(pool.drain(), times)

            pool.wait_ge(rotary_saved.sem, 16)
            split_small(0, 0)
            for s in range(2):
                split(0, s, s, KD, 0)

            with pool.Fori(0, DEPTH) as l:
                def sum_ada(pair, times):
                    raw = ada_raw[0]
                    pool.wait_ge(ada_loaded[0].sem, ada_loaded[0].at(l, pair + 1))
                    pool.tensor_tensor(raw[:], raw[:], c_col[:, 0, 0:4].unsqueeze(2).to_broadcast([P, 4, 256]), ALU.mult)
                    pool.drain()
                    pool.tensor_tensor(raw[:, 0:2, :], raw[:, 0:2, :], raw[:, 2:4, :], ALU.add)
                    pool.drain()
                    pool.wait_ge(ada_sum_used.sem, ada_sum_used.at(l, pair))
                    ada_raw_free[0].inc(pool.tensor_tensor(ada_sum[0][:], raw[:, 0, :], raw[:, 1, :], ALU.add), times)
                    ada_summed[0].inc(pool.drain(), times)

                def lo_of_h(which):
                    for n in range(2 * KD):
                        h, k = divmod(n, KD)
                        pool.wait_ge(h_value.sem, h_value.at(l, 16 * which + n + 1))
                        h_lo.inc(pool.tensor_tensor(op_lo[:, k, half_of(h)], tmp[:, 6 + n % 2, :],
                                                    op_hi[:, k, half_of(h)].bitcast(F32), ALU.subtract))

                for s in range(2):
                    sum_ada(s, 1)
                with pool.Fori(1, ADA_PAIRS // 2) as i:
                    for s in range(2):
                        split(l, s, i * 2 + s, KD, ADA_PAIRS // 2 - 1)
                        sum_ada(i * 2 + s, ADA_PAIRS // 2 - 1)
                with pool.Fori(ADA_PAIRS // 2, (N_IN + KD) // 2 + 1) as i:
                    for s in range(2):
                        split(l, s, i * 2 + s, KD, (N_IN + KD - ADA_PAIRS) // 2 + 1)
                lo_of_h(0)

                def split_part(t2, size, times):
                    with pool.Fori(1, size) as i:
                        for s in range(2):
                            split(l, s, (i + t2) * 2 + s, KD, times * (size - 1))
                    with pool.Fori(0, KD // 2) as i:
                        for s in range(2):
                            split(l, s, (i + (t2 + size)) * 2 + s, size, times * KD // 2)

                with pool.Fori(0, FULL_PARTS) as part:
                    t2 = part * (PART + KD // 2) + (N_IN + KD) // 2
                    split_part(t2, PART, FULL_PARTS)
                    for s in range(2):
                        split(l, s, (t2 + (PART + KD // 2)) * 2 + s, KD, FULL_PARTS)
                split_part(FULL_PARTS * (PART + KD // 2) + (N_IN + KD) // 2, LAST_PART, 1)
                pool.wait_ge(tile_done.sem, tile_done.at(l, N_TILES - 2 * LAST_PART - KD))
                split_small(l + 1)
                for s in range(2):
                    split(l, s, N_TILES + s, KD)
                lo_of_h(1)

        @block.tensor
        def _(pe):
            pe.sem_inc(tile_done.sem, 2)
            pe.sem_inc(ada_sum_used.sem, 1)

            def transpose(out_, in_):
                return pe.transpose(out_, in_, ident[0:in_.shape[0], 0:in_.shape[0]])

            pe.wait_ge(const_loaded.sem, 64)
            n = 0
            unit_done.counted = 0
            last = transpose(ring[0][:, 0:KD], c_rows[:])
            unit_done.inc(last, 0)
            for l in range(DEPTH):
                unit_done.inc(transpose(ring[1 + l][:, 0:48], b_ada_rows[:, l, :]), 0)
            for n in range(3, 19):
                h, k = divmod(n - 3, KD)
                if n >= 4:
                    pe.wait_ge(bank_free[n % 4].sem, n // 4)
                if k == 0:
                    for i in (2 * h, 2 * h + 1):
                        pe.wait_ge(x_loaded[i].sem, 16)
                for i in range(4):
                    last = transpose(ring[n % 4][:, chunk(i)], x_rows[:, 4 * h + i, chunk(k)])
                unit_done.inc(last, 0)
            pe.wait_ge(bank_free[3].sem, 19 // 4)
            for n in range(2 * KD):
                if n % 4 == 0:
                    pe.wait_ge(ada_first_summed.sem, n // 4 + 1)
                last = pe.matmul(ring[3][:, n:n + 1], ada_first[:, 0, chunk(n)], one, start=True, stop=True)
            unit_done.inc(last, 0)

            with pe.Fori(0, DEPTH) as l:
                def enter(unit4, bank):
                    pe.wait_ge(bank_free[bank].sem, bank_free[bank].at(l, unit4))
                    return ring[bank]

                def bank_of(step, i=0):
                    u = UNIT[step] + i
                    return enter(u // 4, u % 4)

                def large(ps, slot, rows, hi, lo):
                    for k in range(rows):
                        pe.matmul(ps[:], w_hi[slot][:, k, :], hi(k), start=(k == 0), stop=False)
                        pe.matmul(ps[:], w_hi[slot][:, k, :], lo(k), start=False, stop=False)
                        last = pe.matmul(ps[:], w_lo[slot][:, k, :], hi(k), start=False, stop=(k == rows - 1))
                    return last

                def operand(h):
                    return (lambda k: op_hi[:, k, half_of(h)]), (lambda k: op_lo[:, k, half_of(h)])

                for step in ORDER:
                    kind, n = step[0], (step[1] if len(step) > 1 else 0)
                    if kind == "params":
                        pe.wait_ge(rows_loaded.sem, rows_loaded.at(l, 15))
                        ps = bank_of(step)
                        unit_done.inc(transpose(ps[:, 0:N_ROWS], par_rows[:]))
                    elif kind == "small":
                        if n == 0:
                            pe.wait_ge(small_split.sem, small_split.at(l, 1))
                        ps = bank_of(step)
                        hi, lo = operand(n)
                        for k in range(KD):
                            pe.wait_ge(h_lo.sem, h_lo.at(l, 8 * n + k - 15))
                            w_h, w_l = (t[:, k * 48:k * 48 + P] for t in (small_hi, small_lo))
                            pe.matmul(ps[:], w_h, hi(k), start=(k == 0), stop=False)
                            pe.matmul(ps[:], w_h, lo(k), start=False, stop=False)
                            last = pe.matmul(ps[:], w_l, hi(k), start=False, stop=(k == KD - 1))
                        unit_done.inc(last)
                    elif kind == "proj":
                        h = step[2]
                        if h == 0:
                            pe.wait_ge(split_done.sem, split_done.at(l, n + 1))
                        ps = bank_of(step)
                        last = large(ps, n % 2, KD, *operand(h))
                        (tile_done if h else half_done).inc(last)
                    elif kind == "ada":
                        for q in range(2):
                            pe.wait_ge(ada_summed[q].sem, ada_summed[q].at(l, n + 1))
                        ps = bank_of(step)
                        for i in range(2):
                            for q in range(2):
                                last = pe.matmul(ps[:, i:i + 1], ada_sum[q][:, chunk(i)], one,
                                                 start=(q == 0), stop=(q == 1))
                        ada_sum_used.inc(last)
                    elif kind == "dt":
                        pe.wait_ge(small_copied.sem, small_copied.at(l, 2))
                        ps = bank_of(step)
                        for c in range(NCH):
                            last = pe.matmul(ps[:, 4 * c:4 * c + 4], small[32:36, chunk(c)], ident[32:36, 32:36],
                                             start=True, stop=True)
                        unit_done.inc(last)
                    elif kind == "dt_cum":
                        pe.wait_ge(dt_ready.sem, dt_ready.at(l, 1))
                        ps = bank_of(step)
                        unit_done.inc(pe.matmul(ps[:, 0:32], cst("causal"), columns[:, 1, :], start=True, stop=True))
                    elif kind == "rotate":
                        h = step[2]
                        pe.wait_ge(raw_copied.sem, raw_copied.at(l, copied_count(8 + n) - 1 + h))
                        ps = bank_of(step)
                        unit_done.inc(pe.matmul(ps[:], cst("perm"), gb[:, n, half_of(h)], start=True, stop=True))
                    elif kind == "ssd_pre":
                        if n == 0:
                            pe.wait_ge(ssd_state.sem, ssd_state.at(l, 1))
                        else:
                            pe.wait_ge(ssd_banks_read.sem, ssd_banks_read.at(l, n))
                        b_cum, b_g, b_t, _ = core
                        for j in range(2):
                            transpose(b_t[:, chunk(j)], ga[:, j, chunk(n)])
                            transpose(b_t[:, chunk(2 + j)], ga[:, 2 + j, chunk(n)])
                        for g in range(2):
                            pe.matmul(b_g[:, chunk(g)], ga[:, 2 + g, chunk(n)], ga[:, 4 + g, chunk(n)],
                                      start=True, stop=True)
                        for hd in range(4):
                            i = 4 * n + hd
                            last = pe.matmul(b_cum[:, chunk(hd)], columns[:, 1, i:i + 1].to_broadcast([P, P]),
                                             cst("causal"), start=True, stop=True)
                        ssd_pre_done.inc(last)
                    elif kind == "ssd_b":
                        ed, ec, v, v2, bt, hs = tmp2k[0], tmp2k[1], tmp1k[5], tmp1k[6], tmp1k[7], tmp1k[8]
                        pe.wait_ge(ssd_operands.sem, ssd_operands.at(l, n + 1))
                        pe.wait_ge(ssd_state.sem, ssd_state.at(l, n + 1))
                        for hd in range(4):
                            j, i = divmod(hd, 2)
                            o = core[3][64 * i:64 * i + 64, chunk(j)]
                            pe.matmul(o, v[:, chunk(hd, 64)], ed[:, chunk(hd)], start=True, stop=False)
                            pe.matmul(o, hs[:, chunk(hd, 64)], ec[:, chunk(hd)], start=False, stop=True)
                        for g in range(2):
                            last = pe.matmul(core[3][:, chunk(2 + g)], bt[:, chunk(g)],
                                             v2[:, chunk(g)], start=True, stop=True)
                        ssd_b_done.inc(last)
                    elif kind in ("ssd_stats", "ret_stats", "gla_stats"):
                        g = ("ssd_stats", "ret_stats", "gla_stats").index(kind)
                        pe.wait_ge(norm_sq.sem, norm_sq.at(l, g + 1))
                        ps = bank_of(step)
                        if g == 0:
                            for c in range(NCH):
                                for j in range(2):
                                    last = pe.matmul(ps[:, c:c + 1], ga[:, 2 + j, chunk(c)], one,
                                                     start=(j == 0), stop=(j == 1))
                        else:
                            raw, sq = (gb[:, 4:6, :], gb[:, 0:2, :]) if g == 1 else (None, ga[:, 0:2, :])
                            for c in range(NCH):
                                for j in range(2):
                                    i = 4 * c + 2 * j
                                    last = pe.matmul(ps[:, i:i + 2], sq[:, j, chunk(c)], cst("head2"),
                                                     start=True, stop=True)
                                    if g == 1:
                                        last = pe.matmul(ps[:, 32 + i:32 + i + 2], raw[:, j, chunk(c)], cst("head2"),
                                                         start=True, stop=True)
                        unit_done.inc(last)
                    elif kind == "ssd_norm":
                        pe.wait_ge(norm_rstd.sem, norm_rstd.at(l, 1))
                        for h in range(2):
                            ps = bank_of(step, h)
                            for c in range(4):
                                last = transpose(ps[:, chunk(c)],
                                                 stat[:, 0, 4 * h + c:4 * h + c + 1].to_broadcast([P, P]))
                            unit_done.inc(last)
                    elif kind in ("ret_norm", "gla_norm"):
                        g = 1 if kind == "ret_norm" else 2
                        pe.wait_ge(norm_wide.sem, norm_wide.at(l, g))
                        u = 0
                        for h in ((0, 1) if g == 1 else (n,)):
                            for j in range(2):
                                for s in ((1, 0) if g == 1 else (0,)):
                                    ps = bank_of(step, u) if g == 1 else core[2 * h + j]
                                    for c in range(4):
                                        i = 4 * (4 * h + c) + 2 * j
                                        wide = wide_stat(g, s).rearrange("p j t -> p (j t)")
                                        last = transpose(ps[:, chunk(c)], wide[:, 64 * i:64 * i + P])
                                    (unit_done if g == 1 else gla_spread).inc(last)
                                    u += 1
                    elif kind == "ret_pre":
                        if n:
                            pe.wait_ge(ret_operands.sem, ret_operands.at(l, n))
                        else:
                            pe.wait_ge(ret_state.sem, ret_state.at(l, 1))
                            pe.wait_ge(raw_copied.sem, raw_copied.at(l, copied_count(13)))
                        for j in range(2):
                            transpose(core[2][:, chunk(j)], gb[:, 2 + j, chunk(n)])
                            transpose(core[2][:, chunk(2 + j)], gb[:, 4 + j, chunk(n)])
                        for j in range(2):
                            for i in range(2):
                                r = slice(64 * i, 64 * i + 64)
                                last = pe.matmul(core[i][:, chunk(j)], gb[r, 2 + j, chunk(n)], gb[r, j, chunk(n)],
                                                 start=True, stop=True)
                        ret_pre_done.inc(last)
                    elif kind == "ret_b":
                        m, kt, v, qg, hs = tmp2k[0], tmp1k[2], tmp1k[3], tmp1k[4], tmp1k[6]
                        pe.wait_ge(ret_operands.sem, ret_operands.at(l, n + 1))
                        pe.wait_ge(ret_state.sem, ret_state.at(l, n + 1))
                        for j in range(2):
                            o = core[3][:, chunk(j)]
                            pe.matmul(o, hs[:, chunk(j)], qg[:, chunk(j)], start=True, stop=False,
                                      skip_group_check=True)
                            for i in range(2):
                                hd = 2 * j + i
                                pe.matmul(o[64 * i:64 * i + 64], v[:, chunk(hd, 64)],
                                          m[:, chunk(hd)], start=False, stop=True,
                                          skip_group_check=True)
                        for j in range(2):
                            last = pe.matmul(core[3][:, chunk(2 + j)], kt[:, chunk(j)], v[:, chunk(j)],
                                             start=True, stop=True)
                        ret_b_done.inc(last)
                    elif kind == "gla_gate":
                        pe.wait_ge(lru_w_loaded.sem, lru_w_loaded.at(l, 9))
                        for h in range(2):
                            ps = bank_of(step, h)
                            unit_done.inc(pe.matmul(ps[:], gate_w[:], small[0:16, half_of(h)], start=True, stop=True))
                    elif kind == "gla_pre":
                        qz = tmp2k[0]
                        if n:
                            pe.wait_ge(gla_masked.sem, gla_masked.at(l, n))
                            pe.wait_ge(gla_kv.sem, gla_kv.at(l, n))
                        else:
                            pe.wait_ge(gla_zeroed.sem, gla_zeroed.at(l, 1))
                        transpose(core[2][:, 0:P], ga[:, 4, chunk(n)])
                        for j in range(2):
                            transpose(core[2][:, chunk(1 + j)], ga[:, 2 + j, chunk(n)])
                        for i in range(2):
                            last = pe.matmul(core[0][64 * i:64 * i + 64, 0:256],
                                             ga[:, 1, P * n + 64 * i:P * n + 64 * i + 64],
                                             qz[:].rearrange("p (h t) -> p h t", h=4)[:, :, chunk(i, 64)],
                                             start=True, stop=True)
                        gla_pre_done.inc(last)
                    elif kind == "gla_b":
                        pe.wait_ge(gla_kv.sem, gla_kv.at(l, n + 1))
                        if n:
                            pe.wait_ge(gla_state.sem, gla_state.at(l, n))
                        for i in range(2):
                            last = pe.matmul(core[1][:, chunk(i, 256)], gla_k[:, chunk(i)], gla_v[n % 2][:],
                                             start=True, stop=True)
                        gla_b_done.inc(last)
                    elif kind == "gla_c":
                        pe.wait_ge(gla_masked.sem, gla_masked.at(l, n + 1))
                        pe.wait_ge(gla_state.sem, gla_state.at(l, n + 1))
                        if n:
                            pe.wait_ge(gla_out.sem, gla_out.at(l, n))
                        for j in range(2):
                            o = core[3][:, chunk(j)]
                            for i in range(2):
                                pe.matmul(o[:, chunk(i, 64)], gla_h[(2 * n + i) % 3][:, chunk(j)],
                                          ga[:, 0, P * n + 64 * i:P * n + 64 * i + 64],
                                          start=(i == 0), stop=False, skip_group_check=True)
                            for i in range(2):
                                hd = 2 * j + i
                                last = pe.matmul(o[64 * i:64 * i + 64], gla_v[n % 2][:, chunk(hd, 64)],
                                                 gla_m[n % 2][:, chunk(hd)], start=False, stop=True,
                                                 skip_group_check=True)
                        gla_c_done.inc(last)
                    elif kind == "lru":
                        pe.wait_ge(lru_xr.sem, lru_xr.at(l, n + 1))
                        u = 0
                        for h in range(2):
                            for m in range(2):
                                ps = bank_of(step, u)
                                unit_done.inc(pe.matmul(ps[:], lru_w[:, m, n, :], gb[:, 2 + n, half_of(h)],
                                                        start=True, stop=True))
                                u += 1

                def ln_sums(which, h):
                    pe.wait_ge(sums_made.sem, sums_made.at(l, 16 * which + (16 if h else 14)))
                    for q in range(2):
                        for c in range(4):
                            last = pe.matmul(core[2 * h][:, 4 * q + c:4 * q + c + 1], tmp[:, 2 * q + h, chunk(c)], one,
                                             start=True, stop=True)
                    ln_summed.inc(last)

                def ln_wide(which, h):
                    pe.wait_ge(ln_rstd.sem, ln_rstd.at(l, 2 * which + h + 1))
                    for q in range(2):
                        for c in range(4):
                            last = transpose(core[2 * h + q][:, chunk(c)],
                                             stat[:, 2 * h + q, c:c + 1].to_broadcast([P, P]))
                    ln_spread.inc(last)

                def before_norm(which, last_pair, unit4, tile2, rows, hi, lo, ready):
                    for d, h in (NORM_UNITS[-4:] if last_pair else NORM_UNITS[:4]):
                        s, i = d % 2, (NORM_UNITS.index((d, h)) % 4)
                        if h == 0:
                            pe.wait_ge(split_done.sem, split_done.at(l, tile2 * 2 + (s + 1)))
                        if (d, h) == (KD - 1, 1):
                            ln_sums(which, 0)
                        ps = enter(unit4, i)
                        for k in range(rows):
                            ready(h, k)
                            pe.matmul(ps[:], w_hi[s][:, k, :], hi(h, k), start=(k == 0), stop=False)
                            pe.matmul(ps[:], w_hi[s][:, k, :], lo(h, k), start=False, stop=False)
                            last = pe.matmul(ps[:], w_lo[s][:, k, :], hi(h, k), start=False, stop=(k == rows - 1))
                        (tile_done if h else half_done).inc(last, 1 if last_pair else KD // 2 - 1)
                    if last_pair:
                        ln_wide(which, 0)
                        ln_sums(which, 1)
                        ln_wide(which, 1)

                def projection_and_norm(which, unit4, tile2, rows, hi, lo, ready):
                    with pe.Fori(0, KD // 2 - 1) as i:
                        before_norm(which, False, i + unit4, i + tile2, rows, hi, lo, ready)
                    n = KD // 2 - 1
                    before_norm(which, True, n + unit4, n + tile2, rows, hi, lo, ready)

                projection_and_norm(0, UNIT_OUT // 4, N_IN // 2, KD,
                                    lambda h, k: op_hi[:, k, half_of(h)], lambda h, k: op_lo[:, k, half_of(h)],
                                    lambda h, k: pe.wait_ge(y_lo.sem, y_lo.at(l, 8 * h + k + 1)))

                def ffn_part(unit4, t2, size, times):
                    with pe.Fori(0, size) as i:
                        for h in range(2):
                            for s in range(2):
                                if h == 0:
                                    pe.wait_ge(split_done.sem, split_done.at(l, (i + t2) * 2 + (s + 1)))
                                ps = enter(i + unit4, 2 * h + s)
                                for k in range(KD):
                                    if s == 0:
                                        pe.wait_ge(h_lo.sem, h_lo.at(l, 8 * h + k + 1))
                                    hi, lo = op_hi[:, k, half_of(h)], op_lo[:, k, half_of(h)]
                                    pe.matmul(ps[:], w_hi[s][:, k, :], hi, start=(k == 0), stop=False)
                                    pe.matmul(ps[:], w_hi[s][:, k, :], lo, start=False, stop=False)
                                    last = pe.matmul(ps[:], w_lo[s][:, k, :], hi, start=False, stop=(k == KD - 1))
                                (tile_done if h else half_done).inc(last, times * size)

                def ffn_down(unit4, t2, size, f0, times):
                    with pe.Fori(0, KD // 2) as i:
                        for s in range(2):
                            pe.wait_ge(split_done.sem, split_done.at(l, (i + t2) * 2 + (s + 1)))
                            for h in range(2):
                                ps = enter(i + unit4, 2 * s + h)
                                for k in range(size):
                                    if s == 0:
                                        pe.wait_ge(up_lo.sem, up_lo.at(l, f0 * 2 + (2 * k + h + 1)))
                                    hi, lo = act_hi[:, k, half_of(h)], act_lo[:, k, half_of(h)]
                                    pe.matmul(ps[:], w_hi[s][:, k, :], hi, start=(k == 0), stop=False)
                                    pe.matmul(ps[:], w_hi[s][:, k, :], lo, start=False, stop=False)
                                    last = pe.matmul(ps[:], w_lo[s][:, k, :], hi, start=False, stop=(k == size - 1))
                                (tile_done if h else half_done).inc(last, times * KD // 2)

                u4, t2 = UNIT_FFN // 4, (N_IN + KD) // 2
                with pe.Fori(0, FULL_PARTS) as part:
                    ffn_part(part * (PART + 4) + u4, part * (PART + 4) + t2, PART, FULL_PARTS)
                    ffn_down(part * (PART + 4) + (u4 + PART), part * (PART + 4) + (t2 + PART), PART,
                             part * PART, FULL_PARTS)
                done = FULL_PARTS * (PART + 4)
                ffn_part(u4 + done, t2 + done, LAST_PART, 1)
                projection_and_norm(1, u4 + done + LAST_PART, t2 + done + LAST_PART, LAST_PART,
                                    lambda h, k: act_hi[:, k, half_of(h)], lambda h, k: act_lo[:, k, half_of(h)],
                                    lambda h, k: pe.wait_ge(up_lo.sem, up_lo.at(l, 2 * (NF - LAST_PART + k) + h + 1)))

            for n in range(2 * NCH):
                c, g = divmod(n, 2)
                if g == 0 and c % 4 == 0:
                    done = ax_half1 if c else ax_half0
                    pe.wait_ge(done.sem, done.at(DEPTH, 0))
                pe.wait_ge(bank_free[n % 4].sem, bank_free[n % 4].at(DEPTH, n // 4))
                for i in range(4):
                    last = transpose(ring[n % 4][:, chunk(i)], ax[:, 4 * g + i, chunk(c)])
                unit_done.inc(last, 0)

        @block.scalar
        def _(act):
            def f(out_, in_, func, **k):
                return act.activation(out_, in_, func, **k)

            act.wait_ge(c_copied.sem, 1)
            c_tanh.inc(f(c_col[:, 1, :], c_col[:, 0, :], ACT.Tanh, scale=0.5), 1)
            for n in range(3, 19):
                h, k = divmod(n - 3, KD)
                act.wait_ge(unit_done.sem, n + 1)
                bank_free[n % 4].inc(f(ax[:, k, half_of(h)], ring[n % 4][:], ACT.Copy, scale=ALPHA), 0)
            ax_half1.inc(act.drain(), 0)
            act.wait_ge(angle_ready.sem, 1)
            f(angle[:, 2, :], angle[:, 0, :], ACT.Sin, scale=0.5)
            angle_sin.inc(f(angle[:, 3, :], angle[:, 0, :], ACT.Sin), 0)
            for s in range(2):
                act.wait_ge(raw_loaded[s].sem, 16)
                w_hi_made.inc(f(w_hi[s][:], w_raw[s][:], ACT.Copy), 0)
            act.wait_ge(mod_first.sem, 1)
            for n in range(2 * KD):
                h, k = divmod(n, KD)
                h_value.inc(f(op_hi[:, k, half_of(h)], ax[:, k, half_of(h)], ACT.Identity,
                              scale=mod_next[:, 8 + k:9 + k], bias=mod_next[:, k:k + 1]), 0)

            with act.Fori(0, DEPTH) as l:
                def wait(signal, n):
                    act.wait_ge(signal.sem, signal.at(l, n))

                def products(step, i=0):
                    u = UNIT[step] + i
                    if step[0] == "proj":
                        wait(tile_done if step[2] else half_done, step[1] + 1)
                    else:
                        wait(unit_done, MISC[step] + i + 1)
                    return ring[u % 4]

                def free(step, instruction, i=0):
                    bank_free[(UNIT[step] + i) % 4].inc(instruction)

                def weight_hi(tile, slot, n, times=1):
                    act.wait_ge(raw_loaded[slot].sem, raw_loaded[slot].at(l, n + 1))
                    act.wait_ge(tile_done.sem, tile_done.at(l, tile - 1))
                    w_hi_made.inc(f(w_hi[slot][:], w_raw[slot][:], ACT.Copy), times)


                copied = 0
                for step in ORDER:
                    kind, n = step[0], (step[1] if len(step) > 1 else 0)
                    if kind == "params":
                        ps = products(step)
                        wait(ax_half1, 0)
                        free(step, f(par[:], ps[:, 0:N_ROWS], ACT.Copy))
                        wait(heads_loaded, 3)
                        f(head_par[:, 0:4], head_par[:, 0:4], ACT.Exp)
                        lam = col("lru_lambda")
                        act.drain()
                        first = ROWS["lru_lambda"][0]
                        lam = par[:, first:first + 2]
                        f(lru_col[:, 0, :], lam, ACT.Abs)
                        act.drain()
                        f(lru_col[:, 0, :], lru_col[:, 0, :], ACT.Exp, scale=-1.0)
                        par_copied.inc(act.drain())
                    elif kind == "small":
                        ps = products(step)
                        free(step, f(small[:, half_of(n)], ps[0:48, :], ACT.Copy))
                        small_copied.inc(act.drain())
                    elif kind == "dt":
                        wait(dt_x, 1)
                        f(columns[:, 1, :], columns[:, 0, :], ACT.Abs)
                        act.drain()
                        dt_exp.inc(f(columns[:, 1, :], columns[:, 1, :], ACT.Exp, scale=-1.0))
                    elif kind == "proj":
                        h = step[2]
                        if n == 2 and h == 0:
                            act.wait_ge(residual_saved.sem, residual_saved.at(l, 2))
                        if n == 16 and h == 0:
                            wait(y_final, 1)
                        if n == 22 and h == 0:
                            wait(y_final, 2)
                        ps = products(step)
                        if n in silu_tiles:
                            gate_tanh.inc(f(y[:, gate_slot[n], half_of(h)], ps[:], ACT.Tanh, scale=0.5))
                        elif n in gate_slot:
                            i = 2 * (n - 24) + h
                            if i:
                                wait(gelu_in, i)
                            gelu_sq.inc(f(tmp2k[4][:], ps[:], ACT.Square))
                            wait(gelu_in, i + 1)
                            gelu_tanh.inc(f(y[:, gate_slot[n], half_of(h)], y[:, gate_slot[n], half_of(h)],
                                            ACT.Tanh, scale=math.sqrt(2 / math.pi)))
                        else:
                            free(step, f(copied_to(n)[:, half_of(h)], ps[:], ACT.Copy))
                            raw_copied.inc(act.drain())
                        if h == 1:
                            weight_hi(n + 2, n % 2, n // 2 + 1)
                    elif kind == "conv":
                        wait(conv_done, n + 1)
                        conv_tanh.inc(f(conv_b[:], conv_a[:], ACT.Tanh))
                    elif kind == "ssd_mid":
                        ed, ec, bt = tmp2k[0], tmp2k[1], tmp1k[7]
                        if n == 0:
                            wait(ssd_state, 1)
                        else:
                            wait(ssd_b_done, n)
                        wait(ssd_pre_done, n + 1)
                        f(bt[:], core[2][:, 256:512], ACT.Copy)
                        ssd_copied.inc(f(ec[:], core[0][:], ACT.Exp))
                        wait(ssd_exponents, n + 1)
                        f(ed[:], ed[:], ACT.Exp)
                        f(te[:], te[:], ACT.Exp)
                        ssd_exp.inc(act.drain())
                    elif kind in ("ssd_gate", "ret_square", "gla_square"):
                        g = ("ssd_gate", "ret_square", "gla_square").index(kind)
                        if g == 0:
                            wait(norm_in, 1)
                        elif g == 1:
                            wait(ret_state, NCH + 1)
                        else:
                            act.drain()
                        raw, sq = ((y[:, 0:2, :], ga[:, 2:4, :]), (gb[:, 4:6, :], gb[:, 0:2, :]),
                                   (ga[:, 2:4, :], ga[:, 0:2, :]))[g]
                        for j in range(2):
                            last = f(sq[:, j, :], raw[:, j, :], ACT.Square)
                        norm_sq.inc(last)
                    elif kind in ("ssd_stats", "ret_stats", "gla_stats"):
                        g = ("ssd_stats", "ret_stats", "gla_stats").index(kind)
                        wait(norm_var, g + 1)
                        norm_dev.inc(f(stat[:, 0, :], stat[:, 0, :], ACT.Sqrt, bias=eps))
                        if g:
                            wait(norm_rstd, g + 1)
                            for i in ((0, 1) if g == 1 else (0,)):
                                last = f(wide_stat(g, i).rearrange("p j (c f) -> p (j c) f", f=64),
                                         stat[:, i, :].unsqueeze(2).to_broadcast([P, 32, 64]), ACT.Copy)
                            norm_wide.inc(last)
                    elif kind == "ret_mid":
                        if n:
                            wait(ret_b_done, n)
                        wait(ret_pre_done, n + 1)
                        ret_v.inc(f(tmp1k[3][:], core[2][:, 256:512], ACT.Copy))
                    elif kind == "gla_gate":
                        wait(gla_gate_x, 1)
                        f(ga[:, 5, :], ga[:, 4, :], ACT.Abs)
                        act.drain()
                        f(ga[:, 5, :], ga[:, 5, :], ACT.Exp, scale=-1.0)
                        act.drain()
                        gla_gate_act.inc(f(ga[:, 5, :], ga[:, 5, :], ACT.Ln, bias=one))
                    elif kind == "gla_cum":
                        wait(gla_cum, 1)
                        f(ga[:, 5, :], ga[:, 4, :], ACT.Exp, scale=1 / 16)
                        act.drain()
                        gla_gate_act.inc(f(ga[:, 4, :], ga[:, 4, :], ACT.Exp, scale=-1 / 16))
                    elif kind == "gla_mid":
                        if n >= 2:
                            wait(gla_c_done, n - 1)
                        wait(gla_pre_done, n + 1)
                        for i in range(2):
                            r = slice(64 * i, 64 * i + 64)
                            f(gla_k[r, chunk(i)], core[2][r, 0:P], ACT.Copy)
                        gla_kv.inc(f(gla_v[n % 2][:], core[2][:, P:3 * P], ACT.Copy))
                    elif kind == "gla_c":
                        wait(gla_c_done, n + 1)
                        gla_out.inc(f(ga[:, 2:4, chunk(n)], core[3][:, 0:256].rearrange("p (j t) -> p j t", j=2),
                                      ACT.Copy))
                    elif kind == "lru":
                        e, g = gb[:, 4, :], gb[:, n, :]
                        fi = gb[:, 5, :]
                        ba, bx = col("lru_ba", n), lru_col[:, 3, n:n + 1]
                        if n:
                            wait(lru_dve, n)
                        for h in range(2):
                            ps = products(step, 2 * h)
                            free(step, f(e[:, half_of(h)], ps[:], ACT.Sigmoid, bias=ba), 2 * h)
                            ps = products(step, 2 * h + 1)
                            free(step, f(fi[:, half_of(h)], ps[:], ACT.Tanh, bias=bx, scale=0.5), 2 * h + 1)
                        act.drain()
                        lru_act.inc(f(g, e, ACT.Tanh, scale=lru_col[:, 1, n:n + 1]))
                        lru_act.inc(f(e, e, ACT.Exp, scale=lru_col[:, 2, n:n + 1]))
                    elif kind == "lru_gate":
                        wait(lru_in, n + 1)
                        lru_act.inc(f(gb[:, n, :], gb[:, n, :], ACT.Sqrt))
                    elif kind == "y_split":
                        h, k = divmod(n, KD)
                        if k == 0:
                            wait(tile_done if h else half_done, N_IN)
                        if n == 0:
                            wait(y_final, 2)
                        if k in (4, 5):
                            wait(lru_final, 2 * (k - 4) + h + 1)
                        if k in (6, 7):
                            wait(gla_final, 2 * h + k - 5)
                        if n == 8:
                            wait(gla_final, 4)
                            residual_loaded.inc(act.dma_start(ax[:], residual.rearrange("k p t -> p k t")))
                        y_hi.inc(f(op_hi[:, k, half_of(h)], y[:, k, half_of(h)], ACT.Copy))

                def layer_norm(which, tile0, slot0):
                    def next_weight(d):
                        weight_hi(tile0 + d + 2, d % 2, slot0 + d // 2 + 1)

                    def deviation(h):
                        wait(ln_var, 2 * which + h + 1)
                        s_ = stat[:, 2 * h + 1, 0:4]
                        ln_dev.inc(f(s_, s_, ACT.Sqrt, bias=eps))

                    for i, (d, h) in enumerate(NORM_UNITS):
                        if h == 1 and i < 12:
                            next_weight(d)
                        wait(z_made, 16 * which + i + 1)
                        if i >= 2:
                            wait(sums_made, 16 * which + i - 1)
                        z_sq.inc(f(tmp[:, 4 + i % 2, :], ax[:, d, half_of(h)], ACT.Square))
                        if i == 13:
                            f(te[:, 0:1], eps, ACT.Sqrt)
                        if i == 14:
                            deviation(0)
                            next_weight(KD - 2)
                    next_weight(KD - 1)

                    def split_h(h, ks):
                        for k in ks:
                            n = 16 * which + 8 * h + k
                            wait(ln_norm, n + 1)
                            wait(h_lo, n - 1)
                            args = dict(scale=fold[:, 2 * which, k:k + 1], bias=fold[:, 2 * which + 1, k:k + 1])
                            f(tmp[:, 6 + n % 2, :], ax[:, k, half_of(h)], ACT.Identity, **args)
                            h_value.inc(f(op_hi[:, k, half_of(h)], ax[:, k, half_of(h)], ACT.Identity, **args))

                    split_h(0, range(2))
                    deviation(1)
                    split_h(0, range(2, KD))
                    split_h(1, range(KD))

                layer_norm(0, N_IN, N_IN // 2)

                def ffn_part(t2, f0, size, times):
                    with act.Fori(0, size) as i:
                        for h in range(2):
                            act.wait_ge((tile_done if h else half_done).sem,
                                        (tile_done if h else half_done).at(l, (i + t2) * 2 + 1))
                            act.wait_ge(up_lo.sem, up_lo.at(l, (i + f0) * 2 + (h - 1)))
                            up_tanh.inc(f(tmp[:, h, :], ring[2 * h][:], ACT.Tanh, scale=0.5), times * size)
                            if h == 1:
                                for s in range(2):
                                    weight_hi((i + t2) * 2 + (2 + s), s, i + t2 + 1, times * size)
                            act.wait_ge(up_act.sem, up_act.at(l, (i + f0) * 2 + (h + 1)))
                            up_hi.inc(f(act_hi[:, bass.ds(i, 1), half_of(h)].rearrange("p a t -> p (a t)"),
                                        tmp[:, 4 + h, :], ACT.Copy), times * size)

                t2 = (N_IN + KD) // 2
                with act.Fori(0, FULL_PARTS) as part:
                    ffn_part(part * (PART + 4) + t2, part * PART, PART, FULL_PARTS)
                    with act.Fori(0, KD // 2) as i:
                        for s in range(2):
                            n2 = i + part * (PART + 4) + (t2 + PART)
                            weight_hi(n2 * 2 + (2 + s), s, n2 + 1, FULL_PARTS * KD // 2)
                ffn_part(t2 + FULL_PARTS * (PART + 4), FULL_PARTS * PART, LAST_PART, 1)
                t2 += FULL_PARTS * (PART + 4) + LAST_PART
                layer_norm(1, 2 * t2, t2)

            for c in range(NCH):
                n = 2 * c
                act.wait_ge(unit_done.sem, unit_done.at(DEPTH, n + 1))
                bank_free[n % 4].inc(f(x_rows[:, c, half_of(0)], ring[n % 4][:], ACT.Copy, scale=1 / ALPHA), 0)
                out_copied[0].inc(act.drain(), 0)

        @block.vector
        def _(dve):
            def tt(out_, a_, b_, op):
                return dve.tensor_tensor(out_, a_, b_, op)

            def ts(out_, a_, s0, s1, op0, op1=ALU.bypass):
                return dve.tensor_scalar(out_, a_, s0, s1, op0, op1) if s1 is not None else \
                    dve.tensor_scalar(out_, a_, s0, None, op0)

            def stt(out_, a_, s, b_, op0, op1):
                return dve.scalar_tensor_tensor(out=out_, in0=a_, scalar=s, in1=b_, op0=op0, op1=op1)

            def log1p(e, s, z, p):
                ts(s, e, 2.0, None, ALU.add)
                dve.drain()
                dve.reciprocal(s, s)
                dve.drain()
                tt(s, e, s, ALU.mult)
                dve.drain()
                tt(z, s, s, ALU.mult)
                dve.drain()
                ts(p, z, 1 / 15, None, ALU.mult)
                for n in (13, 11, 9, 7, 5, 3):
                    dve.drain()
                    stt(p, p, 1 / n, z, ALU.add, ALU.mult)
                dve.drain()
                stt(s, p, 1.0, s, ALU.add, ALU.mult)
                dve.drain()
                ts(s, s, 2.0, None, ALU.mult)
                dve.drain()

            dve.sem_inc(up_lo.sem, 2)
            dve.wait_ge(unit_done.sem, 1)
            bank_free[0].inc(dve.tensor_copy(c_col[:, 0, :], ring[0][:, 0:KD]), 0)
            c_copied.inc(dve.drain(), 1)
            for l in range(DEPTH):
                dve.wait_ge(unit_done.sem, 2 + l)
                bank_free[1 + l].inc(dve.tensor_copy(b_ada[:, l, :], ring[1 + l][:, 0:48]), 0)
            dve.wait_ge(c_tanh.sem, 1)
            stt(c_col[:, 0, :], c_col[:, 1, :], 1.0, c_col[:, 0, :], ALU.add, ALU.mult)
            dve.drain()
            c_ready.inc(ts(c_col[:, 0, :], c_col[:, 0, :], 0.5, None, ALU.mult), 0)
            dve.wait_ge(pos_loaded.sem, 16)
            dve.wait_ge(const_loaded.sem, 64)
            dve.tensor_copy(angle[:, 1, :], angle[:, 0, :].bitcast(I32))
            dve.drain()
            ts(angle[:, 0, :], angle[:, 1, :], cst("freq"), None, ALU.mult)
            dve.drain()
            ts(angle[:, 1, :], angle[:, 0, :], 1 / TWO_PI, 12582912.0, ALU.mult, ALU.add)
            dve.drain()
            ts(angle[:, 1, :], angle[:, 1, :], -12582912.0, None, ALU.add)
            rest = TWO_PI
            for bits in (5, 14, None):
                part = rest if bits is None else math.floor(rest * 2 ** bits) / 2 ** bits
                rest -= part
                dve.drain()
                stt(angle[:, 0, :], angle[:, 1, :], -part, angle[:, 0, :], ALU.mult, ALU.add)
            dve.drain()
            angle_ready.inc(ts(angle[:, 0, :], angle[:, 0, :], 3.1415925, -3.1415925, ALU.min, ALU.max), 0)
            dve.wait_ge(angle_sin.sem, 1)
            tt(angle[:, 2, :], angle[:, 2, :], angle[:, 2, :], ALU.mult)
            dve.drain()
            rotary_made.inc(ts(angle[:, 2, :], angle[:, 2, :], -2.0, 1.0, ALU.mult, ALU.add), 0)
            for i in range(4):
                dve.wait_ge(ada_first_loaded[i].sem, 16)
                o = ada_first[:, 0, chunk(i, 512)]
                ts(o, o, c_col[:, 0, 0:1], None, ALU.mult)
                for k in range(1, KD):
                    dve.drain()
                    stt(o, ada_first[:, k, chunk(i, 512)], c_col[:, 0, k:k + 1], o, ALU.mult, ALU.add)
                ada_first_summed.inc(dve.drain(), 0)
            dve.wait_ge(unit_done.sem, UNITS_0)
            bank_free[3].inc(tt(mod_next[:], ring[3][:, 0:16], b_ada[:, 0, 0:16], ALU.add), 0)
            dve.drain()
            mod_first.inc(ts(mod_next[:, 8:16], mod_next[:, 8:16], 1.0, 1 / ALPHA, ALU.add, ALU.mult), 0)
            dve.sem_inc(ax_half0.sem, 1)
            dve.wait_ge(ax_half1.sem, 1)
            dve.drain()
            for n in range(2 * KD):
                h, k = divmod(n, KD)
                ts(tmp[:, 6 + n % 2, :], ax[:, k, half_of(h)], mod_next[:, 8 + k:9 + k], mod_next[:, k:k + 1],
                   ALU.mult, ALU.add)
                dve.drain()
                dve.wait_ge(h_value.sem, n + 1)
                h_lo.inc(tt(op_lo[:, k, half_of(h)], tmp[:, 6 + n % 2, :],
                            op_hi[:, k, half_of(h)].bitcast(F32), ALU.subtract), 0)

            with dve.Fori(0, DEPTH) as l:
                def wait(signal, n):
                    dve.wait_ge(signal.sem, signal.at(l, n))

                def products(step, i=0):
                    u = UNIT[step] + i
                    if step[0] == "proj":
                        wait(tile_done if step[2] else half_done, step[1] + 1)
                    elif step[0] == "ada":
                        wait(ada_sum_used, step[1] + 1)
                    else:
                        wait(unit_done, MISC[step] + i + 1)
                    return ring[u % 4]

                def free(step, instruction, i=0):
                    bank_free[(UNIT[step] + i) % 4].inc(instruction)

                def convolve(out_, in_, weight, bias):
                    ts(out_, in_, weight(0), bias, ALU.mult, ALU.add)
                    for s in range(1, 4):
                        dve.drain()
                        last = stt(out_[:, s:T], in_[:, 0:T - s], weight(s), out_[:, s:T], ALU.mult, ALU.add)
                    return last

                gates = 0
                for step in ORDER:
                    kind, n = step[0], (step[1] if len(step) > 1 else 0)
                    if kind == "params":
                        wait(par_copied, 1)
                        dve.tensor_copy(b_mod[:, 0:32], b_ada[:, bass.ds(l, 1), 16:48].rearrange("p a n -> p (a n)"))
                        dve.tensor_copy(b_mod[:, 32:48], b_ada[:, bass.ds((l + 1) % DEPTH, 1), 0:16]
                                        .rearrange("p a n -> p (a n)"))
                        for i in range(2):
                            r = slice(64 * i, 64 * i + 64)
                            dve.tensor_copy(head_par[r, 12:14], head_par[r, 8 + i:12:2])
                        for r, factor in ((slice(0, 36), 0.5), (slice(ROWS["ln1_w"][0], N_ROWS), ALPHA)):
                            ts(par[:, r], par[:, r], factor, None, ALU.mult)
                        log1p(*(lru_col[:, i, :] for i in (0, 1, 2, 3)))
                        lam = par[:, ROWS["lru_lambda"][0]:ROWS["lru_lambda"][0] + 2]
                        ts(lru_col[:, 0, :], lam, -1.0, 0.0, ALU.mult, ALU.max)
                        dve.drain()
                        tt(lru_col[:, 1, :], lru_col[:, 0, :], lru_col[:, 1, :], ALU.add)
                        dve.drain()
                        ts(lru_col[:, 1, :], lru_col[:, 1, :], 8.0, None, ALU.mult)
                        dve.drain()
                        ts(lru_col[:, 2, :], lru_col[:, 1, :], -1.0, None, ALU.mult)
                        first = ROWS["lru_bx"][0]
                        ts(lru_col[:, 3, :], par[:, first:first + 2], 0.5, None, ALU.mult)
                        par_ready.inc(dve.drain())
                    elif kind == "dt":
                        ps = products(step)
                        heads = lambda i: columns[:, i, :].rearrange("p (c h) -> p c h", h=4)
                        across = lambda r: head_par[:, r].unsqueeze(1).to_broadcast([P, NCH, 4])
                        free(step, tt(heads(0), ps[:, 0:32].rearrange("p (c h) -> p c h", h=4),
                                      across(slice(4, 8)), ALU.add))
                        dt_x.inc(dve.drain())
                        wait(dt_exp, 1)
                        log1p(columns[:, 1, :], columns[:, 2, :], columns[:, 3, :], columns[:, 4, :])
                        stt(columns[:, 0, :], columns[:, 0, :], 0.0, columns[:, 2, :], ALU.max, ALU.add)
                        dve.drain()
                        dt_ready.inc(stt(heads(1), heads(0), -1.0, across(slice(0, 4)), ALU.mult, ALU.mult))
                    elif kind == "dt_cum":
                        ps = products(step)
                        free(step, dve.tensor_copy(columns[:, 2, :], ps[:, 0:32]))
                    elif kind == "ada_sum":
                        wait(ada_loaded[1], n + 1)
                        wait(ada_sum_used, n)
                        ts(ada_sum[1][:], ada_raw[1][:, 0, :], c_col[:, 0, 4:5], None, ALU.mult)
                        for k in range(1, 4):
                            dve.drain()
                            last = stt(ada_sum[1][:], ada_raw[1][:, k, :], c_col[:, 0, 4 + k:5 + k], ada_sum[1][:],
                                       ALU.mult, ALU.add)
                        ada_raw_free[1].inc(last)
                        ada_summed[1].inc(dve.drain())
                    elif kind == "ada":
                        ps = products(step)
                        to, first = (mod, 2 * n) if n < 16 else (mod_next, 2 * n - 32)
                        free(step, tt(to[:, first:first + 2], ps[:, 0:2], b_mod[:, 2 * n:2 * n + 2], ALU.add))
                        if n == ADA_PAIRS - 1:
                            dve.drain()
                            ts(mod[:, 16:24], mod[:, 16:24], 1.0, 1 / ALPHA, ALU.add, ALU.mult)
                            ts(mod_next[:, 8:16], mod_next[:, 8:16], 1.0, 1 / ALPHA, ALU.add, ALU.mult)
                            ts(mod[:, 24:32], mod[:, 24:32], 0.5, None, ALU.mult)
                            dve.drain()
                            for q, (scale, shift) in enumerate(((mod[:, 16:24], mod[:, 8:16]),
                                                                (mod_next[:, 8:16], mod_next[:, 0:8]))):
                                first = ROWS["ln2_w" if q else "ln1_w"][0]
                                tt(fold[:, 2 * q, :], par[:, first:first + KD], scale, ALU.mult)
                                tt(fold[:, 2 * q + 1, :], par[:, first + KD:first + 2 * KD], scale, ALU.mult)
                                dve.drain()
                                tt(fold[:, 2 * q + 1, :], fold[:, 2 * q + 1, :], shift, ALU.add)
                    elif kind == "proj":
                        h = step[2]
                        if n in silu_tiles:
                            gates += 1
                            wait(gate_tanh, gates)
                            o = y[:, gate_slot[n], half_of(h)]
                            free(step, stt(o, o, 1.0, ring[UNIT[step] % 4][:], ALU.add, ALU.mult))
                        elif n in gate_slot:
                            i = 2 * (n - 24) + h
                            ps, o, sq = ring[UNIT[step] % 4], y[:, gate_slot[n], half_of(h)], tmp2k[4]
                            wait(gelu_sq, i + 1)
                            ts(sq[:], sq[:], 0.044715, 1.0, ALU.mult, ALU.add)
                            dve.drain()
                            gelu_in.inc(tt(o, sq[:], ps[:], ALU.mult))
                            wait(gelu_tanh, i + 1)
                            free(step, stt(o, o, 1.0, ps[:], ALU.add, ALU.mult))
                    elif kind == "conv":
                        wait(raw_copied, copied_count(n + 2))
                        conv_done.inc(convolve(conv_a[:], ga[:, n, :], lambda s: col("ssd_conv_w", 6 * (3 - s) + n),
                                               col("ssd_conv_b", n)))
                        wait(conv_tanh, n + 1)
                        stt(ga[:, n, :], conv_b[:], 1.0, conv_a[:], ALU.add, ALU.mult)
                        dve.drain()
                    elif kind == "ssd_zero":
                        dve.memset(tmp1k[8][:], 0.0)
                        ssd_state.inc(dve.drain())
                    elif kind == "ssd_mid":
                        ed, ec, g, v, v2 = tmp2k[0], tmp2k[1], tmp1k[4], tmp1k[5], tmp1k[6]
                        by_head = lambda t, m: t.rearrange("p (h m) -> p h m", m=m)
                        cums = by_head(core[0][:], P)
                        wait(ssd_pre_done, n + 1)
                        tt(by_head(g[:], P), by_head(core[1][:, 0:256], P),
                           cst("causal").unsqueeze(1).to_broadcast([P, 2, P]), ALU.mult)
                        wait(ssd_copied, n + 1)
                        for hd in range(4):
                            ts(ed[:, chunk(hd)], core[0][:, chunk(hd)], columns[:, 2, 4 * n + hd:4 * n + hd + 1], 0.0,
                               ALU.subtract, ALU.min)
                        dve.tensor_copy(te[:, 4:8], cums[:, :, P - 1])
                        tt(te[:, 0:4], cums[:, :, P - 1], columns[:, 2, 4 * n:4 * n + 4], ALU.subtract)
                        ssd_exponents.inc(dve.drain())
                        dt4 = columns[:, 0, 4 * n:4 * n + 4].unsqueeze(2).to_broadcast([P, 4, 64])
                        tt(by_head(v[:], 64), by_head(core[2][:, 0:256], 64), dt4, ALU.mult)
                        ssd_banks_read.inc(dve.drain())
                        for gr in range(2):
                            o = ec[:, chunk(gr, 256)].rearrange("p (i m) -> p i m", i=2)
                            tt(o, o, ga[:, 4 + gr, chunk(n)].unsqueeze(1).to_broadcast([P, 2, P]), ALU.mult)
                        wait(ssd_exp, n + 1)
                        for gr in range(2):
                            o = ed[:, chunk(gr, 256)].rearrange("p (i m) -> p i m", i=2)
                            tt(o, o, g[:, chunk(gr)].unsqueeze(1).to_broadcast([P, 2, P]), ALU.mult)
                        tt(by_head(v2[:], 64), by_head(v[:], 64), te[:, 0:4].unsqueeze(2).to_broadcast([P, 4, 64]),
                           ALU.mult)
                        ssd_operands.inc(dve.drain())
                    elif kind == "ssd_b":
                        hs = tmp1k[8][:].rearrange("p (h m) -> p h m", m=64)
                        wait(ssd_b_done, n + 1)
                        tt(hs, hs, te[:, 4:8].unsqueeze(2).to_broadcast([P, 4, 64]), ALU.mult)
                        dve.drain()
                        tt(tmp1k[8][:], tmp1k[8][:], core[3][:, 256:512], ALU.add)
                        for j in range(2):
                            o = ga[:, j, chunk(n)]
                            stt(o, o, head_par[:, 12 + j:13 + j], core[3][:, chunk(j)], ALU.mult, ALU.add)
                        ssd_state.inc(dve.drain())
                    elif kind == "ssd_gate":
                        for j in range(2):
                            tt(y[:, j, :], y[:, j, :], ga[:, j, :], ALU.mult)
                        norm_in.inc(dve.drain())
                    elif kind == "ssd_stats":
                        ps = products(step)
                        free(step, ts(stat[:, 0, 0:8], ps[:, 0:8], 1 / (4 * GW), None, ALU.mult))
                        norm_var.inc(dve.memset(stat[:, 0, 8:32], 1.0))
                        wait(norm_dev, 1)
                        norm_rstd.inc(dve.reciprocal(stat[:, 0, :], stat[:, 0, :]))
                    elif kind == "ssd_norm":
                        for h in range(2):
                            ps = products(step, h)
                            for j in range(2):
                                o = y[:, j, half_of(h)]
                                last = stt(o, o, col("ssd_norm_w", j), ps[:], ALU.mult, ALU.mult)
                            free(step, last, h)
                        y_final.inc(dve.drain())
                    elif kind == "rotate":
                        h = step[2]
                        if n == 0 and h == 0:
                            dve.wait_ge(rotary_loaded.sem, rotary_loaded.at(l, 1))
                        ps = products(step)
                        t_ = tmp2k[5]
                        o = gb[:, n, half_of(h)]
                        free(step, tt(t_[:], cos_sin[:, 1, half_of(h)], ps[:], ALU.mult))
                        tt(o, o, cos_sin[:, 0, half_of(h)], ALU.mult)
                        dve.drain()
                        tt(o, o, t_[:], ALU.add)
                        dve.drain()
                    elif kind == "ret_zero":
                        dve.memset(tmp1k[6][:], 0.0)
                        ret_state.inc(dve.drain())
                    elif kind == "ret_mid":
                        m, kt, qg = tmp2k[0], tmp1k[2], tmp1k[4]
                        by = lambda t, w: t.rearrange("p (h m) -> p h m", m=w)
                        tt(by(qg[:], P), gb[:, 0:2, chunk(n)], by(cst("ret_in"), P), ALU.mult)
                        wait(ret_pre_done, n + 1)
                        for i in range(2):
                            tt(by(m[:], P)[:, i::2, :], by(core[i][:, 0:256], P), by(cst("ret_decay"), P)[:, i::2, :],
                               ALU.mult)
                        wait(ret_v, n + 1)
                        tt(by(kt[:], 64), by(core[2][:, 0:256], 64), cst("ret_end").unsqueeze(2).to_broadcast([P, 4, 64]),
                           ALU.mult)
                        ret_operands.inc(dve.drain())
                    elif kind == "ret_b":
                        st, hs = tmp1k[5], tmp1k[6]
                        wait(ret_b_done, n + 1)
                        by = lambda t, w: t.rearrange("p (h m) -> p h m", m=w)
                        tt(by(st[:], P), by(core[3][:, 256:512], P), cst("block2").unsqueeze(1).to_broadcast([P, 2, P]),
                           ALU.mult)
                        dve.tensor_copy(gb[:, 4:6, chunk(n)], by(core[3][:, 0:256], P))
                        dve.drain()
                        for j in range(2):
                            stt(hs[:, chunk(j)], hs[:, chunk(j)], cst("ret_chunk")[:, j:j + 1], st[:, chunk(j)],
                                ALU.mult, ALU.add)
                        ret_state.inc(dve.drain())
                    elif kind == "ret_stats":
                        ps = products(step)
                        ts(stat[:, 1, :], ps[:, 32:64], 1 / 64, None, ALU.mult)
                        dve.drain()
                        tt(stat[:, 2, :], stat[:, 1, :], stat[:, 1, :], ALU.mult)
                        dve.drain()
                        free(step, stt(stat[:, 0, :], ps[:, 0:32], 1 / 64, stat[:, 2, :], ALU.mult, ALU.subtract))
                        norm_var.inc(dve.drain())
                        wait(norm_dev, 2)
                        norm_rstd.inc(dve.reciprocal(stat[:, 0, :], stat[:, 0, :]))
                    elif kind == "ret_norm":
                        u = 0
                        for h in range(2):
                            for j in range(2):
                                o = gb[:, 4 + j, half_of(h)]
                                ps = products(step, u)
                                free(step, tt(o, o, ps[:], ALU.subtract), u)
                                dve.drain()
                                ps = products(step, u + 1)
                                free(step, stt(o, o, col("ret_norm_w", j), ps[:], ALU.mult, ALU.mult), u + 1)
                                dve.drain()
                                tt(y[:, 2 + j, half_of(h)], y[:, 2 + j, half_of(h)], o, ALU.mult)
                                u += 2
                        y_final.inc(dve.drain())
                    elif kind == "gla_gate":
                        for h in range(2):
                            ps = products(step, h)
                            free(step, ts(ga[:, 4, half_of(h)], ps[:], col("gla_bg"), None, ALU.add), h)
                        gla_gate_x.inc(dve.drain())
                    elif kind == "gla_cum":
                        wait(gla_gate_act, 1)
                        stt(ga[:, 4, :], ga[:, 4, :], 0.0, ga[:, 5, :], ALU.min, ALU.subtract)
                        dve.drain()
                        dve.memset(ga[:, 5, :], 1.0)
                        dve.drain()
                        dve.memset(ga[:, 5, 0:T:64], 0.0)
                        dve.drain()
                        gla_cum.inc(dve.tensor_tensor_scan(ga[:, 4, :], ga[:, 5, :], ga[:, 4, :], 0.0, ALU.mult, ALU.add))
                    elif kind == "gla_scale":
                        wait(gla_gate_act, 2)
                        wait(raw_copied, copied_count(19))
                        stt(ga[:, 0, :], ga[:, 0, :], 32 ** -0.5, ga[:, 5, :], ALU.mult, ALU.mult)
                        tt(ga[:, 1, :], ga[:, 1, :], ga[:, 4, :], ALU.mult)
                        dve.drain()
                        by = lambda t: t.rearrange("p (c t) -> p c t", t=64)
                        tt(by(ga[:, 4, :]), by(ga[:, 1, :]),
                           by(ga[:, 5, :])[:, :, 63:64].to_broadcast([P, T // 64, 64]), ALU.mult)
                        dve.drain()
                    elif kind in ("gla_zero", "gla_mid"):
                        by = lambda t: t.rearrange("p (h t) -> p h t", h=4)
                        if kind == "gla_zero":
                            for t in (gla_h[0], gla_k, *gla_m):
                                dve.memset(t[:], 0.0)
                        else:
                            if n >= 2:
                                wait(gla_c_done, n - 1)
                            wait(gla_pre_done, n + 1)
                            for i in range(2):
                                r = slice(64 * i, 64 * i + 64)
                                tt(by(gla_m[n % 2][r, :])[:, :, chunk(i, 64)], by(core[0][r, 0:256]),
                                   cst("causal64", r).unsqueeze(1).to_broadcast([64, 4, 64]), ALU.mult)
                        c = 0 if kind == "gla_zero" else n + 1
                        if c < NCH:
                            tt(by(tmp2k[0][:]), ga[:, 0, chunk(c)].unsqueeze(1).to_broadcast([P, 4, P]),
                               cst("head4").unsqueeze(2).to_broadcast([P, 4, P]), ALU.mult)
                        (gla_zeroed if kind == "gla_zero" else gla_masked).inc(dve.drain())
                    elif kind == "gla_b":
                        wait(gla_b_done, n + 1)
                        for i in range(2):
                            tt(gla_st[i][:], core[1][:, chunk(i, 256)], cst("block4"), ALU.mult)
                        for i in range(2):
                            dve.drain()
                            end = P * n + 64 * i + 63
                            stt(gla_h[(2 * n + i + 1) % 3][:], gla_h[(2 * n + i) % 3][:], ga[:, 5, end:end + 1],
                                gla_st[i][:], ALU.mult, ALU.add)
                        gla_state.inc(dve.drain())
                    elif kind == "gla_stats":
                        ps = products(step)
                        free(step, ts(stat[:, 0, :], ps[:, 0:32], 1 / 64, None, ALU.mult))
                        norm_var.inc(dve.drain())
                        wait(norm_dev, 3)
                        norm_rstd.inc(dve.reciprocal(stat[:, 0, :], stat[:, 0, :]))
                    elif kind == "gla_norm":
                        for j in range(2):
                            o = ga[:, 2 + j, half_of(n)]
                            wait(gla_spread, 2 * n + j + 1)
                            stt(o, o, col("gla_norm_w", j), core[2 * n + j][:], ALU.mult, ALU.mult)
                            dve.drain()
                            gla_final.inc(tt(y[:, 6 + j, half_of(n)], y[:, 6 + j, half_of(n)], o, ALU.mult))
                    elif kind == "lru_conv":
                        wait(raw_copied, copied_count(22 + n))
                        lru_xr.inc(convolve(gb[:, 2 + n, :], gb[:, n, :], lambda s: col("lru_conv_w", 2 * (3 - s) + n),
                                            col("lru_conv_b", n)))
                    elif kind == "lru_gate":
                        xr, e, fi, g = gb[:, 2 + n, :], gb[:, 4, :], gb[:, 5, :], gb[:, n, :]
                        wait(lru_act, 3 * n + 1)
                        stt(fi, fi, 1.0, xr, ALU.add, ALU.mult)
                        dve.drain()
                        wait(lru_act, 3 * n + 2)
                        tt(xr, e, e, ALU.mult)
                        dve.drain()
                        lru_in.inc(stt(g, xr, 1.0, g, ALU.add, ALU.mult))
                    elif kind == "lru_scan":
                        e, fi, g = gb[:, 4, :], gb[:, 5, :], gb[:, n, :]
                        wait(lru_act, 3 * n + 3)
                        tt(fi, fi, g, ALU.mult)
                        dve.drain()
                        lru_dve.inc(dve.tensor_tensor_scan(g, e, fi, 0.0, ALU.mult, ALU.add))
                    elif kind == "lru_out":
                        j, h = divmod(n, 2)
                        o = y[:, 4 + j, half_of(h)]
                        dve.drain()
                        lru_final.inc(stt(o, gb[:, j, half_of(h)], 0.25, o, ALU.mult, ALU.mult))
                    elif kind == "y_split":
                        h, k = divmod(n, KD)
                        wait(y_hi, n + 1)
                        y_lo.inc(tt(op_lo[:, k, half_of(h)], y[:, k, half_of(h)],
                                    op_hi[:, k, half_of(h)].bitcast(F32), ALU.subtract))

                def add_products(d, h, bank, signal, tile, gate):
                    dve.wait_ge(signal.sem, signal.at(l, tile))
                    o = ax[:, d, half_of(h)]
                    return stt(o, ring[bank][:], gate[:, d:d + 1], o, ALU.mult, ALU.add)

                def layer_norm(which, tile0, gate):
                    def add_square(i):
                        d, h = NORM_UNITS[i]
                        wait(z_sq, 16 * which + i + 1)
                        q = tmp[:, 2 + h, :]
                        if d == 0:
                            sums_made.inc(dve.tensor_copy(q, tmp[:, 4 + i % 2, :]))
                        else:
                            sums_made.inc(tt(q, q, tmp[:, 4 + i % 2, :], ALU.add))

                    def statistics(h):
                        wait(ln_summed, 2 * which + h + 1)
                        ts(stat[:, 2 * h, 0:4], core[2 * h][:, 0:4], 1 / D, None, ALU.mult)
                        dve.drain()
                        tt(stat[:, 2 * h, 4:8], stat[:, 2 * h, 0:4], stat[:, 2 * h, 0:4], ALU.mult)
                        dve.drain()
                        stt(stat[:, 2 * h + 1, 0:4], core[2 * h][:, 4:8], 1 / D, stat[:, 2 * h, 4:8],
                            ALU.mult, ALU.subtract)
                        ln_var.inc(dve.drain())

                    def reciprocal(h):
                        wait(ln_dev, 2 * which + h + 1)
                        ln_rstd.inc(dve.reciprocal(stat[:, 2 * h + 1, 0:4], stat[:, 2 * h + 1, 0:4]))

                    def normalise(h, ks):
                        if 0 in ks:
                            wait(ln_spread, 2 * which + h + 1)
                        for q, op in enumerate((ALU.subtract, ALU.mult)):
                            for k in ks:
                                o = ax[:, k, half_of(h)]
                                last = tt(o, o, core[2 * h + q][:], op)
                                if q:
                                    ln_norm.inc(last)
                            if q == 0:
                                dve.drain()

                    def affine(h, k):
                        wait(h_value, 16 * which + 8 * h + k + 1)
                        first = ROWS["ln2_w" if which else "ln1_w"][0] + k
                        o = ax[:, k, half_of(h)]
                        ts(o, o, par[:, first:first + 1], par[:, first + KD:first + KD + 1], ALU.mult, ALU.add)

                    for i, (d, h) in enumerate(NORM_UNITS):
                        bank_free[i % 4].inc(add_products(d, h, i % 4, tile_done if h else half_done,
                                                          tile0 + d + 1, gate))
                        z_made.inc(dve.drain())
                        o = tmp[:, h, :]
                        if d == 0:
                            dve.tensor_copy(o, ax[:, d, half_of(h)])
                        else:
                            tt(o, o, ax[:, d, half_of(h)], ALU.add)
                        if i == 15:
                            normalise(0, range(1))
                        if i:
                            add_square(i - 1)
                        if i == 14:
                            statistics(0)
                            reciprocal(0)
                    dve.drain()
                    add_square(15)
                    normalise(0, range(1, 2))
                    statistics(1)
                    normalise(0, range(2, 4))
                    reciprocal(1)
                    normalise(0, range(4, 6))
                    normalise(0, range(6, KD))
                    for k in range(0, KD, 2):
                        normalise(1, range(k, k + 2))
                    for k in range(KD):
                        affine(0, k)
                    if which:
                        ax_half0.inc(dve.drain())
                    for k in range(KD):
                        affine(1, k)
                    if which:
                        ax_half1.inc(dve.drain())

                dve.wait_ge(residual_loaded.sem, residual_loaded.at(l, 1))
                layer_norm(0, N_IN, mod[:, 0:8])

                def ffn_part(t2, f0, size, times):
                    with dve.Fori(0, size) as i:
                        for h in range(2):
                            n = (i + f0) * 2 + (h + 1)
                            dve.wait_ge(up_tanh.sem, up_tanh.at(l, n))
                            bank_free[2 * h].inc(stt(tmp[:, 2 + h, :], tmp[:, h, :], 1.0, ring[2 * h][:],
                                                     ALU.add, ALU.mult), times * size)
                            done = tile_done if h else half_done
                            dve.drain()
                            dve.wait_ge(done.sem, done.at(l, (i + t2) * 2 + 2))
                            bank_free[2 * h + 1].inc(tt(tmp[:, 4 + h, :], tmp[:, 2 + h, :], ring[2 * h + 1][:],
                                                        ALU.mult), times * size)
                            up_act.inc(dve.drain(), times * size)
                            dve.wait_ge(up_hi.sem, up_hi.at(l, n))
                            hidden = lambda t: t[:, bass.ds(i, 1), half_of(h)].rearrange("p a t -> p (a t)")
                            up_lo.inc(tt(hidden(act_lo), tmp[:, 4 + h, :], hidden(act_hi).bitcast(F32),
                                         ALU.subtract), times * size)

                t2 = (N_IN + KD) // 2
                with dve.Fori(0, FULL_PARTS) as part:
                    ffn_part(part * (PART + 4) + t2, part * PART, PART, FULL_PARTS)
                    for d in range(KD):
                        for h in range(2):
                            bank = (2 * d + h) % 4
                            bank_free[bank].inc(add_products(
                                d, h, bank, tile_done if h else half_done,
                                (part * (PART + 4) + (t2 + PART)) * 2 + (d + 1), mod[:, 24:32]), FULL_PARTS)
                t2 += FULL_PARTS * (PART + 4)
                ffn_part(t2, FULL_PARTS * PART, LAST_PART, 1)
                layer_norm(1, 2 * (t2 + LAST_PART), mod[:, 24:32])

            for c in range(NCH):
                n = 2 * c + 1
                dve.wait_ge(unit_done.sem, unit_done.at(DEPTH, n + 1))
                bank_free[n % 4].inc(ts(x_rows[:, c, half_of(1)], ring[n % 4][:], 1 / ALPHA, None, ALU.mult), 0)
                out_copied[1].inc(dve.drain(), 0)

        wrong = [(s.name, s.layer, s.counted) for s in Signal.all if s.layer and s.layer != s.counted]
        assert not wrong, wrong


_INS = ["x", "c", "positions", "w_ada", "b_ada", "w_in", "ssd_conv_w", "ssd_conv_b", "ssd_dt_bias", "ssd_a_log",
        "ssd_d", "ssd_norm_w", "ret_norm_w", "lru_conv_w", "lru_conv_b", "lru_wa", "lru_ba", "lru_wx", "lru_bx",
        "lru_lambda", "gla_wg2", "gla_bg", "gla_norm_w", "w_out", "ln1_w", "ln1_b", "ffn_w_up", "ffn_w_down",
        "ln2_w", "ln2_b"]


def kernel(**inputs):
    import numpy as _np
    import concourse.bacc as _bacc
    from concourse import mybir as _mybir
    from concourse.bass_utils import run_bass_kernel_spmd as _run

    nc = _bacc.Bacc("TRN2", target_bir_lowering=False, num_devices=1)
    arrays, args = {}, {}
    for name in _INS + ["const"]:
        v = constants() if name == "const" else _np.ascontiguousarray(inputs[name])
        arrays[f"in_{name}"] = v
        args[name] = nc.dram_tensor(f"in_{name}", v.shape, _mybir.dt.from_np(v.dtype), kind="ExternalInput").ap()
    out = nc.dram_tensor("out_0", (1, T, D), _mybir.dt.float32, kind="ExternalOutput").ap()
    nc.disable_value_cache = True
    build(nc, args, out)
    return _run(nc, [arrays], core_ids=[0]).results[0]["out_0"]
```
